# Optimizing a Trainium2 kernel written in Bass

```python
import math
import jax, jax.numpy as jnp
from jax import lax
import numpy as np

D_MODEL = 1024
BATCH = 1
SEQ = 512
DEPTH = 2

BLOCK_Q = 128
EPS = 1e-6
MLA_HEADS = 6
MLA_Q_LORA = 384
MLA_KV_LORA = 256
MLA_NOPE = 64
MLA_ROPE = 32
MLA_V = 64
ROPE_THETA = 10000.0
DSA_HEADS = 5
DSA_DIM = 64
IDX_HEADS = 8
IDX_DIM = 64
DSA_TOPK = 256
SB_HEADS = 5
SB_DIM = 64
REL_BUCKETS = 32
REL_MAX_DIST = 128
D_FF = -(-8 * D_MODEL // (3 * 256)) * 256
PLE_DIM = 256

MIX_WIDTH = MLA_HEADS * MLA_V + DSA_HEADS * DSA_DIM + SB_HEADS * SB_DIM
IN_SPLITS = (MLA_Q_LORA, MLA_KV_LORA, MLA_ROPE,
             DSA_HEADS * DSA_DIM, DSA_DIM, DSA_DIM,
             IDX_HEADS * IDX_DIM, IDX_DIM, IDX_HEADS,
             SB_HEADS * SB_DIM, SB_HEADS * SB_DIM, SB_HEADS * SB_DIM)
D_IN = sum(IN_SPLITS)


def rms_norm(x, g):
    xf = x.astype(jnp.float32)
    y = xf * lax.rsqrt(jnp.mean(xf * xf, axis=-1, keepdims=True) + EPS)
    return (y * g.astype(jnp.float32)).astype(x.dtype)

def apply_rope(x, pos):
    half = x.shape[-1] // 2
    inv = ROPE_THETA ** (-jnp.arange(half, dtype=jnp.float32) / half)
    ang = pos.astype(jnp.float32)[:, None] * inv[None, :]
    cos = jnp.cos(ang)[None, :, None, :].astype(x.dtype)
    sin = jnp.sin(ang)[None, :, None, :].astype(x.dtype)
    x1, x2 = x[..., :half], x[..., half:]
    return jnp.concatenate([x1 * cos - x2 * sin, x1 * sin + x2 * cos], axis=-1)

def t5_bucket(dist):
    max_exact = REL_BUCKETS // 2
    d = jnp.maximum(dist, 1).astype(jnp.float32)
    large = max_exact + (jnp.log(d / max_exact) / math.log(REL_MAX_DIST / max_exact)
                         * (REL_BUCKETS - max_exact)).astype(jnp.int32)
    large = jnp.minimum(large, REL_BUCKETS - 1)
    return jnp.where(dist < max_exact, dist, large)

def mixer_block(q0, pos, mla_q, mla_k, mla_v, dsa_q, dsa_k, dsa_v,
                idx_q, idx_k, idx_w, sb_q, sb_k, sb_v, rel_bias, topk):
    B = mla_q.shape[0]
    sl = lambda a: lax.dynamic_slice_in_dim(a, q0, BLOCK_Q, axis=1)
    qpos = q0 + jnp.arange(BLOCK_Q, dtype=jnp.int32)
    causal = pos[None, :] <= qpos[:, None]
    strict = pos[None, :] < qpos[:, None]

    s = jnp.einsum('bqhd,bkhd->bhqk', sl(mla_q), mla_k).astype(jnp.float32) * (MLA_NOPE + MLA_ROPE) ** -0.5
    s = jnp.where(causal[None, None], s, -jnp.inf)
    pr = jax.nn.softmax(s, axis=-1).astype(mla_v.dtype)
    o_mla = jnp.einsum('bhqk,bkhd->bqhd', pr, mla_v).reshape(B, BLOCK_Q, MLA_HEADS * MLA_V)

    ilog = jnp.einsum('bqhd,bkd->bqhk', sl(idx_q), idx_k) * IDX_DIM ** -0.5
    isc = jnp.einsum('bqhk,bqh->bqk', jax.nn.relu(ilog), sl(idx_w)).astype(jnp.float32)
    isc = jnp.where(causal[None], isc, -jnp.inf)
    _, sel = lax.top_k(isc, topk)
    valid = sel <= qpos[None, :, None]
    gather = jax.vmap(lambda a, i: a[i])
    kg = gather(dsa_k, sel)
    vg = gather(dsa_v, sel)
    bias = rel_bias[t5_bucket(jnp.maximum(qpos[None, :, None] - sel, 0))]
    a = (jnp.einsum('bqhd,bqjd->bhqj', sl(dsa_q), kg).astype(jnp.float32) * DSA_DIM ** -0.5
         + jnp.transpose(bias, (0, 3, 1, 2)).astype(jnp.float32))
    a = jnp.where(valid[:, None], a, -jnp.inf)
    pa = jax.nn.softmax(a, axis=-1).astype(vg.dtype)
    o_dsa = jnp.einsum('bhqj,bqjd->bqhd', pa, vg).reshape(B, BLOCK_Q, DSA_HEADS * DSA_DIM)

    z = jnp.einsum('bqhd,bkhd->bhqk', sl(sb_q), sb_k).astype(jnp.float32) * SB_DIM ** -0.5
    m = strict[None, None]
    l1m = jnp.where(m, jax.nn.log_sigmoid(-z), 0.0)
    suffix = lax.cumsum(l1m, axis=3, reverse=True) - l1m
    w = jnp.where(m, jnp.exp(jax.nn.log_sigmoid(z) + suffix), 0.0).astype(sb_v.dtype)
    o_sb = jnp.einsum('bhqk,bkhd->bqhd', w, sb_v).reshape(B, BLOCK_Q, SB_HEADS * SB_DIM)

    return jnp.concatenate([o_mla, o_dsa, o_sb], axis=-1)

def first_inputs(seed: int = 0) -> dict:
    key = jax.random.key(seed)
    ks = jax.random.split(key, 18)
    f32 = jnp.float32
    nrm = lambda k, shape, scale: jax.random.normal(k, shape, f32) * scale
    gain = lambda k, shape: 1.0 + 0.05 * jax.random.normal(k, shape, f32)
    return {
        "x": nrm(ks[0], (BATCH, SEQ, D_MODEL), 1.0),
        "p": nrm(ks[1], (DEPTH, BATCH, SEQ, PLE_DIM), 1.0),
        "w_in": nrm(ks[2], (DEPTH, D_MODEL, D_IN), D_MODEL ** -0.5),
        "attn_norm": gain(ks[3], (DEPTH, D_MODEL)),
        "mla_q_norm": gain(ks[4], (DEPTH, MLA_Q_LORA)),
        "mla_w_uq": nrm(ks[5], (DEPTH, MLA_Q_LORA, MLA_HEADS * (MLA_NOPE + MLA_ROPE)), MLA_Q_LORA ** -0.5),
        "mla_kv_norm": gain(ks[6], (DEPTH, MLA_KV_LORA)),
        "mla_w_ukv": nrm(ks[7], (DEPTH, MLA_KV_LORA, MLA_HEADS * (MLA_NOPE + MLA_V)), MLA_KV_LORA ** -0.5),
        "rel_bias": nrm(ks[8], (REL_BUCKETS, DSA_HEADS), 0.5),
        "w_o": nrm(ks[9], (DEPTH, MIX_WIDTH, D_MODEL), MIX_WIDTH ** -0.5),
        "ffn_norm": gain(ks[10], (DEPTH, D_MODEL)),
        "w_gate": nrm(ks[11], (DEPTH, D_MODEL, D_FF), D_MODEL ** -0.5),
        "w_up": nrm(ks[12], (DEPTH, D_MODEL, D_FF), D_MODEL ** -0.5),
        "w_down": nrm(ks[13], (DEPTH, D_FF, D_MODEL), D_FF ** -0.5),
        "ple_norm": gain(ks[14], (DEPTH, D_MODEL)),
        "w_ple_gate": nrm(ks[15], (DEPTH, D_MODEL, D_MODEL), D_MODEL ** -0.5),
        "w_ple_proj": nrm(ks[16], (DEPTH, PLE_DIM, D_MODEL), PLE_DIM ** -0.5),
        "final_norm": gain(ks[17], (D_MODEL,)),
    }

def first_block(x, p, w_in, attn_norm, mla_q_norm, mla_w_uq, mla_kv_norm, mla_w_ukv,
              rel_bias, w_o, ffn_norm, w_gate, w_up, w_down, ple_norm, w_ple_gate,
              w_ple_proj, final_norm):
    B, S, _ = x.shape
    n_blk = S // BLOCK_Q
    topk = min(DSA_TOPK, S // 4)
    pos = jnp.arange(S, dtype=jnp.int32)
    offsets = [int(o) for o in np.cumsum(IN_SPLITS)[:-1]]
    starts = jnp.arange(n_blk, dtype=jnp.int32) * BLOCK_Q
    h = x
    for i in range(DEPTH):
        hn = rms_norm(h, attn_norm[i])
        proj = hn @ w_in[i]
        (c_q, c_kv, k_rope, dq, dk, dv, iq, ik, iw, sq, sk, sv) = jnp.split(proj, offsets, axis=-1)

        q = (rms_norm(c_q, mla_q_norm[i]) @ mla_w_uq[i]).reshape(B, S, MLA_HEADS, MLA_NOPE + MLA_ROPE)
        q = jnp.concatenate([q[..., :MLA_NOPE], apply_rope(q[..., MLA_NOPE:], pos)], axis=-1)
        kv = (rms_norm(c_kv, mla_kv_norm[i]) @ mla_w_ukv[i]).reshape(B, S, MLA_HEADS, MLA_NOPE + MLA_V)
        kr = apply_rope(k_rope[:, :, None, :], pos)
        mla_k = jnp.concatenate([kv[..., :MLA_NOPE],
                                 jnp.broadcast_to(kr, (B, S, MLA_HEADS, MLA_ROPE))], axis=-1)
        mla_v = kv[..., MLA_NOPE:]

        dsa_q = dq.reshape(B, S, DSA_HEADS, DSA_DIM)
        idx_q = iq.reshape(B, S, IDX_HEADS, IDX_DIM)
        idx_w = iw * IDX_HEADS ** -0.5

        sb_q = sq.reshape(B, S, SB_HEADS, SB_DIM)
        sb_k = sk.reshape(B, S, SB_HEADS, SB_DIM)
        sb_v = sv.reshape(B, S, SB_HEADS, SB_DIM)

        blocks = lax.map(lambda q0: mixer_block(q0, pos, q, mla_k, mla_v, dsa_q, dk, dv,
                                                idx_q, ik, idx_w, sb_q, sb_k, sb_v,
                                                rel_bias, topk), starts)
        mix = jnp.transpose(blocks, (1, 0, 2, 3)).reshape(B, S, MIX_WIDTH)
        h = h + mix @ w_o[i]

        hf = rms_norm(h, ffn_norm[i])
        h = h + (jax.nn.silu(hf @ w_gate[i]) * (hf @ w_up[i])) @ w_down[i]

        g = jax.nn.sigmoid(rms_norm(h, ple_norm[i]) @ w_ple_gate[i])
        h = h + g * (p[i] @ w_ple_proj[i])
    return rms_norm(h, final_norm)


DEPTH_2 = 1

HEAD_DIM = 64
NSA_HEADS = 8
NSA_KV_HEADS = 2
SWA_HEADS = 8
SWA_KV_HEADS = 2
CMP_BLOCK = 32
CMP_STRIDE = 16
CMP_HIDDEN = 256
SLC_BLOCK = 64
N_SELECT = 16
NSA_WINDOW = 512
SWA_WINDOW = 128
Q_BLOCK = 128
RMS_EPS = 1e-6
NEG = -1e30
BIG = 1e30
NSA_WIDTH = NSA_HEADS * HEAD_DIM
SWA_WIDTH = SWA_HEADS * HEAD_DIM
KV_NSA = NSA_KV_HEADS * HEAD_DIM
KV_SWA = SWA_KV_HEADS * HEAD_DIM
SPLIT_SIZES = (NSA_WIDTH, 2 * KV_NSA, 2 * KV_NSA, 2 * KV_NSA, 3 * NSA_HEADS, NSA_WIDTH,
               SWA_WIDTH, 2 * KV_SWA, SWA_WIDTH, 2 * D_MODEL)
D_IN_2 = sum(SPLIT_SIZES)


def split_points():
    pts, acc = [], 0
    for s in SPLIT_SIZES[:-1]:
        acc += s
        pts.append(acc)
    return pts

def alibi_slopes(n, n_kv):
    s = 2.0 ** (-8.0 * (np.arange(n) + 1) / n)
    return jnp.asarray(s, dtype=jnp.float32).reshape(n_kv, n // n_kv)

def rms_norm_2(x, g):
    xf = x.astype(jnp.float32)
    y = xf * lax.rsqrt(jnp.mean(xf * xf, axis=-1, keepdims=True) + RMS_EPS)
    return (y * g.astype(jnp.float32)).astype(x.dtype)

def q_heads(t, n_kv, r):
    B, S, _ = t.shape
    return t.reshape(B, S, n_kv, r, HEAD_DIM).transpose(0, 2, 3, 1, 4)

def kv_heads(t, n_kv):
    B, S, _ = t.shape
    return t.reshape(B, S, n_kv, HEAD_DIM).transpose(0, 2, 1, 3)

def merge_heads(o):
    B, G, r, S, dh = o.shape
    return o.transpose(0, 3, 1, 2, 4).reshape(B, S, G * r * dh)

def banded_attention(q, k, v, slopes, window, sinks=None):
    B, G, r, S, dh = q.shape
    nprev = window // Q_BLOCK
    nqb = S // Q_BLOCK
    lk = (nprev + 1) * Q_BLOCK
    pad = nprev * Q_BLOCK
    kp = jnp.pad(k, ((0, 0), (0, 0), (pad, 0), (0, 0)))
    vp = jnp.pad(v, ((0, 0), (0, 0), (pad, 0), (0, 0)))
    idx = jnp.arange(nqb)[:, None] * Q_BLOCK + jnp.arange(lk)[None, :]
    kb = kp[:, :, idx].astype(jnp.float32)
    vb = vp[:, :, idx].astype(jnp.float32)
    qb = q.reshape(B, G, r, nqb, Q_BLOCK, dh).astype(jnp.float32)
    s = jnp.einsum('bgrnqd,bgnkd->bgrnqk', qb, kb) * (dh ** -0.5)
    qpos = jnp.arange(nqb)[:, None] * Q_BLOCK + jnp.arange(Q_BLOCK)[None, :]
    kpos = idx - pad
    dist = qpos[:, :, None] - kpos[:, None, :]
    valid = (dist >= 0) & (dist < window) & (kpos[:, None, :] >= 0)
    s = s - slopes[None, :, :, None, None, None] * dist.astype(jnp.float32)
    s = jnp.where(valid, s, NEG)
    if sinks is not None:
        sink = jnp.broadcast_to(sinks.astype(jnp.float32).reshape(1, G, r, 1, 1, 1), s.shape[:-1] + (1,))
        p = jax.nn.softmax(jnp.concatenate([s, sink], axis=-1), axis=-1)[..., :-1]
    else:
        p = jax.nn.softmax(s, axis=-1)
    o = jnp.einsum('bgrnqk,bgnkd->bgrnqd', p, vb)
    return o.reshape(B, G, r, S, dh).astype(q.dtype)

def compress_blocks(t, pe, w1, w2):
    B, G, S, dh = t.shape
    nc = (S - CMP_BLOCK) // CMP_STRIDE + 1
    idx = jnp.arange(nc)[:, None] * CMP_STRIDE + jnp.arange(CMP_BLOCK)[None, :]
    blk = t[:, :, idx] + pe
    flat = blk.reshape(B, G, nc, CMP_BLOCK * dh)
    return jax.nn.silu(flat @ w1) @ w2

def compressed_attention(q, kc, vc, slopes):
    B, G, r, S, dh = q.shape
    nc = kc.shape[2]
    s = jnp.einsum('bgrqd,bgcd->bgrqc', q.astype(jnp.float32), kc.astype(jnp.float32)) * (dh ** -0.5)
    end = jnp.arange(nc) * CMP_STRIDE + CMP_BLOCK - 1
    dist = jnp.arange(S)[:, None] - end[None, :]
    valid = dist >= 0
    s = s - slopes[None, :, :, None, None] * dist.astype(jnp.float32)
    s = jnp.where(valid, s, NEG)
    p = jax.nn.softmax(s, axis=-1) * jnp.any(valid, axis=-1)[:, None].astype(jnp.float32)
    o = jnp.einsum('bgrqc,bgcd->bgrqd', p, vc.astype(jnp.float32))
    return o.astype(q.dtype), p

def select_blocks(p_cmp):
    p = p_cmp.sum(axis=2)
    S, nc = p.shape[2], p.shape[3]
    nsb = S // SLC_BLOCK
    ratio = SLC_BLOCK // CMP_STRIDE
    span = CMP_BLOCK // CMP_STRIDE
    offs = (jnp.arange(ratio)[:, None] + jnp.arange(span)[None, :]).reshape(-1)
    cidx = ratio * jnp.arange(nsb)[:, None] - offs[None, :]
    ok = (cidx >= 0) & (cidx < nc)
    imp = jnp.where(ok, p[..., jnp.clip(cidx, 0, nc - 1)], 0.0).sum(axis=-1)
    cur = jnp.arange(S) // SLC_BLOCK
    j = jnp.arange(nsb)
    causal = j[None, :] <= cur[:, None]
    forced = (j[None, :] == 0) | (j[None, :] == cur[:, None]) | (j[None, :] == cur[:, None] - 1)
    score = jnp.where(causal & forced, BIG, jnp.where(causal, imp, NEG))
    _, idx = lax.top_k(score, min(N_SELECT, nsb))
    return idx

def selected_attention(q, k, v, blk_idx, slopes):
    B, G, r, S, dh = q.shape
    nsb = S // SLC_BLOCK
    n_sel = blk_idx.shape[-1]
    nqc = S // Q_BLOCK
    kb = k.reshape(B, G, nsb, SLC_BLOCK, dh)
    vb = v.reshape(B, G, nsb, SLC_BLOCK, dh)
    qc = q.reshape(B, G, r, nqc, Q_BLOCK, dh).transpose(3, 0, 1, 2, 4, 5)
    ic = blk_idx.reshape(B, G, nqc, Q_BLOCK, n_sel).transpose(2, 0, 1, 3, 4)
    qpos = jnp.arange(S).reshape(nqc, Q_BLOCK)
    gather = jax.vmap(jax.vmap(lambda blocks, ix: blocks[ix]))

    def one_block(args):
        q_i, ix, qp = args
        k_sel = gather(kb, ix).astype(jnp.float32)
        v_sel = gather(vb, ix).astype(jnp.float32)
        kpos = ix[..., None] * SLC_BLOCK + jnp.arange(SLC_BLOCK)
        dist = (qp[None, None, :, None, None] - kpos)[:, :, None]
        s = jnp.einsum('bgrqd,bgqnkd->bgrqnk', q_i.astype(jnp.float32), k_sel) * (dh ** -0.5)
        s = s - slopes[None, :, :, None, None, None] * dist.astype(jnp.float32)
        s = jnp.where(dist >= 0, s, NEG).reshape(B, G, r, Q_BLOCK, n_sel * SLC_BLOCK)
        p = jax.nn.softmax(s, axis=-1)
        return jnp.einsum('bgrqk,bgqkd->bgrqd', p, v_sel.reshape(B, G, Q_BLOCK, n_sel * SLC_BLOCK, dh))

    o = lax.map(one_block, (qc, ic, qpos))
    return o.transpose(1, 2, 3, 0, 4, 5).reshape(B, G, r, S, dh).astype(q.dtype)

def second_inputs(seed: int = 0) -> dict:
    key = jax.random.key(seed)
    ks = jax.random.split(key, 20)
    D, L, dh = D_MODEL, DEPTH_2, HEAD_DIM
    nrm = lambda k, shape, fan: jax.random.normal(k, shape, jnp.float32) * (fan ** -0.5)
    return {
        'x': jax.random.normal(ks[0], (BATCH, SEQ, D), jnp.float32),
        'c': jax.random.normal(ks[1], (BATCH, D), jnp.float32),
        'w_ada': nrm(ks[2], (L, D, 3 * D), D) * 0.5,
        'b_ada': 0.01 * jax.random.normal(ks[3], (L, 3 * D), jnp.float32),
        'g_pre': 1.0 + 0.05 * jax.random.normal(ks[4], (L, D), jnp.float32),
        'g_post': 1.0 + 0.05 * jax.random.normal(ks[5], (L, D), jnp.float32),
        'w_in': nrm(ks[6], (L, D, D_IN_2), D),
        'pe_cmp_k': 0.02 * jax.random.normal(ks[7], (L, CMP_BLOCK, dh), jnp.float32),
        'pe_cmp_v': 0.02 * jax.random.normal(ks[8], (L, CMP_BLOCK, dh), jnp.float32),
        'w_cmp_k1': nrm(ks[9], (L, CMP_BLOCK * dh, CMP_HIDDEN), CMP_BLOCK * dh),
        'w_cmp_k2': nrm(ks[10], (L, CMP_HIDDEN, dh), CMP_HIDDEN),
        'w_cmp_v1': nrm(ks[11], (L, CMP_BLOCK * dh, CMP_HIDDEN), CMP_BLOCK * dh),
        'w_cmp_v2': nrm(ks[12], (L, CMP_HIDDEN, dh), CMP_HIDDEN),
        'w_o_nsa': nrm(ks[13], (L, NSA_WIDTH, D), NSA_WIDTH),
        'w_o_swa': nrm(ks[14], (L, SWA_WIDTH, D), SWA_WIDTH),
        'w_out': nrm(ks[15], (L, D, D), D),
        'sinks': jax.random.normal(ks[16], (L, SWA_HEADS), jnp.float32),
    }

def second_block(x, c, w_ada, b_ada, g_pre, g_post, w_in, pe_cmp_k, pe_cmp_v, w_cmp_k1, w_cmp_k2,
              w_cmp_v1, w_cmp_v2, w_o_nsa, w_o_swa, w_out, sinks):
    B, S, D = x.shape
    ra = NSA_HEADS // NSA_KV_HEADS
    rb = SWA_HEADS // SWA_KV_HEADS
    slopes_a = alibi_slopes(NSA_HEADS, NSA_KV_HEADS)
    slopes_b = alibi_slopes(SWA_HEADS, SWA_KV_HEADS)
    pts = split_points()
    for l in range(DEPTH_2):
        mod = c @ w_ada[l] + b_ada[l]
        shift, scale, gate = jnp.split(mod, 3, axis=-1)
        h = rms_norm_2(x, g_pre[l]) * (1.0 + scale[:, None, :]) + shift[:, None, :]
        proj = h @ w_in[l]
        q_a, kv_c, kv_s, kv_w, g_nsa, z_a, q_b, kv_b, z_b, merge = jnp.split(proj, pts, axis=-1)

        qa = q_heads(q_a, NSA_KV_HEADS, ra)
        kc_raw, vc_raw = jnp.split(kv_c, 2, axis=-1)
        ks_, vs_ = jnp.split(kv_s, 2, axis=-1)
        kw_, vw_ = jnp.split(kv_w, 2, axis=-1)
        kc = compress_blocks(kv_heads(kc_raw, NSA_KV_HEADS), pe_cmp_k[l], w_cmp_k1[l], w_cmp_k2[l])
        vc = compress_blocks(kv_heads(vc_raw, NSA_KV_HEADS), pe_cmp_v[l], w_cmp_v1[l], w_cmp_v2[l])
        o_cmp, p_cmp = compressed_attention(qa, kc, vc, slopes_a)
        blk_idx = select_blocks(p_cmp)
        o_slc = selected_attention(qa, kv_heads(ks_, NSA_KV_HEADS), kv_heads(vs_, NSA_KV_HEADS), blk_idx, slopes_a)
        o_win = banded_attention(qa, kv_heads(kw_, NSA_KV_HEADS), kv_heads(vw_, NSA_KV_HEADS), slopes_a, NSA_WINDOW)
        gts = jax.nn.sigmoid(g_nsa.reshape(B, S, 3, NSA_KV_HEADS, ra)).transpose(2, 0, 3, 4, 1)[..., None]
        o_a = gts[0] * o_cmp + gts[1] * o_slc + gts[2] * o_win
        y_a = (merge_heads(o_a) * jax.nn.silu(z_a)) @ w_o_nsa[l]

        qb = q_heads(q_b, SWA_KV_HEADS, rb)
        kb_, vb_ = jnp.split(kv_b, 2, axis=-1)
        o_b = banded_attention(qb, kv_heads(kb_, SWA_KV_HEADS), kv_heads(vb_, SWA_KV_HEADS), slopes_b,
                               SWA_WINDOW, sinks=sinks[l])
        y_b = (merge_heads(o_b) * jax.nn.silu(z_b)) @ w_o_swa[l]

        m_a, m_b = jnp.split(merge, 2, axis=-1)
        y = (jax.nn.sigmoid(m_a) * y_a + jax.nn.sigmoid(m_b) * y_b) @ w_out[l]
        x = x + gate[:, None, :] * rms_norm_2(y, g_post[l])
    return x


def setup_inputs(seed=0):
    out = dict(first_inputs(seed))
    for name, value in second_inputs(seed + 1).items():
        if name != "x":
            out[name + "_2"] = value
    return out


def reference(
    x, p, w_in, attn_norm, mla_q_norm, mla_w_uq, mla_kv_norm, mla_w_ukv, rel_bias, w_o,
    ffn_norm, w_gate, w_up, w_down, ple_norm, w_ple_gate, w_ple_proj, final_norm, c_2, w_ada_2,
    b_ada_2, g_pre_2, g_post_2, w_in_2, pe_cmp_k_2, pe_cmp_v_2, w_cmp_k1_2, w_cmp_k2_2,
    w_cmp_v1_2, w_cmp_v2_2, w_o_nsa_2, w_o_swa_2, w_out_2, sinks_2,
):
    x = first_block(
        x, p, w_in, attn_norm, mla_q_norm, mla_w_uq, mla_kv_norm, mla_w_ukv, rel_bias, w_o,
        ffn_norm, w_gate, w_up, w_down, ple_norm, w_ple_gate, w_ple_proj, final_norm,
    )
    return second_block(
        x, c_2, w_ada_2, b_ada_2, g_pre_2, g_post_2, w_in_2, pe_cmp_k_2, pe_cmp_v_2, w_cmp_k1_2,
        w_cmp_k2_2, w_cmp_v1_2, w_cmp_v2_2, w_o_nsa_2, w_o_swa_2, w_out_2, sinks_2,
    )


_drawn_inputs = setup_inputs


def setup_inputs(seed=0):
    import zlib

    import numpy as np

    out = dict(_drawn_inputs(seed))
    spreads = {}
    factors = {'mla_q_norm': 7.504,
     'mla_kv_norm': 4.815,
     'ple_norm': 4.344,
     'b_ada_2': 4.056,
     'g_post_2': 2.675,
     'pe_cmp_k_2': 64.0,
     'pe_cmp_v_2': 8.0}
    for name, (base, spread) in spreads.items():
        noise = np.random.default_rng([zlib.crc32(name.encode()), seed]).standard_normal(out[name].shape)
        drawn = base * np.exp(spread * noise) if base else spread * noise
        out[name] = __import__('jax').numpy.asarray(drawn.astype(out[name].dtype))
    for name, factor in factors.items():
        out[name] = (out[name] * factor).astype(out[name].dtype)
    return out
```

```python
import numpy as np

import concourse.bass as bass
from concourse import mybir

F32 = mybir.dt.float32
F32R = mybir.dt.float32r
ALU = mybir.AluOpType
ACT = mybir.ActivationFunctionType
AX_X = mybir.AxisListType.X

P = 128
S = 512
NT = S // P
D = 1024
KD = D // P
DEPTH = 2
EPS = 1e-6
BIG = 1e30

Q_LORA, KV_LORA, NOPE, ROPE, VDIM = 384, 256, 64, 32, 64
MLA_H, DSA_H, SB_H, IDX_H = 6, 5, 5, 8
HD = 64
TOPK = min(256, S // 4)
D_FF = -(-8 * D // (3 * 256)) * 256
FG = 2
FJ = D_FF // P // FG
PLE = 256
REL_BUCKETS, REL_MAX = 32, 128
MIX_H = MLA_H + DSA_H + SB_H

BLK = 8
SLOTS = 3

NSA_H = 8
CB, CS, CH = 32, 16, 256
NC = (S - CB) // CS + 1
NCP = 32

HEADS = [("m", 0), ("s", 0), ("m", 1), ("s", 1), ("m", 2), ("s", 2), ("m", 3), ("s", 3),
         ("m", 4), ("s", 4), ("m", 5), ("d", 0), ("d", 1), ("d", 2), ("d", 3), ("d", 4)]
UNITS = [(i, t) for i in range(MIX_H) for t in range(NT)]
LAG = 2


def attention_order(n_units, last_of_head, lag=LAG):
    order, due = [], None
    for u in range(n_units + lag):
        if u < n_units:
            order.append(("S", u))
        if u >= lag:
            order.append(("T", u - lag))
            if due is not None:
                order.append(("O", due))
                due = None
            if last_of_head(u - lag):
                due = u - lag
    if due is not None:
        order.append(("O", due))
    return order


def layer_groups():
    g = [("norm", 0), ("iw", 0)]
    g += [("iq", j) for j in range(4)] + [("dqik", 0)]
    g += [("cq", j) for j in range(3)] + [("ckv", j) for j in range(2)] + [("x", 0)]
    g += [("norm", 1), ("norm", 2)]
    g += [("ix", t, h) for t in range(1, NT) for h in range(IDX_H)]
    g += [("uq", h) for h in range(MLA_H)] + [("uk", j) for j in range(3)] + [("uv", t) for t in range(NT)]
    g += [("dq", j) for j in range(2)] + [("sq", j) for j in range(2)] + [("sk", j) for j in range(2)] + [("s4", 0)]
    g += [("tv", t) for t in range(NT)]
    g += [(k, *UNITS[u]) if k != "O" else (k, UNITS[u][0])
          for k, u in attention_order(len(UNITS), lambda u: UNITS[u][1] == NT - 1)]
    g += [("wo", j) for j in range(KD)]
    g += [("norm", 3)]
    for f in range(FG):
        for j in range(FJ):
            g += [("fg", f, j), ("fu", f, j)]
        g += [("fd", f, j) for j in range(KD)]
    g += [("norm", 4)]
    for j in range(KD):
        g += [("pp", j), ("pg", j)]
    return g


def place_groups(order):
    pools = {"S": (4, 5), "ix": (4, 5), "cS": (4, 5), "T": (6, 7), "cT": (6, 7)}
    turn, last, out = {}, {}, {}
    for n, key in enumerate(order):
        pool = pools.get(key[0], (0, 1, 2, 3))
        i = turn.get(pool, 0)
        turn[pool] = i + 1
        bank = pool[i % len(pool)]
        out[key] = (bank, n + 1, last.get(bank))
        last[bank] = key
    return out, last


LAYER_ORDER = layer_groups()
LAYER_GROUPS, LAYER_LAST = place_groups(LAYER_ORDER)

NORMS = [(0, KD, D), (KD, 3, Q_LORA), (KD + 3, 2, KV_LORA), (KD + 5, KD, D), (2 * KD + 5, KD, D)]
NORM_TILES = 3 * KD + 5
N_IX = (NT - 1) * IDX_H
MD_UNITS = [u for u in UNITS if HEADS[u[0]][0] != "s"]
SB_UNITS = [u for u in UNITS if HEADS[u[0]][0] == "s"]
MD_AT = {u: n for n, u in enumerate(MD_UNITS)}
SB_AT = {u: n for n, u in enumerate(SB_UNITS)}
N_DSA = DSA_H * NT

PER = dict(
    norm_sq=NORM_TILES, norm_sum=NORM_TILES, norm_ln=5, norm_rstd=5, norm_x=NORM_TILES, norm_hi=NORM_TILES,
    norm_lo=NORM_TILES,
    iw_out=1, iq_out=4, dqik_out=3, c_out=5, dk_out=2, kr_step=3, kr_copied=2,
    ix_relu=N_IX, ix_acc=N_IX, ix_masked=NT - 1, topk_max=TOPK // 8 * (NT - 1), topk_cut=TOPK // 8 * (NT - 1),
    sel_out=NT - 1, mq_out=MLA_H, mk_out=MLA_H, mv_out=NT, dq_out=2, sqk_out=6, tv_out=NT,
    biased=N_DSA, masked=len(MD_UNITS), exped=len(MD_UNITS), inverted=len(MD_UNITS), scaled=len(MD_UNITS),
    sb_abs=len(SB_UNITS), sb_exp=len(SB_UNITS), sb_ln=len(SB_UNITS), sb_neg=len(SB_UNITS), sb_scan=len(SB_UNITS),
    sb_log=len(SB_UNITS), sb_masked=len(SB_UNITS), sb_w=len(SB_UNITS),
    pt_act=len(MD_UNITS), pt_dve=len(SB_UNITS), o_hi=MIX_H, o_lo=MIX_H,
    h_wo=KD, silu_out=FG * FJ, ff_out=FG * FJ, ff_hi=FG * FJ, ff_lo=FG * FJ, h_ffn=FG * KD,
    p_hi=1, p_lo=1, sig_out=KD, ple_out=KD, h_ple=KD,
)

def released(key):
    kind, n = key[0], key[1]
    if kind == "norm":
        return [("norm_ln", n + 1)]
    if kind == "O":
        return [("o_lo", n + 1)]
    if kind == "x":
        return [("kr_step", 2), ("dk_out", 2)]
    if kind in ("S", "T"):
        u = key[1:]
        head, i = HEADS[n]
        if kind == "T":
            return [("pt_dve", SB_AT[u] + 1) if head == "s" else ("pt_act", MD_AT[u] + 1)]
        if head == "s":
            return [("sb_log", SB_AT[u] + 1)]
        return [("masked", MD_AT[u] + 1) if head == "m" else ("biased", i * NT + u[1] + 1)]
    return [{
        "iw": ("iw_out", 1), "iq": ("iq_out", n + 1), "dqik": ("dqik_out", 3), "cq": ("c_out", n + 1),
        "ckv": ("c_out", n + 4), "ix": ("ix_relu", (n - 1) * IDX_H + key[-1] + 1),
        "uq": ("mq_out", n + 1), "uk": ("mk_out", 2 * n + 2), "uv": ("mv_out", n + 1), "dq": ("dq_out", n + 1),
        "sq": ("sqk_out", n + 1), "sk": ("sqk_out", n + 3), "s4": ("sqk_out", 6), "tv": ("tv_out", n + 1),
        "wo": ("h_wo", n + 1), "fg": ("silu_out", n * FJ + key[-1] + 1), "fu": ("ff_out", n * FJ + key[-1] + 1),
        "fd": ("h_ffn", n * KD + key[-1] + 1), "pp": ("ple_out", n + 1), "pg": ("sig_out", n + 1),
    }[kind]]


SLOPES = [2.0 ** (-8.0 * (n + 1) / NSA_H) for n in range(NSA_H)]
assert S // 64 <= 16
SUBS = [(b, j, e) for j in range(4) for e in range(2) for b in ("sel", "win")] + \
       [("swa", j, e) for j in range(4) for e in range(2)]
TUNITS = [(i, t) for i in range(len(SUBS)) for t in range(NT)]
N_SWA = NSA_H


def tail_groups():
    g = [("mod", 0), ("norm", 0), ("norm", 1), ("gw", 0), ("kc", 0), ("vc", 0)]
    g += [("qa", j) for j in range(4)] + [("hid", 0), ("hid", 1)]
    g += [("ks", 0), ("kw", 0)] + [("hT", 0), ("hT", 1)] + [("vt", t) for t in range(NT)]
    g += [("kcT", 0), ("vcT", 0)]
    g += [("qb", j) for j in range(4)] + [("kb", 0)]
    for t in range(NT):
        g += [("cS", t)]
    for t in range(NT):
        g += [("cT", t)]
    for k, u in attention_order(len(TUNITS), lambda u: TUNITS[u][1] == NT - 1):
        g.append((k, *TUNITS[u]) if k != "O" else (k, TUNITS[u][0]))
    g += [("z", j) for j in range(8)]
    for j in range(KD):
        g += [("ma", j), ("ya", j), ("mb", j), ("yb", j)]
    g += [("wout", j) for j in range(KD)] + [("norm", 2)]
    return g


def shares_bank(key):
    return key[0] == "O" and key[1] % (4 if SUBS[key[1]][0] != "swa" else 2) != 0


def place_tail():
    out, last, turn = {}, {}, {}
    pools = {"S": (4, 5), "cS": (4, 5), "T": (6, 7), "cT": (6, 7), "hT": (6, 7)}
    for n, key in enumerate(tail_groups()):
        if shares_bank(key):
            bank = out["O", key[1] - 1][0]
            out[key] = (bank, n + 1, "same")
            last[bank] = key
            continue
        pool = pools.get(key[0], (0, 1, 2, 3))
        i = turn.get(pool, 0)
        turn[pool] = i + 1
        bank = pool[i % len(pool)]
        out[key] = (bank, n + 1, last.get(bank))
        last[bank] = key
    return out


TAIL_GROUPS = place_tail()


def tail_released(key):
    kind, n = key[0], key[1]
    if kind == "O":
        b, j, e = SUBS[n]
        return [("heads_out", j + 1 + (4 if b == "swa" else 0))]
    if kind == "S":
        return [("t_masked", n * NT + key[2] + 1)]
    if kind == "T":
        return [("t_pt", n * NT + key[2] + 1)]
    return [{
        "mod": ("mod_out", 1), "norm": ("t_ln", n + 1), "gw": ("gates_out", 1), "kc": ("cmp_in", 4), "vc": ("cmp_in", 8),
        "qa": ("q_out", n + 1), "qb": ("q_out", n + 5), "hid": ("hid_out", n + 1), "hT": ("hidT_out", n + 1),
        "ks": ("k_out", 1), "kw": ("k_out", 2), "kb": ("k_out", 3), "vt": ("v_out", n + 1),
        "kcT": ("kc_out", 2), "vcT": ("vc_out", 4), "cS": ("c_masked", n + 1), "cT": ("c_pt", n + 1),
        "z": ("z_out", n + 1), "ma": ("merge_out", 2 * n + 1), "mb": ("merge_out", 2 * n + 2),
        "ya": ("y_part", 2 * n + 1), "yb": ("y_part", 2 * n + 2), "wout": ("y2_out", n + 1),
    }[kind]]


ADA = 3 * KD
GAIN_PER_LAYER = NORM_TILES
G_FINAL = DEPTH * GAIN_PER_LAYER
G_PRE = G_FINAL + KD
G_POST = G_PRE + KD
G_BADA = G_POST + KD
G_C = G_BADA + 3 * KD
N_GAINS = G_C + KD


def tail_blocks():
    up = lambda n: -(-n // BLK) * BLK
    n = 2 + KD * (2 + 4 + 2)
    n = up(n) + KD // 2 * BLK
    n += KD * (4 + 1 + 8) + KD * (2 * KD + 2 * 4) + KD * KD
    return -(-up(n) // (BLK * SLOTS)) * BLK * SLOTS


def layer_blocks():
    up = lambda n: -(-n // BLK) * BLK
    n = 1 + 4 * KD + KD + 5 * KD + KD
    n = up(n + 3 * MLA_H + 2 * 3) + BLK
    n += 7 * KD + KD // 2 * BLK
    return up(n + KD * KD + FG * (2 * FJ * KD + KD * FJ) + KD * (2 + KD))


def build(nc, x_t, p_t, wstream, gains, rel_bias, c_rope_q, c_rope_k, c_onehot, c_eye, c_causal, c_strict,
          w_ada, w_cmp1, w_cmp2, pe_t, sinks, c_alibi, c_window, c_cmp, c_seen,
          out_t, layers=DEPTH):
    total_chunks = wstream.shape[0]
    layer_chunks = layer_blocks() // BLK
    sem_handles = {}

    def sem(name):
        if name not in sem_handles:
            sem_handles[name] = nc.semaphore(name).__enter__()
        return sem_handles[name]

    base = -(-nc.sbuf_base // 64) * 64
    cursor = [base]

    def sb(name, shape, dt=F32, offset=None):
        words = int(np.prod(shape[1:]))
        at_ = cursor[0] if offset is None else offset
        t = nc.alloc_sbuf_tensor_at(name, shape, dt, offset=at_)
        if offset is None:
            cursor[0] += -(-words * 4 // 32) * 32
        return t

    banks = [nc.psum_tensor(f"bank{b}", [P, S], F32).__enter__() for b in range(8)]

    raw = [sb(f"raw{s}", [P, BLK * P]) for s in range(SLOTS)]
    w_hi = [sb(f"w_hi{s}", [P, BLK * P], F32R) for s in range(SLOTS)]
    w_lo = [sb(f"w_lo{s}", [P, BLK * P], F32R) for s in range(SLOTS)]
    h = sb("h", [P, KD, S])
    act_hi = sb("act_hi", [P, KD, S], F32R)
    act_lo = sb("act_lo", [P, KD, S], F32R)
    norm_at = cursor[0]
    sq = sb("sq", [P, 2, S])
    ssum = sb("ssum", [P, S])
    rstd = sb("rstd", [P, S])
    xn = sb("xn", [P, 2, S])
    isc = sb("isc", [P, NT - 1, S], offset=norm_at)
    eye = sb("eye", [P, P])
    ones = sb("ones", [P, P])
    rope_q = sb("rope_q", [P, S])
    rope_k = sb("rope_k", [P, S])
    causal = sb("causal", [P, S])
    strict = sb("strict", [P, S])
    strict_neg = sb("strict_neg", [P, P])
    g_sb = sb("g_sb", [P, N_GAINS])
    eps_col = sb("eps_col", [P, 1])
    iw_w = sb("iw_w", [P, NT, IDX_H])
    stat_min = sb("stat_min", [P, 4])
    stat_sum = sb("stat_sum", [P, 4])
    stat_inv = sb("stat_inv", [P, 4])
    top8 = sb("top8", [P, NT - 1, 8])
    nc_small = cursor[0]
    cursor[0] += 4 * (5 * KD + NT * 3 * NSA_H)
    tail_region = cursor[0]
    bias = sb("bias", [P, DSA_H, S])
    region = cursor[0]
    rel_sb = sb("rel_sb", [REL_BUCKETS, DSA_H], offset=region)
    onehot = sb("onehot", [REL_BUCKETS, 640], offset=region + 64)
    rows_sb = sb("rows_sb", [DSA_H, 640], offset=region + 64 + 4 * 640)
    mq = sb("mq", [P, MLA_H, S])
    mk = sb("mk", [P, MLA_H, S])
    mv = sb("mv", [P, NT, MLA_H * VDIM])
    dq = sb("dq", [P, 3, S])
    dk = sb("dk", [P, S])
    tv = sb("tv", [P, NT, HD * (1 + SB_H)])
    share = cursor[0]
    iq = sb("iq", [P, 4, S], offset=share)
    ik = sb("ik", [P, S], offset=share + 4 * 4 * S)
    bq = sb("bq", [P, 3, S])
    bk = sb("bk", [P, 3, S])
    work = cursor[0]
    c_raw = sb("c_raw", [P, 5, S])
    c_hi = sb("c_hi", [P, 5, S], F32R)
    c_lo = sb("c_lo", [P, 5, S], F32R)
    top = cursor[0]
    cursor[0] = work
    xs = sb("xs", [P, 3, S])
    z1 = sb("z1", [P, 2, S])
    pr = sb("pr", [P, 3, S])
    pt = sb("pt", [P, 2, NT, S])
    relu = z1
    kr = sb("kr", [P, 2, S], offset=work + 5 * 4 * S * 3)
    top = max(top, cursor[0], work + 5 * 4 * S * 3 + 2 * 4 * S)
    cursor[0] = region
    ff_hi = sb("ff_hi", [P, FJ, S], F32R)
    ff_lo = sb("ff_lo", [P, FJ, S], F32R)
    gate = sb("gate", [P, 2, S])
    ffx = sb("ffx", [P, 2, S])
    p_raw = sb("p_raw", [P, 2, S])
    pp_hi = sb("pp_hi", [P, 2, S], F32R)
    pp_lo = sb("pp_lo", [P, 2, S], F32R)
    top = max(top, cursor[0])
    ada = sb("ada", [P, 2, D])
    mod_acc = sb("mod_acc", [P, 3 * D])
    top = max(top, cursor[0])
    mod = sb("mod", [P, 3 * KD], offset=nc_small)
    gain_pre = sb("gain_pre", [P, KD], offset=nc_small + 4 * 3 * KD)
    gain_post = sb("gain_post", [P, KD], offset=nc_small + 4 * 4 * KD)
    gates = sb("gates", [P, NT, 3 * NSA_H], offset=nc_small + 4 * 5 * KD)
    cursor[0] = tail_region
    KB = 1024
    qa = sb("qa", [P, 4, S])
    w1_at = cursor[0]
    alibi = sb("alibi", [P, NSA_H, S])
    window = sb("window", [P, NSA_H, 2 * P + 1])
    qb_at = cursor[0]
    qb = sb("qb", [P, 4, S])
    w1 = sb("w1", [P, 2, CB // 2, CH], offset=w1_at)
    assert w1_at + 32 * KB <= cursor[0]
    cmp_mask = sb("cmp_mask", [P, NT, NSA_H * NCP])
    ks = sb("ks", [P, S])
    kw = sb("kw", [P, S])
    kb = sb("kb", [P, S])
    vt = sb("vt", [P, NT, 3 * P])
    kct = sb("kct", [P, 2 * NCP])
    vbd = sb("vbd", [P, P])
    cpt = sb("cpt", [P, 2, S])
    cst = sb("cst", [P, 4, NSA_H])
    seen = sb("seen", [P, NT])
    sink_row = sb("sink_row", [1, NSA_H])
    ones_row = sb("ones_row", [1, P])
    pe_sb = sb("pe_sb", [P, 2, CB // 2])
    w2 = sb("w2", [P, 2, 2, HD])
    tail_work = cursor[0]
    xs2 = sb("xs2", [P, 3, S])
    pr2 = sb("pr2", [P, 3, S])
    pt2 = sb("pt2", [P, 2, NT, S])
    top = max(top, cursor[0])
    cursor[0] = tail_work
    cmp_x = sb("cmp_x", [P, 2, CB // 2, 2 * NCP])
    hid = sb("hid", [2 * NCP, 2, CH])
    hid_t = sb("hid_t", [P, 2, 2, 2 * NCP])
    assert cursor[0] <= tail_work + 12 * KB
    cursor[0] = w1_at
    u_hi = sb("u_hi", [P, 8, S], F32R)
    silu_z = sb("silu_z", [P, 2, S])
    ux = sb("ux", [P, 2, S])
    assert cursor[0] <= qb_at
    cursor[0] = qb_at + 8 * KB
    u_lo = sb("u_lo", [P, 8, S], F32R)
    y_hi = sb("y_hi", [P, KD, S], F32R)
    y_lo = sb("y_lo", [P, KD, S], F32R)
    yx = sb("yx", [P, 4, S], offset=tail_region)
    y2 = sb("y2", [P, KD, S], offset=w1_at)
    top = max(top, cursor[0])
    assert top <= nc.sbuf_usable_end
    bias_dram = nc.dram_tensor("bias_rows", (DSA_H, 640), F32, kind="Internal")

    n_groups = len(LAYER_ORDER)
    block = nc.Block().__enter__()

    class Layer:

        def __init__(self, n):
            self.n = n

        def at(self, name, count):
            return sem(name), self.n * PER.get(name, 0) + count

        def psum(self, *key):
            bank, place, _ = LAYER_GROUPS[key]
            return banks[bank], (sem("psum_ready"), self.n * n_groups + place)

    class Tail(Layer):

        def psum(self, *key):
            bank, place, _ = TAIL_GROUPS[key]
            return banks[bank], (sem("psum_ready"), self.n * n_groups + place)

    def width(t):
        return (t + 1) * P

    def keys_of(sub, t):
        return (0, t + 1) if SUBS[sub][0] != "swa" else (max(t - 1, 0), min(t, 1) + 1)

    def half(i):
        return slice(64 * (i % 2), 64 * (i % 2) + 64)

    @block.sync
    def _(sp):
        for dst, src in ((g_sb, gains), (eye, c_eye), (rope_q, c_rope_q), (rope_k, c_rope_k),
                         (causal, c_causal), (strict, c_strict)):
            sp.dma_start(dst[:], src).then_inc(sem("consts_in"), 16)
        sp.dma_start(h[:], x_t).then_inc(sem("x_in"), 16)
        sp.dma_start(rel_sb[:], rel_bias).then_inc(sem("rel_in"), 16)
        sp.dma_start(onehot[:], c_onehot).then_inc(sem("rel_in"), 16)
        for s in range(SLOTS):
            sp.dma_start(raw[s][:], wstream[s]).then_inc(sem(f"raw_in{s}"), 16)
        sp.wait_ge(sem("rows_out"), 2)
        sp.dma_start(bias_dram.ap(), rows_sb[:]).then_inc(sem("rows_stored"), 16)
        sp.wait_ge(sem("rows_stored"), 16)
        for n in range(DSA_H):
            sp.dma_start(bias[:, n, :], bass.AP(bias_dram, n * 640, [[1, P], [1, S]]))\
                .then_inc(sem("bias_in"), 16)
        with sp.Fori(1, total_chunks // SLOTS) as i:
            for s in range(SLOTS):
                sp.wait_ge(sem("split_lo"), i * SLOTS + (s + 1 - SLOTS))
                sp.dma_start(raw[s][:], wstream[i * SLOTS + s]).then_inc(sem(f"raw_in{s}"), 16)
        for k in range(KD):
            sp.wait_ge(sem("x_final"), k + 1)
            sp.dma_start(out_t[:, k, :], h[:, k, :]).then_inc(sem("stored"), 16)
        sp.wait_ge(sem("stored"), 16 * KD)

    @block.gpsimd
    def _(pool):
        pool.memset(ones[:], 1.0).then_inc(sem("ones_set"), 1)
        pool.memset(eps_col[:], EPS).then_inc(sem("eps_set"), 1)

        def split(s, count, used):
            pool.wait_ge(sem(f"raw_in{s}"), count)
            if used is not None:
                pool.wait_ge(sem("chunk_used"), used)
            pool.sem_inc(sem("slot_turn"), 1)
            pool.tensor_scalar(w_hi[s][:], raw[s][:], 1.0, 0.0, ALU.mult, ALU.add).then_inc(sem("split_hi"), 1)
            return s

        def rest(s, hi_count):
            pool.wait_ge(sem("split_hi"), hi_count)
            pool.tensor_tensor(w_lo[s][:], raw[s][:], w_hi[s][:].bitcast(F32), ALU.subtract)\
                .then_inc(sem("split_lo"), 1)

        for s in range(SLOTS):
            split(s, 16, None)
            rest(s, s + 1)
        with pool.Fori(1, total_chunks // SLOTS) as i:
            for s in range(SLOTS):
                landed, used, hi_done = [pool.snap(v) for v in (i * 16 + 16, i * SLOTS + (s + 1 - SLOTS),
                                                                i * SLOTS + (s + 1))]
                split(s, landed, used)
                rest(s, hi_done)

    @block.tensor
    def _(pe):
        stream = {"block": 0, "pending": 0}

        def finish(ins, last):
            if last:
                ins.then_inc(sem("psum_ready"), 1)
            elif stream["pending"]:
                ins.then_inc(sem("chunk_used"), stream["pending"])
                stream["pending"] = 0
            return ins

        def open_group(L, key):
            if isinstance(L, Tail):
                bank, _, prev = TAIL_GROUPS[key]
                if prev != "same":
                    for name, count in released(LAYER_LAST[bank]) if prev is None else tail_released(prev):
                        pe.wait_ge(*Layer(L.n - (prev is None)).at(name, count))
                return banks[bank]
            bank, _, prev = LAYER_GROUPS[key]
            n = L.n
            if prev is None:
                n, prev = n - 1, LAYER_LAST[bank]
            if n >= 0:
                for name, count in released(prev):
                    pe.wait_ge(*Layer(n).at(name, count))
            return banks[bank]

        def next_block(n=1):
            b = stream["block"]
            chunk = b // BLK
            assert (b + n - 1) // BLK == chunk
            if b % BLK == 0:
                pe.wait_ge(sem("split_lo"), chunk + 1)
            stream["block"] = b + n
            cols = slice(b % BLK * P, (b % BLK + n) * P)
            return w_hi[chunk % SLOTS][:, cols], w_lo[chunk % SLOTS][:, cols]

        def end_block():
            if stream["block"] % BLK == 0:
                stream["pending"] += 1

        def align():
            if stream["block"] % BLK:
                stream["block"] += BLK - stream["block"] % BLK
                stream["pending"] += 1

        def linear(L, key, tiles, ready=None):
            acc = open_group(L, key)
            n = len(tiles)
            for k, (hi, lo) in enumerate(tiles):
                if ready is not None:
                    pe.wait_ge(*ready(k))
                wh, wl = next_block()
                finish(pe.matmul(acc[:], wh, hi, start=k == 0, stop=False), False)
                finish(pe.matmul(acc[:], wh, lo, start=False, stop=False), False)
                ins = pe.matmul(acc[:], wl, hi, start=False, stop=k == n - 1)
                end_block()
                finish(ins, k == n - 1)

        def tiles_of(hi, lo, n, first=0):
            return [(hi[:, k, :], lo[:, k, :]) for k in range(first, first + n)]

        def token_major(L, kind, hi, lo, n, first=0, per_chunk=2, n_blocks=3):
            accs = [open_group(L, (kind, t)) for t in range(NT)]
            align()
            for k in range(n):
                wh, wl = next_block(n_blocks)
                for t in range(NT):
                    cols = slice(t * P, t * P + P)
                    o = accs[t][:, 0:n_blocks * P]
                    a_hi, a_lo = hi[:, first + k, cols], lo[:, first + k, cols]
                    finish(pe.matmul(o, a_hi, wh, start=k == 0, stop=False), False)
                    finish(pe.matmul(o, a_lo, wh, start=False, stop=False), False)
                    ins = pe.matmul(o, a_hi, wl, start=False, stop=k == n - 1)
                    finish(ins, k == n - 1)
                if k % per_chunk == per_chunk - 1 or k == n - 1:
                    align()

        def norm_sum(L, i):
            first, n, _ = NORMS[i]
            acc = open_group(L, ("norm", i))
            pe.wait_ge(*L.at("norm_sum", first + n))
            finish(pe.matmul(acc[:], ones[:], ssum[:], start=True, stop=True), True)

        def attention(L):
            def scores(i, t):
                kind, n = HEADS[i]
                acc = open_group(L, ("S", i, t))
                cols = slice(t * P, t * P + P)
                if kind == "m":
                    pe.wait_ge(*L.at("mq_out", n + 1))
                    pe.wait_ge(*L.at("mk_out", n + 1))
                    pe.wait_ge(*L.at("kr_copied", 2))
                    q, k = mq[:, n, cols], mk[:, n, 0:width(t)]
                elif kind == "d":
                    pe.wait_ge(*L.at("dq_out", 2))
                    pe.wait_ge(*L.at("dqik_out", 3))
                    pe.wait_ge(*L.at("dk_out", 2))
                    q, k = dq[half(n), n // 2, cols], dk[half(n), 0:width(t)]
                else:
                    pe.wait_ge(*L.at("sqk_out", 6))
                    q, k = bq[half(n), n // 2, cols], bk[half(n), n // 2, 0:width(t)]
                finish(pe.matmul(acc[:, 0:width(t)], q, k, start=True, stop=True), True)

            def transpose(i, t):
                kind, n = HEADS[i]
                acc = open_group(L, ("T", i, t))
                if kind == "s":
                    pe.wait_ge(*L.at("sb_w", SB_AT[i, t] + 1))
                else:
                    pe.wait_ge(*L.at("scaled", MD_AT[i, t] + 1))
                src = pr[:, (i * NT + t) % 3, :]
                for k in range(t + 1):
                    cols = slice(k * P, k * P + P)
                    finish(pe.transpose(acc[:, cols], src[:, cols], eye[:]), k == t)

            def output(i):
                kind, n = HEADS[i]
                acc = open_group(L, ("O", i))
                if kind == "s":
                    pe.wait_ge(*L.at("pt_dve", SB_AT[i, NT - 1] + 1))
                else:
                    pe.wait_ge(*L.at("pt_act", MD_AT[i, NT - 1] + 1))
                if kind == "m":
                    pe.wait_ge(*L.at("mv_out", NT))
                else:
                    pe.wait_ge(*L.at("tv_out", NT))
                for k in range(NT):
                    if kind == "m":
                        v = mv[:, k, n * VDIM:(n + 1) * VDIM]
                    elif kind == "d":
                        v = tv[:, k, 0:HD]
                    else:
                        v = tv[:, k, HD * (1 + n):HD * (2 + n)]
                    finish(pe.matmul(acc[half(i), k * P:S], v, pt[:, i % 2, k, k * P:S], start=k == 0,
                                     stop=k == NT - 1), k == NT - 1)

            for kind, u in attention_order(len(UNITS), lambda u: UNITS[u][1] == NT - 1):
                if kind == "S":
                    scores(*UNITS[u])
                elif kind == "T":
                    transpose(*UNITS[u])
                else:
                    output(UNITS[u][0])

        pe.wait_ge(sem("ones_set"), 1)
        pe.wait_ge(sem("consts_in"), 16 * 6)
        pe.wait_ge(sem("rel_in"), 32)
        for c in range(2):
            pe.matmul(banks[c][0:DSA_H, 0:320], rel_sb[:], onehot[:, c * 320:(c + 1) * 320], start=True, stop=True)\
                .then_inc(sem("rows_ready"), 1)
        pe.wait_ge(sem("rows_out"), 2)
        for layer in range(layers):
            L = Layer(layer)
            stream["block"] = layer * layer_chunks * BLK
            hn = tiles_of(act_hi, act_lo, KD)
            norm_sum(L, 0)
            acc = open_group(L, ("iw", 0))
            pe.wait_ge(*L.at("norm_lo", KD))
            wh, wl = next_block()
            for t in range(NT):
                for k in range(KD):
                    cols = slice(t * P, t * P + P)
                    o = acc[:, t * IDX_H:(t + 1) * IDX_H]
                    ws = slice(k * IDX_H, (k + 1) * IDX_H)
                    finish(pe.matmul(o, act_hi[:, k, cols], wh[:, ws], start=k == 0, stop=False), False)
                    finish(pe.matmul(o, act_lo[:, k, cols], wh[:, ws], start=False, stop=False), False)
                    ins = pe.matmul(o, act_hi[:, k, cols], wl[:, ws], start=False, stop=k == KD - 1)
                    finish(ins, t == NT - 1 and k == KD - 1)
            end_block()
            for j in range(4):
                linear(L, ("iq", j), hn)
            linear(L, ("dqik", 0), hn)
            for j in range(3):
                linear(L, ("cq", j), hn)
            for j in range(2):
                linear(L, ("ckv", j), hn)
            linear(L, ("x", 0), hn)
            norm_sum(L, 1)
            norm_sum(L, 2)
            for t in range(1, NT):
                for n in range(IDX_H):
                    acc = open_group(L, ("ix", t, n))
                    pe.wait_ge(*L.at("dqik_out", 3))
                    pe.wait_ge(*L.at("iq_out", 4))
                    finish(pe.matmul(acc[:, 0:width(t)], iq[half(n), n // 2, t * P:t * P + P],
                                     ik[half(n), 0:width(t)], start=True, stop=True), True)
            for n in range(MLA_H):
                linear(L, ("uq", n), tiles_of(c_hi, c_lo, 3), lambda k: L.at("norm_lo", KD + k + 1))
            for j in range(3):
                linear(L, ("uk", j), tiles_of(c_hi, c_lo, 2, 3), lambda k: L.at("norm_lo", KD + 3 + k + 1))
            token_major(L, "uv", c_hi, c_lo, 2, 3)
            for j in range(2):
                linear(L, ("dq", j), hn)
            for j in range(2):
                linear(L, ("sq", j), hn)
            for j in range(2):
                linear(L, ("sk", j), hn)
            linear(L, ("s4", 0), hn)
            token_major(L, "tv", act_hi, act_lo, KD)
            attention(L)
            for j in range(KD):
                linear(L, ("wo", j), hn, lambda k: L.at("o_lo", 2 * k + 2))
            norm_sum(L, 3)
            for f in range(FG):
                for j in range(FJ):
                    ready = (lambda k: L.at("norm_lo", NORMS[3][0] + k + 1)) if f == j == 0 else None
                    linear(L, ("fg", f, j), hn, ready)
                    linear(L, ("fu", f, j), hn)
                for j in range(KD):
                    ready = (lambda k: L.at("ff_lo", f * FJ + k + 1)) if j == 0 else None
                    linear(L, ("fd", f, j), tiles_of(ff_hi, ff_lo, FJ), ready)
            norm_sum(L, 4)
            for j in range(KD):
                linear(L, ("pp", j), tiles_of(pp_hi, pp_lo, 2), lambda k: L.at("p_lo", 1))
                ready = (lambda k: L.at("norm_lo", NORMS[4][0] + k + 1)) if j == 0 else None
                linear(L, ("pg", j), hn, ready)
            align()
            assert stream["block"] <= (layer + 1) * layer_chunks * BLK
            while stream["block"] < (layer + 1) * layer_chunks * BLK:
                stream["block"] += BLK
                stream["pending"] += 1

        L = Tail(layers)
        stream["block"] = layers * layer_chunks * BLK
        acc = open_group(L, ("mod", 0))
        pe.wait_ge(sem("ada_summed"), ADA)
        for n in range(3 * KD):
            finish(pe.matmul(acc[:, n:n + 1], mod_acc[:, n * P:(n + 1) * P], ones[:, 0:1], start=True, stop=True),
                   n == 3 * KD - 1)
        for n in range(2):
            acc = open_group(L, ("norm", n))
            pe.wait_ge(sem("t_sum"), KD * (n + 1))
            finish(pe.matmul(acc[:], ones[:], ssum[:], start=True, stop=True), True)
        acc = open_group(L, ("gw", 0))
        for k in range(KD):
            pe.wait_ge(sem("t_lo"), k + 1)
        wh, wl = next_block(2)
        for t in range(NT):
            for k in range(KD):
                cols, ws = slice(t * P, t * P + P), slice(k * 3 * NSA_H, (k + 1) * 3 * NSA_H)
                o = acc[:, t * 3 * NSA_H:(t + 1) * 3 * NSA_H]
                finish(pe.matmul(o, act_hi[:, k, cols], wh[:, ws], start=k == 0, stop=False), False)
                finish(pe.matmul(o, act_lo[:, k, cols], wh[:, ws], start=False, stop=False), False)
                finish(pe.matmul(o, act_hi[:, k, cols], wl[:, ws], start=False, stop=k == KD - 1),
                       t == NT - 1 and k == KD - 1)
        hn = tiles_of(act_hi, act_lo, KD)
        linear(L, ("kc", 0), hn)
        linear(L, ("vc", 0), hn)
        for j in range(4):
            linear(L, ("qa", j), hn)
        pe.wait_ge(sem("cmp_w_in"), 16 * 2)
        for n in range(2):
            acc = open_group(L, ("hid", n))
            pe.wait_ge(sem("cmp_in"), 4 * n + 4)
            for k in range(CB // 2):
                finish(pe.matmul(acc[0:2 * NCP, 0:CH], cmp_x[:, n, k, :], w1[:, n, k, :], start=k == 0,
                                 stop=k == CB // 2 - 1), k == CB // 2 - 1)
        linear(L, ("ks", 0), hn)
        linear(L, ("kw", 0), hn)
        for n in range(2):
            acc = open_group(L, ("hT", n))
            pe.wait_ge(sem("hid_out"), n + 1)
            for c in range(2):
                finish(pe.transpose(acc[:, c * 2 * NCP:(c + 1) * 2 * NCP], hid[:, n, c * P:(c + 1) * P],
                                    eye[0:2 * NCP, 0:2 * NCP]), c == 1)
        token_major(L, "vt", act_hi, act_lo, KD)
        acc = open_group(L, ("kcT", 0))
        pe.wait_ge(sem("hidT_out"), 1)
        for c in range(2):
            finish(pe.matmul(acc[0:HD, 0:2 * NCP], w2[:, 0, c, :], hid_t[:, 0, c, :], start=c == 0, stop=c == 1), c == 1)
        acc = open_group(L, ("vcT", 0))
        pe.wait_ge(sem("hidT_out"), 2)
        for c in range(2):
            finish(pe.matmul(acc[0:2 * NCP, 0:HD], hid_t[:, 1, c, :], w2[:, 1, c, :], start=c == 0, stop=c == 1), c == 1)
        for j in range(4):
            linear(L, ("qb", j), hn)
        linear(L, ("kb", 0), hn)
        for t in range(NT):
            acc = open_group(L, ("cS", t))
            pe.wait_ge(sem("kc_out"), 2)
            pe.wait_ge(sem("q_out"), 4)
            for j in range(4):
                finish(pe.matmul(acc[:, j * 2 * NCP:(j + 1) * 2 * NCP], qa[:, j, t * P:t * P + P], kct[:],
                                 start=True, stop=True), j == 3)
        for t in range(NT):
            acc = open_group(L, ("cT", t))
            pe.wait_ge(sem("c_scaled"), t + 1)
            for c in range(2):
                finish(pe.transpose(acc[:, c * P:(c + 1) * P], xs2[:, t % 3, c * P:(c + 1) * P], eye[:]), c == 1)

        def t_scores(i, t):
            b, j, e = SUBS[i]
            acc = open_group(L, ("S", i, t))
            first, n = keys_of(i, t)
            pe.wait_ge(sem("q_out"), 8)
            pe.wait_ge(sem("k_out"), 3)
            q = (qb if b == "swa" else qa)[half(e), j, t * P:t * P + P]
            k = {"sel": ks, "win": kw, "swa": kb}[b][half(e), first * P:(first + n) * P]
            finish(pe.matmul(acc[:, 0:n * P], q, k, start=True, stop=True), b != "swa")
            if b == "swa":
                head = j + 4 * e
                finish(pe.matmul(acc[:, n * P:n * P + 1], ones_row[:], sink_row[:, head:head + 1], start=True,
                                 stop=True), True)

        def t_transpose(i, t):
            acc = open_group(L, ("T", i, t))
            pe.wait_ge(sem("t_scaled"), i * NT + t + 1)
            _, n = keys_of(i, t)
            for k in range(n):
                cols = slice(k * P, k * P + P)
                finish(pe.transpose(acc[:, cols], pr2[:, (i * NT + t) % 3, cols], eye[:]), k == n - 1)

        def t_output(i):
            b, j, e = SUBS[i]
            acc = open_group(L, ("O", i))
            pe.wait_ge(sem("t_pt"), (i + 1) * NT)
            if b == "sel" and e == 0:
                pe.wait_ge(sem("vc_out"), 4)
                pe.wait_ge(sem("c_pt"), NT)
                rows = half(j)
                finish(pe.matmul(acc[:], vbd[rows, :], cpt[rows, j // 2, :], start=True, stop=False), False)
            pe.wait_ge(sem("v_out"), NT)
            v0 = {"sel": 0, "win": P, "swa": 2 * P}[b] + e * HD
            if b == "swa":
                for t in range(NT):
                    first, n = keys_of(i, t)
                    for k in range(first, first + n):
                        cols = slice(t * P, t * P + P)
                        finish(pe.matmul(acc[half(e), cols], vt[:, k, v0:v0 + HD], pt2[:, i % 2, k, cols],
                                         start=k == first, stop=k == first + n - 1), t == NT - 1 and k == NT - 1)
            else:
                for k in range(NT):
                    last = k == NT - 1
                    finish(pe.matmul(acc[half(e), k * P:S], vt[:, k, v0:v0 + HD], pt2[:, i % 2, k, k * P:S],
                                     start=False, stop=last and b == "win"), last)

        pe.wait_ge(sem("sinks_in"), 16)
        pe.wait_ge(sem("ones_row_set"), 1)
        for kind, u in attention_order(len(TUNITS), lambda u: TUNITS[u][1] == NT - 1):
            if kind == "S":
                t_scores(*TUNITS[u])
            elif kind == "T":
                t_transpose(*TUNITS[u])
            else:
                t_output(TUNITS[u][0])
        for j in range(8):
            linear(L, ("z", j), hn)
        for j in range(KD):
            linear(L, ("ma", j), hn)
            linear(L, ("ya", j), tiles_of(u_hi, u_lo, 4), lambda k: L.at("u_lo", k + 1))
            linear(L, ("mb", j), hn)
            linear(L, ("yb", j), tiles_of(u_hi, u_lo, 4, 4), lambda k: L.at("u_lo", k + 5))
        for j in range(KD):
            linear(L, ("wout", j), tiles_of(y_hi, y_lo, KD), lambda k: L.at("y_lo", k + 1))
        acc = open_group(L, ("norm", 2))
        pe.wait_ge(sem("t_sum"), 3 * KD)
        finish(pe.matmul(acc[:], ones[:], ssum[:], start=True, stop=True), True)

    @block.scalar
    def _(act):
        def use_exp_ln():
            act.preload_act_table_set("natural_log_exp_and_others")

        def squares(L, i, src, ready):
            first, n, _ = NORMS[i]
            for k in range(n):
                act.wait_ge(*ready(k))
                if first + k >= 2 or L.n:
                    act.wait_ge(*L.at("norm_sum", first + k - 1))
                act.activation(sq[:, (first + k) % 2, :], src(k), ACT.Square)\
                    .then_inc(sem("norm_sq"), 1)

        def norm_rest(L, i, hi, first_tile=0):
            first, n, dim = NORMS[i]
            ps, ready = L.psum("norm", i)
            act.wait_ge(*ready)
            if i or L.n:
                act.wait_ge(*L.at("norm_x", first))
            act.activation(rstd[:], ps[:], ACT.Ln, bias=eps_col[:], scale=1.0 / dim).then_inc(sem("norm_ln"), 1)
            act.wait_ge(*L.at("norm_ln", i + 1))
            act.activation(rstd[:], rstd[:], ACT.Exp, scale=-0.5).then_inc(sem("norm_rstd"), 1)
            for k in range(n):
                act.wait_ge(*L.at("norm_x", first + k + 1))
                act.activation(hi[:, first_tile + k, :], xn[:, (first + k) % 2, :], ACT.Copy)\
                    .then_inc(sem("norm_hi"), 1)

        def take(L, key, name, pairs, scale=1.0):
            ps, ready = L.psum(*key)
            act.wait_ge(*ready)
            for dst, rows in pairs:
                act.activation(dst, ps[rows, :], ACT.Copy, scale=scale).then_inc(sem(name), 1)

        full, lower, upper = slice(0, P), slice(0, 64), slice(64, P)

        def ada_load(n):
            if n < ADA:
                if n >= 2:
                    act.wait_ge(sem("ada_summed"), n - 1)
                k, c = divmod(n, 3)
                act.dma_start(ada[:, n % 2, :], w_ada[:, k, c * D:(c + 1) * D]).then_inc(sem(f"ada_in{n % 2}"), 16)

        act.wait_ge(sem("x_in"), 16)
        act.wait_ge(sem("eps_set"), 1)
        act.wait_ge(sem("consts_in"), 16 * 6)
        for layer in range(layers):
            L = Layer(layer)
            use_exp_ln()
            if layer == 0:
                squares(L, 0, lambda k: h[:, k, :], lambda k: (sem("x_in"), 16))
            else:
                squares(L, 0, lambda k: h[:, k, :], lambda k: Layer(layer - 1).at("h_ple", k + 1))
            norm_rest(L, 0, act_hi)
            ps, ready = L.psum("iw", 0)
            act.wait_ge(*ready)
            act.activation(iw_w[:].rearrange("p t h -> p (t h)"), ps[:, 0:NT * IDX_H], ACT.Copy,
                           scale=IDX_H ** -0.5).then_inc(sem("iw_out"), 1)
            for j in range(4):
                take(L, ("iq", j), "iq_out", [(iq[:, j, :], full)], HD ** -0.5)
            ps, ready = L.psum("dqik", 0)
            act.wait_ge(*ready)
            act.activation(dq[lower, 2, :], ps[lower, :], ACT.Copy, scale=-HD ** -0.5).then_inc(sem("dqik_out"), 1)
            act.activation(ik[lower, :], ps[upper, :], ACT.Copy).then_inc(sem("dqik_out"), 1)
            act.activation(ik[upper, :], ps[upper, :], ACT.Copy).then_inc(sem("dqik_out"), 1)
            for j in range(3):
                take(L, ("cq", j), "c_out", [(c_raw[:, j, :], full)])
            for j in range(2):
                take(L, ("ckv", j), "c_out", [(c_raw[:, 3 + j, :], full)])
            ps, ready = L.psum("x", 0)
            act.wait_ge(*ready)
            act.activation(dk[lower, :], ps[lower, :], ACT.Copy).then_inc(sem("dk_out"), 1)
            act.activation(dk[upper, :], ps[lower, :], ACT.Copy).then_inc(sem("dk_out"), 1)
            squares(L, 1, lambda k: c_raw[:, k, :], lambda k: L.at("c_out", k + 1))
            norm_rest(L, 1, c_hi, 0)
            squares(L, 2, lambda k: c_raw[:, 3 + k, :], lambda k: L.at("c_out", 4 + k))
            norm_rest(L, 2, c_hi, 3)
            act.wait_ge(*L.at("kr_step", 3))
            for r in (64, 96):
                act.activation(mk[r:r + 32, :, :], kr[64:96, 0, :].unsqueeze(1).broadcast_to([32, MLA_H, S]),
                               ACT.Copy).then_inc(sem("kr_copied"), 1)
            u = 0
            for t in range(1, NT):
                for n in range(IDX_H):
                    ps, ready = L.psum("ix", t, n)
                    act.wait_ge(*ready)
                    if u >= 2:
                        act.wait_ge(*L.at("ix_acc", u - 1))
                    act.activation(relu[:, u % 2, 0:width(t)], ps[:, 0:width(t)], ACT.Relu)\
                        .then_inc(sem("ix_relu"), 1)
                    u += 1
            for j in range(3):
                take(L, ("uk", j), "mk_out", [(mk[lower, 2 * j, :], lower), (mk[lower, 2 * j + 1, :], upper)])
            for t in range(NT):
                ps, ready = L.psum("uv", t)
                act.wait_ge(*ready)
                act.activation(mv[:, t, :], ps[:, 0:MLA_H * VDIM], ACT.Copy).then_inc(sem("mv_out"), 1)
            for j in range(2):
                take(L, ("dq", j), "dq_out", [(dq[:, j, :], full)], -HD ** -0.5)
            for j in range(2):
                take(L, ("sq", j), "sqk_out", [(bq[:, j, :], full)], HD ** -0.5)
            for j in range(2):
                take(L, ("sk", j), "sqk_out", [(bk[:, j, :], full)])
            ps, ready = L.psum("s4", 0)
            act.wait_ge(*ready)
            act.activation(bq[lower, 2, :], ps[lower, :], ACT.Copy, scale=HD ** -0.5).then_inc(sem("sqk_out"), 1)
            act.activation(bk[lower, 2, :], ps[upper, :], ACT.Copy).then_inc(sem("sqk_out"), 1)
            for t in range(NT):
                ps, ready = L.psum("tv", t)
                act.wait_ge(*ready)
                act.activation(tv[:, t, :], ps[:, 0:HD * (1 + SB_H)], ACT.Copy).then_inc(sem("tv_out"), 1)

            def before_scores_out(i, t):
                u = i * NT + t
                if u >= 3:
                    act.wait_ge(*L.psum("T", *UNITS[u - 3])[1])

            def softmax_exp(i, t):
                n = MD_AT[i, t]
                u = i * NT + t
                before_scores_out(i, t)
                act.wait_ge(*L.at("masked", n + 1))
                if n >= 4:
                    act.wait_ge(*L.at("inverted", n - 3))
                act.activation(pr[:, u % 3, 0:width(t)], xs[:, u % 3, 0:width(t)], ACT.Exp,
                               bias=stat_min[:, n % 4:n % 4 + 1], scale=-1.0,
                               accum_out=stat_sum[:, n % 4:n % 4 + 1]).then_inc(sem("exped"), 1)

            def stick_logs(i, t):
                n = SB_AT[i, t]
                w = width(t)
                ps, ready = L.psum("S", i, t)
                act.wait_ge(*ready)
                if n >= 2:
                    act.wait_ge(*L.at("sb_log", n - 1))
                b = z1[:, n % 2, 0:w]
                act.activation(b, ps[:, 0:w], ACT.Abs).then_inc(sem("sb_abs"), 1)
                act.wait_ge(*L.at("sb_abs", n + 1))
                act.activation(b, b, ACT.Exp, scale=-1.0).then_inc(sem("sb_exp"), 1)
                act.wait_ge(*L.at("sb_exp", n + 1))
                act.activation(b, b, ACT.Ln, bias=1.0).then_inc(sem("sb_ln"), 1)

            def stick_exp(i, t):
                n = SB_AT[i, t]
                u = i * NT + t
                before_scores_out(i, t)
                act.wait_ge(*L.at("sb_masked", n + 1))
                act.activation(pr[:, u % 3, 0:width(t)], xs[:, u % 3, 0:width(t)], ACT.Exp)\
                    .then_inc(sem("sb_w"), 1)

            def probs_out(i, t):
                ps, ready = L.psum("T", i, t)
                act.wait_ge(*ready)
                if t == 0 and i >= 2:
                    act.wait_ge(*L.psum("O", i - 2)[1])
                act.activation(pt[:, i % 2, 0:t + 1, t * P:t * P + P],
                               ps[:, 0:width(t)].rearrange("p (k q) -> p k q", q=P), ACT.Copy)\
                    .then_inc(sem("pt_act"), 1)

            def head_out(i):
                ps, ready = L.psum("O", i)
                act.wait_ge(*ready)
                act.activation(act_hi[half(i), i // 2, :], ps[half(i), :], ACT.Copy).then_inc(sem("o_hi"), 1)

            for kind, u in attention_order(len(UNITS), lambda u: UNITS[u][1] == NT - 1):
                i, t = UNITS[u]
                stick = HEADS[i][0] == "s"
                if kind == "S":
                    if stick:
                        stick_logs(i, t)
                    if u >= 1:
                        pi, ptt = UNITS[u - 1]
                        if HEADS[pi][0] == "s":
                            stick_exp(pi, ptt)
                    if not stick:
                        softmax_exp(i, t)
                    if u == len(UNITS) - 1 and stick:
                        stick_exp(i, t)
                elif kind == "T":
                    if not stick:
                        probs_out(i, t)
                else:
                    head_out(i)

            squares(L, 3, lambda k: h[:, k, :], lambda k: L.at("h_wo", k + 1))
            norm_rest(L, 3, act_hi)
            act.dma_start(p_raw[:], p_t[layer]).then_inc(sem("p_in"), 16)
            act.wait_ge(sem("p_in"), 16 * (layer + 1))
            act.activation(pp_hi[:], p_raw[:], ACT.Copy).then_inc(sem("p_hi"), 1)
            if layer == layers - 1:
                ada_load(0)
                ada_load(1)
            for f in range(FG):
                for j in range(FJ):
                    n = f * FJ + j
                    ps, ready = L.psum("fg", f, j)
                    act.wait_ge(*ready)
                    if n >= 2:
                        act.wait_ge(*L.at("ff_out", n - 1))
                    act.activation(gate[:, n % 2, :], ps[:], ACT.Silu).then_inc(sem("silu_out"), 1)
                    act.wait_ge(*L.at("ff_out", n + 1))
                    act.activation(ff_hi[:, j, :], ffx[:, n % 2, :], ACT.Copy).then_inc(sem("ff_hi"), 1)
                    if layer == layers - 1 and n < ADA // 2:
                        ada_load(2 * n + 2)
                        ada_load(2 * n + 3)
            use_exp_ln()
            squares(L, 4, lambda k: h[:, k, :], lambda k: L.at("h_ffn", KD + k + 1))
            norm_rest(L, 4, act_hi)
            for j in range(KD):
                ps, ready = L.psum("pg", j)
                act.wait_ge(*ready)
                if j >= 2:
                    act.wait_ge(*L.at("ple_out", j - 1))
                else:
                    act.wait_ge(*L.at("ff_out", FG * FJ))
                act.activation(gate[:, j % 2, :], ps[:], ACT.Sigmoid).then_inc(sem("sig_out"), 1)

        L = Tail(layers)
        use_exp_ln()

        def t_squares(i, src, ready):
            for k in range(KD):
                act.wait_ge(*ready(k))
                if k >= 2:
                    act.wait_ge(sem("t_sum"), i * KD + k - 1)
                act.activation(sq[:, k % 2, :], src(k), ACT.Square).then_inc(sem("t_sq"), 1)

        def t_rstd(i):
            ps, ready = L.psum("norm", i)
            act.wait_ge(*ready)
            act.activation(rstd[:], ps[:], ACT.Ln, bias=eps_col[:], scale=1.0 / D).then_inc(sem("t_ln"), 1)
            act.wait_ge(sem("t_ln"), i + 1)
            act.activation(rstd[:], rstd[:], ACT.Exp, scale=-0.5).then_inc(sem("t_rstd"), 1)

        t_squares(0, lambda k: h[:, k, :], lambda k: Layer(layers - 1).at("h_ple", k + 1))
        t_rstd(0)
        act.wait_ge(sem("mod_out"), 1)
        act.dma_start(pe_sb[:], pe_t).then_inc(sem("pe_in"), 16)
        act.dma_start(w1[:], w_cmp1).then_inc(sem("cmp_w_in"), 16)
        act.dma_start(w2[:], w_cmp2).then_inc(sem("cmp_w_in"), 16)
        act.dma_start(sink_row[:], sinks).then_inc(sem("sinks_in"), 16)
        act.dma_start(seen[:], c_seen).then_inc(sem("masks_in"), 16)
        act.dma_start(cmp_mask[:], c_cmp).then_inc(sem("masks_in"), 16)
        t_squares(1, lambda k: h[:, k, :], lambda k: (sem("fin_x"), k + 1))
        act.wait_ge(sem("fin_x"), KD)
        t_rstd(1)
        for k in range(KD):
            act.wait_ge(sem("t_x"), k + 1)
            act.activation(act_hi[:, k, :], xn[:, k % 2, :], ACT.Identity, bias=mod[:, k:k + 1])\
                .then_inc(sem("t_hi"), 1)
        ps, ready = L.psum("gw", 0)
        act.wait_ge(*ready)
        act.activation(gates[:].rearrange("p t h -> p (t h)"), ps[:, 0:NT * 3 * NSA_H], ACT.Sigmoid)\
            .then_inc(sem("gates_out"), 1)
        for j in range(4):
            take(L, ("qa", j), "q_out", [(qa[:, j, :], full)], -HD ** -0.5)
        for n in range(2):
            ps, ready = L.psum("hid", n)
            act.wait_ge(*ready)
            act.activation(hid[:, n, :], ps[0:2 * NCP, 0:CH], ACT.Silu).then_inc(sem("hid_out"), 1)
        act.dma_start(alibi[:], c_alibi).then_inc(sem("masks_in"), 16)
        act.dma_start(window[:], c_window).then_inc(sem("masks_in"), 16)
        use_exp_ln()
        take(L, ("ks", 0), "k_out", [(ks[:], full)])
        take(L, ("kw", 0), "k_out", [(kw[:], full)])
        for n in range(2):
            ps, ready = L.psum("hT", n)
            act.wait_ge(*ready)
            act.activation(hid_t[:, n, :, :].rearrange("p a b -> p (a b)"), ps[:, 0:4 * NCP], ACT.Copy)\
                .then_inc(sem("hidT_out"), 1)
        for t in range(NT):
            ps, ready = L.psum("vt", t)
            act.wait_ge(*ready)
            act.activation(vt[:, t, :], ps[:, 0:3 * P], ACT.Copy).then_inc(sem("v_out"), 1)
        ps, ready = L.psum("kcT", 0)
        act.wait_ge(*ready)
        act.wait_ge(sem("kct_set"), 1)
        for e in range(2):
            act.activation(kct[half(e), e * NCP:(e + 1) * NCP], ps[0:HD, e * NCP:(e + 1) * NCP], ACT.Copy).then_inc(sem("kc_out"), 1)
        ps, ready = L.psum("vcT", 0)
        act.wait_ge(*ready)
        act.wait_ge(sem("vbd_set"), 1)
        for r in range(4):
            e = r % 2
            act.activation(vbd[r * NCP:(r + 1) * NCP, e * HD:(e + 1) * HD], ps[e * NCP:(e + 1) * NCP, 0:HD], ACT.Copy)\
                .then_inc(sem("vc_out"), 1)
        for j in range(4):
            take(L, ("qb", j), "q_out", [(qb[:, j, :], full)], -HD ** -0.5)
        take(L, ("kb", 0), "k_out", [(kb[:], full)])
        for t in range(NT):
            act.wait_ge(sem("c_centred"), t + 1)
            act.activation(xs2[:, t % 3, 0:NSA_H * NCP], xs2[:, t % 3, 0:NSA_H * NCP], ACT.Exp)\
                .then_inc(sem("c_exped"), 1)
        for t in range(NT):
            ps, ready = L.psum("cT", t)
            act.wait_ge(*ready)
            act.activation(cpt[:, :, t * P:t * P + P], ps[:, 0:2 * P].rearrange("p (c q) -> p c q", q=P), ACT.Copy)\
                .then_inc(sem("c_pt"), 1)
        for kind, u in attention_order(len(TUNITS), lambda u: TUNITS[u][1] == NT - 1):
            i, t = TUNITS[u]
            b, j, e = SUBS[i]
            first, n = keys_of(i, t)
            if kind == "S":
                if u >= 3:
                    act.wait_ge(*L.psum("T", *TUNITS[u - 3])[1])
                act.wait_ge(sem("t_masked"), u + 1)
                if u >= 4:
                    act.wait_ge(sem("t_inverted"), u - 3)
                w = n * P + (b == "swa")
                act.activation(pr2[:, u % 3, 0:w], xs2[:, u % 3, 0:w], ACT.Exp, bias=stat_min[:, u % 4:u % 4 + 1],
                               scale=-1.0, accum_out=stat_sum[:, u % 4:u % 4 + 1]).then_inc(sem("t_exped"), 1)
            elif kind == "T":
                ps, ready = L.psum("T", i, t)
                act.wait_ge(*ready)
                if t == 0 and i >= 2:
                    act.wait_ge(*L.psum("O", i - 2)[1])
                act.activation(pt2[:, i % 2, first:first + n, t * P:t * P + P],
                               ps[:, 0:n * P].rearrange("p (k q) -> p k q", q=P), ACT.Copy).then_inc(sem("t_pt"), 1)
            elif e == 1 and b != "sel":
                ps, ready = L.psum("O", i)
                act.wait_ge(*ready)
                act.activation((qb if b == "swa" else qa)[:, j, :], ps[:], ACT.Copy).then_inc(sem("heads_out"), 1)
        for j in range(8):
            ps, ready = L.psum("z", j)
            act.wait_ge(*ready)
            if j >= 2:
                act.wait_ge(sem("u_out"), j - 1)
            act.activation(silu_z[:, j % 2, :], ps[:], ACT.Silu).then_inc(sem("z_out"), 1)
            act.wait_ge(sem("u_out"), j + 1)
            act.activation(u_hi[:, j, :], ux[:, j % 2, :], ACT.Copy).then_inc(sem("u_hi"), 1)
        for j in range(KD):
            for c, name in enumerate(("ma", "mb")):
                ps, ready = L.psum(name, j)
                act.wait_ge(*ready)
                if j:
                    act.wait_ge(sem("y_part"), 2 * j + c - 1)
                act.activation(yx[:, c, :], ps[:], ACT.Sigmoid).then_inc(sem("merge_out"), 1)
            act.wait_ge(sem("y_out"), j + 1)
            act.activation(y_hi[:, j, :], yx[:, 2 + j % 2, :], ACT.Copy).then_inc(sem("y_hi"), 1)
        use_exp_ln()
        for j in range(KD):
            take(L, ("wout", j), "y2_out", [(y2[:, j, :], full)])
            if j >= 2:
                act.wait_ge(sem("t_sum"), 2 * KD + j - 1)
            act.wait_ge(sem("y2_out"), j + 1)
            act.activation(sq[:, j % 2, :], y2[:, j, :], ACT.Square).then_inc(sem("t_sq"), 1)
        t_rstd(2)

    @block.vector
    def _(dve):
        def sums(L, i):
            first, n, _ = NORMS[i]
            for k in range(n):
                b = sq[:, (first + k) % 2, :]
                dve.wait_ge(*L.at("norm_sq", first + k + 1))
                if k:
                    dve.wait_ge(*L.at("norm_sum", first + k))
                    dve.tensor_tensor(ssum[:], ssum[:], b, ALU.add).then_inc(sem("norm_sum"), 1)
                else:
                    if i or L.n:
                        Lp, ip = (L, i - 1) if i else (Layer(L.n - 1), 4)
                        dve.wait_ge(*Lp.psum("norm", ip)[1])
                    dve.tensor_copy(ssum[:], b).then_inc(sem("norm_sum"), 1)

        def normed(L, i, src, lo, hi, first_tile=0):
            first, n, _ = NORMS[i]
            g0 = L.n * GAIN_PER_LAYER + first
            dve.wait_ge(*L.at("norm_rstd", i + 1))

            def low(k):
                dve.wait_ge(*L.at("norm_hi", first + k + 1))
                dve.tensor_tensor(lo[:, first_tile + k, :], xn[:, (first + k) % 2, :],
                                  hi[:, first_tile + k, :].bitcast(F32), ALU.subtract).then_inc(sem("norm_lo"), 1)

            for k in range(n):
                if first + k >= 2 or L.n:
                    dve.wait_ge(*L.at("norm_lo", first + k - 1))
                dve.scalar_tensor_tensor(xn[:, (first + k) % 2, :], src(k), g_sb[:, g0 + k:g0 + k + 1], rstd[:],
                                         ALU.mult, ALU.mult).then_inc(sem("norm_x"), 1)
                if k:
                    low(k - 1)
            low(n - 1)

        def ada_sum(n):
            k, c = divmod(n, 3)
            dve.wait_ge(sem(f"ada_in{n % 2}"), 16 * (n // 2 + 1))
            acc, col = mod_acc[:, c * D:(c + 1) * D], g_sb[:, G_C + k:G_C + k + 1]
            if k == 0:
                dve.tensor_scalar(acc, ada[:, n % 2, :], col, None, ALU.mult).then_inc(sem("ada_summed"), 1)
            else:
                dve.wait_ge(sem("ada_summed"), n - 2)
                dve.scalar_tensor_tensor(acc, ada[:, n % 2, :], col, acc, ALU.mult, ALU.add)\
                    .then_inc(sem("ada_summed"), 1)

        dve.wait_ge(sem("x_in"), 16)
        dve.wait_ge(sem("consts_in"), 16 * 6)
        for c in range(2):
            dve.wait_ge(sem("rows_ready"), c + 1)
            dve.tensor_scalar(rows_sb[:, c * 320:(c + 1) * 320], banks[c][0:DSA_H, 0:320], -1.0, None, ALU.mult)\
                .then_inc(sem("rows_out"), 1)
        dve.tensor_scalar(strict_neg[:], strict[:, S - P:S], BIG, -BIG, ALU.mult, ALU.add)\
            .then_inc(sem("strict_set"), 1)
        dve.wait_ge(sem("strict_set"), 1)
        for layer in range(layers):
            L = Layer(layer)
            sums(L, 0)
            normed(L, 0, lambda k: h[:, k, :], act_lo, act_hi)
            ps, ready = L.psum("x", 0)
            dve.wait_ge(*ready)
            dve.tensor_tensor(kr[64:96, 0, :], ps[64:96, :], rope_k[64:96, :], ALU.mult).then_inc(sem("kr_step"), 1)
            dve.tensor_tensor(kr[64:96, 1, :], ps[96:128, :], rope_k[96:128, :], ALU.mult).then_inc(sem("kr_step"), 1)
            dve.wait_ge(*L.at("kr_step", 2))
            dve.tensor_tensor(kr[64:96, 0, :], kr[64:96, 0, :], kr[64:96, 1, :], ALU.add).then_inc(sem("kr_step"), 1)
            sums(L, 1)
            normed(L, 1, lambda k: c_raw[:, k, :], c_lo, c_hi, 0)
            sums(L, 2)
            normed(L, 2, lambda k: c_raw[:, 3 + k, :], c_lo, c_hi, 3)
            dve.wait_ge(*L.at("norm_lo", KD + 5))
            dve.wait_ge(*L.at("iw_out", 1))
            u = 0
            for t in range(1, NT):
                w = width(t)
                for n in range(IDX_H):
                    dve.wait_ge(*L.at("ix_relu", u + 1))
                    col = iw_w[:, t, n:n + 1]
                    if n == 0:
                        dve.tensor_scalar(isc[:, t - 1, 0:w], relu[:, u % 2, 0:w], col, None, ALU.mult)\
                            .then_inc(sem("ix_acc"), 1)
                    else:
                        dve.wait_ge(*L.at("ix_acc", u))
                        dve.scalar_tensor_tensor(isc[:, t - 1, 0:w], relu[:, u % 2, 0:w], col, isc[:, t - 1, 0:w],
                                                 ALU.mult, ALU.add).then_inc(sem("ix_acc"), 1)
                    u += 1
                dve.wait_ge(*L.at("ix_acc", u))
                dve.tensor_tensor(isc[:, t - 1, w - P:w], isc[:, t - 1, w - P:w], causal[:, S - P:S], ALU.subtract)\
                    .then_inc(sem("ix_masked"), 1)
            for n in range(MLA_H):
                ps, ready = L.psum("uq", n)
                dve.wait_ge(*ready)
                dve.tensor_tensor(mq[:, n, :], ps[:], rope_q[:], ALU.mult).then_inc(sem("mq_out"), 1)
            n = 0
            dve.wait_ge(*L.at("ix_masked", NT - 1))
            for r in range(TOPK // 8):
                for t in range(1, NT):
                    if r:
                        dve.wait_ge(*L.at("topk_cut", n + t - 1 - (NT - 1) + 1))
                    dve.max(top8[:, t - 1, :], isc[:, t - 1, 0:width(t)]).then_inc(sem("topk_max"), 1)
                for t in range(1, NT):
                    dve.wait_ge(*L.at("topk_max", n + t))
                    dve.match_replace(isc[:, t - 1, 0:width(t)], top8[:, t - 1, :], isc[:, t - 1, 0:width(t)], -3e38)\
                        .then_inc(sem("topk_cut"), 1)
                n += NT - 1
            for t in range(1, NT):
                dve.wait_ge(*L.at("topk_cut", n - (NT - 1) + t))
                dve.tensor_scalar(isc[:, t - 1, 0:width(t)], isc[:, t - 1, 0:width(t)], -2e38, BIG,
                                  ALU.is_gt, ALU.mult).then_inc(sem("sel_out"), 1)

            def softmax_mask(i, t):
                kind, m = HEADS[i]
                n, u, w = MD_AT[i, t], i * NT + t, width(t)
                ps, ready = L.psum("S", i, t)
                dve.wait_ge(*ready)
                if u >= 3:
                    free_x(*UNITS[u - 3])
                if n >= 4:
                    dve.wait_ge(*L.at("exped", n - 3))
                x = xs[:, u % 3, 0:w]
                least = stat_min[:, n % 4:n % 4 + 1]
                src = ps[:, 0:w]
                mask = causal[:, S - w:S]
                if kind == "d":
                    dve.tensor_tensor(x, src, bias[:, m, 0:w][:, ::-1], ALU.add).then_inc(sem("biased"), 1)
                    dve.wait_ge(*L.at("biased", m * NT + t + 1))
                    src = x
                    if t:
                        mask = isc[:, t - 1, 0:w]
                dve.tensor_tensor_reduce(out=x, in0=src, in1=mask, scale=1.0, scalar=3e38, op0=ALU.add, op1=ALU.min,
                                         accum_out=least).then_inc(sem("masked"), 1)

            def free_x(i, t):
                if HEADS[i][0] == "s":
                    dve.wait_ge(*L.at("sb_w", SB_AT[i, t] + 1))
                else:
                    dve.wait_ge(*L.at("exped", MD_AT[i, t] + 1))

            def softmax_scale(i, t):
                n, u, w = MD_AT[i, t], i * NT + t, width(t)
                dve.wait_ge(*L.at("exped", n + 1))
                if n >= 4:
                    dve.wait_ge(*L.at("scaled", n - 3))
                inv = stat_inv[:, n % 4:n % 4 + 1]
                dve.reciprocal(inv, stat_sum[:, n % 4:n % 4 + 1]).then_inc(sem("inverted"), 1)
                dve.wait_ge(*L.at("inverted", n + 1))
                dve.tensor_scalar(pr[:, u % 3, 0:w], pr[:, u % 3, 0:w], inv, None, ALU.mult)\
                    .then_inc(sem("scaled"), 1)

            def stick_sums(i, t):
                n, u, w = SB_AT[i, t], i * NT + t, width(t)
                ps, _ = L.psum("S", i, t)
                if u >= 3:
                    free_x(*UNITS[u - 3])
                x, b = xs[:, u % 3, 0:w], z1[:, n % 2, 0:w]
                dve.wait_ge(*L.at("sb_ln", n + 1))
                dve.scalar_tensor_tensor(x, ps[:, 0:w], 0.0, b, ALU.max, ALU.add).then_inc(sem("sb_neg"), 1)
                dve.wait_ge(*L.at("sb_neg", n + 1))
                dve.tensor_tensor_scan(b[:, ::-1], x[:, ::-1], strict[:, S - w:S][:, ::-1], 0.0, ALU.add, ALU.mult)\
                    .then_inc(sem("sb_scan"), 1)
                dve.wait_ge(*L.at("sb_scan", n + 1))
                dve.tensor_tensor(x, ps[:, 0:w], b, ALU.subtract).then_inc(sem("sb_log"), 1)
                dve.wait_ge(*L.at("sb_log", n + 1))
                dve.tensor_tensor(xs[:, u % 3, w - P:w], xs[:, u % 3, w - P:w], strict_neg[:], ALU.add)\
                    .then_inc(sem("sb_masked"), 1)

            def probs_out(i, t):
                ps, ready = L.psum("T", i, t)
                dve.wait_ge(*ready)
                if t == 0 and i >= 2:
                    dve.wait_ge(*L.psum("O", i - 2)[1])
                dve.tensor_copy(pt[:, i % 2, 0:t + 1, t * P:t * P + P],
                                ps[:, 0:width(t)].rearrange("p (k q) -> p k q", q=P)).then_inc(sem("pt_dve"), 1)

            if layer == 0:
                dve.wait_ge(sem("bias_in"), 16 * DSA_H)
            for kind, u in attention_order(len(UNITS), lambda u: UNITS[u][1] == NT - 1):
                i, t = UNITS[u]
                stick = HEADS[i][0] == "s"
                if kind == "S":
                    if u and HEADS[UNITS[u - 1][0]][0] != "s" and stick:
                        softmax_scale(*UNITS[u - 1])
                    (stick_sums if stick else softmax_mask)(i, t)
                    if u and HEADS[UNITS[u - 1][0]][0] != "s" and not stick:
                        softmax_scale(*UNITS[u - 1])
                    if u == len(UNITS) - 1 and not stick:
                        softmax_scale(i, t)
                elif kind == "T":
                    if stick:
                        probs_out(i, t)
                else:
                    dve.wait_ge(*L.at("o_hi", i + 1))
                    dve.tensor_tensor(act_lo[half(i), i // 2, :], L.psum("O", i)[0][half(i), :],
                                      act_hi[half(i), i // 2, :].bitcast(F32), ALU.subtract).then_inc(sem("o_lo"), 1)

            def add_to_h(key, name, j):
                ps, ready = L.psum(*key)
                dve.wait_ge(*ready)
                dve.tensor_tensor(h[:, j, :], h[:, j, :], ps[:], ALU.add).then_inc(sem(name), 1)

            def sum_of(i, k):
                first, n, _ = NORMS[i]
                b = sq[:, (first + k) % 2, :]
                dve.wait_ge(*L.at("norm_sq", first + k + 1))
                if k:
                    dve.wait_ge(*L.at("norm_sum", first + k))
                    dve.tensor_tensor(ssum[:], ssum[:], b, ALU.add).then_inc(sem("norm_sum"), 1)
                else:
                    dve.tensor_copy(ssum[:], b).then_inc(sem("norm_sum"), 1)

            for j in range(KD):
                add_to_h(("wo", j), "h_wo", j)
                if j:
                    sum_of(3, j - 1)
            sum_of(3, KD - 1)
            normed(L, 3, lambda k: h[:, k, :], act_lo, act_hi)
            dve.wait_ge(*L.at("p_hi", 1))
            dve.tensor_tensor(pp_lo[:], p_raw[:], pp_hi[:].bitcast(F32), ALU.subtract).then_inc(sem("p_lo"), 1)
            for f in range(FG):
                for j in range(FJ):
                    n = f * FJ + j
                    ps, ready = L.psum("fu", f, j)
                    dve.wait_ge(*ready)
                    dve.wait_ge(*L.at("silu_out", n + 1))
                    if n >= 2:
                        dve.wait_ge(*L.at("ff_lo", n - 1))
                    dve.tensor_tensor(ffx[:, n % 2, :], gate[:, n % 2, :], ps[:], ALU.mult).then_inc(sem("ff_out"), 1)
                    dve.wait_ge(*L.at("ff_hi", n + 1))
                    dve.tensor_tensor(ff_lo[:, j, :], ffx[:, n % 2, :], ff_hi[:, j, :].bitcast(F32), ALU.subtract)\
                        .then_inc(sem("ff_lo"), 1)
                    if layer == layers - 1 and n < ADA // 2:
                        ada_sum(2 * n)
                        ada_sum(2 * n + 1)
                for j in range(KD):
                    if f:
                        dve.wait_ge(*L.at("h_ffn", j + 1))
                    add_to_h(("fd", f, j), "h_ffn", j)
                    if f and j:
                        sum_of(4, j - 1)
            sum_of(4, KD - 1)
            normed(L, 4, lambda k: h[:, k, :], act_lo, act_hi)
            for j in range(KD):
                dve.wait_ge(*L.at("sig_out", j + 1))
                if j >= 2:
                    dve.wait_ge(*L.at("h_ple", j - 1))
                dve.tensor_tensor(ffx[:, j % 2, :], gate[:, j % 2, :], L.psum("pp", j)[0][:], ALU.mult)\
                    .then_inc(sem("ple_out"), 1)
                dve.wait_ge(*L.at("ple_out", j + 1))
                dve.tensor_tensor(h[:, j, :], h[:, j, :], ffx[:, j % 2, :], ALU.add).then_inc(sem("h_ple"), 1)

        L = Tail(layers)

        def t_sums(i):
            for k in range(KD):
                dve.wait_ge(sem("t_sq"), i * KD + k + 1)
                if k:
                    dve.wait_ge(sem("t_sum"), i * KD + k)
                    dve.tensor_tensor(ssum[:], ssum[:], sq[:, k % 2, :], ALU.add).then_inc(sem("t_sum"), 1)
                else:
                    if i:
                        dve.wait_ge(*L.psum("norm", i - 1)[1])
                    dve.tensor_copy(ssum[:], sq[:, 0, :]).then_inc(sem("t_sum"), 1)

        ps, ready = L.psum("mod", 0)
        dve.wait_ge(*ready)
        dve.wait_ge(*Layer(layers - 1).at("h_ple", KD))
        dve.memset(ones_row[:], -1.0).then_inc(sem("ones_row_set"), 1)
        dve.memset(vbd[:], 0.0).then_inc(sem("vbd_set"), 1)
        dve.memset(kct[:], 0.0).then_inc(sem("kct_set"), 1)
        dve.memset(cmp_x[:], 0.0).then_inc(sem("cmp_x_set"), 1)
        dve.tensor_tensor(mod[:], ps[:, 0:3 * KD], g_sb[:, G_BADA:G_BADA + 3 * KD], ALU.add).then_inc(sem("mod_out"), 1)
        dve.wait_ge(sem("mod_out"), 1)
        dve.scalar_tensor_tensor(gain_pre[:], mod[:, KD:2 * KD], 1.0, g_sb[:, G_PRE:G_PRE + KD], ALU.add, ALU.mult)\
            .then_inc(sem("gains_set"), 1)
        dve.tensor_tensor(gain_post[:], mod[:, 2 * KD:3 * KD], g_sb[:, G_POST:G_POST + KD], ALU.mult)\
            .then_inc(sem("gains_set"), 1)
        t_sums(0)
        dve.wait_ge(sem("t_rstd"), 1)
        for k in range(KD):
            dve.scalar_tensor_tensor(h[:, k, :], h[:, k, :], g_sb[:, G_FINAL + k:G_FINAL + k + 1], rstd[:],
                                     ALU.mult, ALU.mult).then_inc(sem("fin_x"), 1)
        t_sums(1)
        dve.wait_ge(sem("t_rstd"), 2)
        dve.wait_ge(sem("gains_set"), 2)

        def t_low(k):
            dve.wait_ge(sem("t_hi"), k + 1)
            dve.scalar_tensor_tensor(act_lo[:, k, :], xn[:, k % 2, :], mod[:, k:k + 1], act_hi[:, k, :].bitcast(F32),
                                     ALU.add, ALU.subtract).then_inc(sem("t_lo"), 1)

        for k in range(KD):
            if k >= 2:
                dve.wait_ge(sem("t_lo"), k - 1)
            dve.scalar_tensor_tensor(xn[:, k % 2, :], h[:, k, :], gain_pre[:, k:k + 1], rstd[:], ALU.mult, ALU.mult)\
                .then_inc(sem("t_x"), 1)
            if k:
                t_low(k - 1)
        t_low(KD - 1)
        dve.wait_ge(sem("pe_in"), 16)
        dve.wait_ge(sem("cmp_x_set"), 1)
        for n, name in enumerate(("kc", "vc")):
            ps, ready = L.psum(name, 0)
            dve.wait_ge(*ready)
            for g in range(2):
                for e in range(2):
                    src = ps[half(g), :]
                    src = bass.AP(src.tensor, src.offset + e, [src.ap[0], [2, CB // 2], [CS, NC]])
                    pos = pe_sb[half(e), n, :].unsqueeze(2).broadcast_to([64, CB // 2, NC])
                    dve.tensor_tensor(cmp_x[half(e), n, :, g * NCP:g * NCP + NC], src, pos, ALU.add)\
                        .then_inc(sem("cmp_in"), 1)
        dve.wait_ge(sem("masks_in"), 16 * 4)
        dve.wait_ge(sem("gates_out"), 1)
        for t in range(NT):
            ps, ready = L.psum("cS", t)
            dve.wait_ge(*ready)
            if t >= 3:
                dve.wait_ge(*L.psum("cT", t - 3)[1])
            flat = xs2[:, t % 3, 0:NSA_H * NCP]
            x = flat.rearrange("p (h c) -> p h c", c=NCP)
            col = [cst[:, c, :] for c in range(4)]
            wide = lambda a: a.unsqueeze(2).broadcast_to([P, NSA_H, NCP])
            dve.tensor_tensor(flat, ps[:, 0:NSA_H * NCP], cmp_mask[:, t, :], ALU.add).then_inc(sem("c_masked"), 1)
            dve.wait_ge(sem("c_masked"), t + 1)
            dve.tensor_reduce(col[0], x, AX_X, ALU.min).then_inc(sem("c_min"), 1)
            dve.wait_ge(sem("c_min"), t + 1)
            dve.tensor_tensor(x, wide(col[0]), x, ALU.subtract).then_inc(sem("c_centred"), 1)
            dve.wait_ge(sem("c_exped"), t + 1)
            dve.tensor_reduce(col[1], x, AX_X, ALU.add).then_inc(sem("c_sum"), 1)
            dve.wait_ge(sem("c_sum"), t + 1)
            dve.reciprocal(col[2], col[1]).then_inc(sem("c_inv"), 1)
            dve.wait_ge(sem("c_inv"), t + 1)
            dve.scalar_tensor_tensor(col[3], col[2], seen[:, t:t + 1], gates[:, t, 0:NSA_H], ALU.mult, ALU.mult)\
                .then_inc(sem("c_coef"), 1)
            dve.wait_ge(sem("c_coef"), t + 1)
            dve.tensor_tensor(x, x, wide(col[3]), ALU.mult).then_inc(sem("c_scaled"), 1)

        def t_mask(i, t):
            b, j, e = SUBS[i]
            u = i * NT + t
            _, n = keys_of(i, t)
            ps, ready = L.psum("S", i, t)
            dve.wait_ge(*ready)
            if u >= 3:
                dve.wait_ge(sem("t_exped"), u - 2)
            else:
                dve.wait_ge(*L.psum("cT", NT - 1)[1])
            head = j + 4 * e
            if b == "swa":
                w = n * P + 1
                mask = window[:, head, 2 * P + 1 - w:2 * P + 1]
            else:
                w = n * P
                mask = alibi[:, head, S - w:S]
            dve.tensor_tensor_reduce(out=xs2[:, u % 3, 0:w], in0=ps[:, 0:w], in1=mask, scale=1.0, scalar=3e38,
                                     op0=ALU.add, op1=ALU.min, accum_out=stat_min[:, u % 4:u % 4 + 1])\
                .then_inc(sem("t_masked"), 1)

        def t_scale(i, t):
            b, j, e = SUBS[i]
            u = i * NT + t
            w = keys_of(i, t)[1] * P
            dve.wait_ge(sem("t_exped"), u + 1)
            if u >= 4:
                dve.wait_ge(sem("t_scaled"), u - 3)
            inv = stat_inv[:, u % 4:u % 4 + 1]
            dve.reciprocal(inv, stat_sum[:, u % 4:u % 4 + 1]).then_inc(sem("t_inverted"), 1)
            dve.wait_ge(sem("t_inverted"), u + 1)
            x = pr2[:, u % 3, 0:w]
            if b == "swa":
                dve.tensor_scalar(x, x, inv, None, ALU.mult).then_inc(sem("t_scaled"), 1)
            else:
                g = (1 if b == "sel" else 2) * NSA_H + 2 * j + e
                dve.tensor_scalar(x, x, inv, gates[:, t, g:g + 1], ALU.mult, ALU.mult).then_inc(sem("t_scaled"), 1)

        for u, (i, t) in enumerate(TUNITS):
            t_mask(i, t)
            if u:
                t_scale(*TUNITS[u - 1])
        t_scale(*TUNITS[-1])
        for j in range(8):
            dve.wait_ge(sem("z_out"), j + 1)
            if j >= 2:
                dve.wait_ge(sem("u_lo"), j - 1)
            dve.wait_ge(sem("heads_out"), 8)
            dve.tensor_tensor(ux[:, j % 2, :], silu_z[:, j % 2, :], (qa if j < 4 else qb)[:, j % 4, :],
                              ALU.mult).then_inc(sem("u_out"), 1)
            dve.wait_ge(sem("u_hi"), j + 1)
            dve.tensor_tensor(u_lo[:, j, :], ux[:, j % 2, :], u_hi[:, j, :].bitcast(F32), ALU.subtract)\
                .then_inc(sem("u_lo"), 1)
        for j in range(KD):
            for c, name in enumerate(("ya", "yb")):
                ps, ready = L.psum(name, j)
                dve.wait_ge(*ready)
                dve.wait_ge(sem("merge_out"), 2 * j + c + 1)
                dve.tensor_tensor(yx[:, c, :], yx[:, c, :], ps[:], ALU.mult).then_inc(sem("y_part"), 1)
            dve.wait_ge(sem("y_part"), 2 * j + 2)
            if j >= 2:
                dve.wait_ge(sem("y_lo"), j - 1)
            dve.tensor_tensor(yx[:, 2 + j % 2, :], yx[:, 0, :], yx[:, 1, :], ALU.add).then_inc(sem("y_out"), 1)
            dve.wait_ge(sem("y_hi"), j + 1)
            dve.tensor_tensor(y_lo[:, j, :], yx[:, 2 + j % 2, :], y_hi[:, j, :].bitcast(F32), ALU.subtract)\
                .then_inc(sem("y_lo"), 1)
        t_sums(2)
        dve.wait_ge(sem("t_rstd"), 3)
        for k in range(KD):
            if k >= 2:
                dve.wait_ge(sem("x_final"), k - 1)
            dve.scalar_tensor_tensor(xn[:, k % 2, :], y2[:, k, :], gain_post[:, k:k + 1], rstd[:], ALU.mult, ALU.mult)\
                .then_inc(sem("post_x"), 1)
            dve.wait_ge(sem("post_x"), k + 1)
            dve.tensor_tensor(h[:, k, :], h[:, k, :], xn[:, k % 2, :], ALU.add).then_inc(sem("x_final"), 1)


def bucket_table():
    import math
    dist = np.maximum(np.arange(S + P) - (P - 1), 0)
    half_b = REL_BUCKETS // 2
    d = np.maximum(dist, 1).astype(np.float32)
    large = half_b + (np.log(d / np.float32(half_b)) / np.float32(math.log(REL_MAX / half_b))
                      * np.float32(REL_BUCKETS - half_b)).astype(np.int32)
    bucket = np.where(dist < half_b, dist, np.minimum(large, REL_BUCKETS - 1))
    return (np.arange(REL_BUCKETS)[:, None] == bucket[None, :]).astype(np.float32)


def rope_tables():
    half_r = ROPE // 2
    inv = np.float32(10000.0) ** (-np.arange(half_r, dtype=np.float32) / np.float32(half_r))
    ang = np.arange(S, dtype=np.float32)[None, :] * inv[:, None]
    cos, sin = np.cos(ang).astype(np.float32), np.sin(ang).astype(np.float32)
    t = np.concatenate([np.ones((NOPE, S), np.float32), cos, cos, -sin, sin])
    return (t * np.float32(-(NOPE + ROPE) ** -0.5)).astype(np.float32), t


def shifted(fn):
    dist = np.arange(P)[:, None] + (S - P) - np.arange(S)[None, :]
    return fn(dist).astype(np.float32)


def blocks(w):
    return [w[k * P:(k + 1) * P] for k in range(w.shape[0] // P)]


def pad_cols(w, n=P):
    return np.concatenate([w, np.zeros((w.shape[0], n - w.shape[1]), w.dtype)], 1) if w.shape[1] < n else w


def padded(out):
    while len(out) % BLK:
        out.append(np.zeros((P, P), np.float32))


def layer_stream(w_in, w_uq, w_ukv, w_o, w_gate, w_up, w_down, w_pg, w_pp):
    cuts = np.cumsum([0, Q_LORA, KV_LORA, ROPE, DSA_H * HD, HD, HD, IDX_H * HD, HD, IDX_H,
                      SB_H * HD, SB_H * HD, SB_H * HD])
    cq, ckv, kr, dq, dk, dv, iq, ik, iw, sq, sk, sv = [w_in[:, a:b] for a, b in zip(cuts[:-1], cuts[1:])]
    swap = np.r_[ROPE // 2:ROPE, 0:ROPE // 2]
    out = [pad_cols(np.concatenate(blocks(iw), 1))]

    def tile(w):
        out.extend(blocks(w))

    def tiles(w):
        for j in range(w.shape[1] // P):
            tile(w[:, j * P:(j + 1) * P])

    def rows(w, per_chunk=2):
        padded(out)
        for k, b in enumerate(blocks(w)):
            out.extend(b[:, j * P:(j + 1) * P] for j in range(w.shape[1] // P))
            if k % per_chunk == per_chunk - 1:
                padded(out)
        padded(out)

    tiles(iq)
    tile(np.concatenate([dq[:, 4 * HD:], ik], 1))
    tiles(cq)
    tiles(ckv)
    tile(np.concatenate([dk, kr, kr[:, swap]], 1))
    uq = w_uq.reshape(Q_LORA, MLA_H, NOPE + ROPE)
    for n in range(MLA_H):
        r = uq[:, n, NOPE:]
        tile(np.concatenate([uq[:, n, :NOPE], r, r[:, swap]], 1))
    ukv = w_ukv.reshape(KV_LORA, MLA_H, NOPE + VDIM)
    tiles(ukv[:, :, :NOPE].reshape(KV_LORA, -1))
    rows(ukv[:, :, NOPE:].reshape(KV_LORA, -1))
    tiles(dq[:, :4 * HD])
    tiles(sq[:, :4 * HD])
    tiles(sk[:, :4 * HD])
    tile(np.concatenate([sq[:, 4 * HD:], sk[:, 4 * HD:]], 1))
    rows(np.concatenate([dv, sv], 1))
    first = {"m": 0, "d": MLA_H, "s": MLA_H + DSA_H}
    tiles(np.concatenate([w_o[(first[k] + n) * HD:(first[k] + n + 1) * HD] for k, n in HEADS]))
    for f in range(FG):
        for j in range(f * FJ, (f + 1) * FJ):
            tile(w_gate[:, j * P:(j + 1) * P])
            tile(w_up[:, j * P:(j + 1) * P])
        tiles(w_down[f * FJ * P:(f + 1) * FJ * P])
    for j in range(KD):
        tile(w_pp[:, j * P:(j + 1) * P])
        tile(w_pg[:, j * P:(j + 1) * P])
    padded(out)
    assert len(out) == layer_blocks(), (len(out), layer_blocks())
    return out


def tail_stream(w_in, w_o_nsa, w_o_swa, w_out):
    pair = np.array([j + 4 * e for j in range(4) for e in range(2)])
    by_pair = (pair[:, None] * HD + np.arange(HD)).reshape(-1)
    cuts = np.cumsum([0, NSA_H * HD, P, P, P, P, P, P, 3 * NSA_H, NSA_H * HD, NSA_H * HD, P, P, NSA_H * HD, D, D])
    qa, kc, vc, ks, vs, kw, vw, gw, za, qb, kb, vb, zb, ma, mb = [w_in[:, a:b] for a, b in zip(cuts[:-1], cuts[1:])]
    gw = gw.reshape(D, 3, NSA_H)[:, :, pair].reshape(D, 3 * NSA_H)
    gw = pad_cols(np.concatenate(blocks(gw), 1), 2 * P)
    out = [gw[:, :P], gw[:, P:]]

    def tiles(w):
        for j in range(w.shape[1] // P):
            out.extend(blocks(w[:, j * P:(j + 1) * P]))

    for w in (kc, vc, qa[:, by_pair], ks, kw):
        tiles(w)
    padded(out)
    for k, b in enumerate(blocks(np.concatenate([vs, vw, vb], 1))):
        out.extend(b[:, j * P:(j + 1) * P] for j in range(3))
        if k % 2:
            padded(out)
    for w in (qb[:, by_pair], kb, za[:, by_pair], zb[:, by_pair]):
        tiles(w)
    for j in range(KD):
        cols = slice(j * P, (j + 1) * P)
        for w in (ma, w_o_nsa[by_pair], mb, w_o_swa[by_pair]):
            tiles(w[:, cols])
    tiles(w_out)
    while len(out) < tail_blocks():
        out.append(np.zeros((P, P), np.float32))
    assert len(out) == tail_blocks()
    return out


def tail_tables():
    d = np.arange(P)[:, None] + (S - P) - np.arange(S)[None, :]
    alibi = np.stack([np.where(d >= 0, s * d, BIG) for s in SLOPES], 1)
    d = np.arange(P)[:, None] + P - np.arange(2 * P)[None, :]
    window = np.zeros((P, NSA_H, 2 * P + 1))
    for n, s in enumerate(SLOPES):
        window[:, n, :2 * P] = np.where((d >= 0) & (d < P), s * d, BIG)
    cmp_mask = np.full((P, NT, NSA_H, NCP), BIG)
    for t in range(NT):
        d = (np.arange(P) + t * P)[:, None] - (np.arange(NC) * CS + CB - 1)[None, :]
        for j in range(4):
            for e in range(2):
                cmp_mask[:, t, 2 * j + e, :NC] = np.where(d >= 0, SLOPES[j + 4 * e] * d, BIG)
    seen = (np.arange(P)[:, None] + np.arange(NT)[None, :] * P >= CB - 1)
    return [a.astype(np.float32) for a in (alibi, window, cmp_mask.reshape(P, NT, -1), seen)]


def chunked(out):
    a = np.stack(out).reshape(-1, BLK, P, P)
    return np.ascontiguousarray(a.transpose(0, 2, 1, 3).reshape(-1, P, BLK * P))


def columns(v):
    return np.asarray(v).reshape(-1, P).T


def feature_major(x):
    return np.ascontiguousarray(x.T.reshape(-1, P, S).transpose(1, 0, 2))


def layout(a):
    f = {k: np.asarray(v) for k, v in a.items()}
    stream = []
    for i in range(DEPTH):
        stream += layer_stream(*(f[k][i] for k in ("w_in", "mla_w_uq", "mla_w_ukv", "w_o", "w_gate", "w_up", "w_down",
                                                   "w_ple_gate", "w_ple_proj")))
    stream += tail_stream(*(f[k][0] for k in ("w_in_2", "w_o_nsa_2", "w_o_swa_2", "w_out_2")))
    gains = [columns(f[k][i]) for i in range(DEPTH)
             for k in ("attn_norm", "mla_q_norm", "mla_kv_norm", "ffn_norm", "ple_norm")]
    gains += [columns(f[k]) for k in ("final_norm", "g_pre_2", "g_post_2", "b_ada_2", "c_2")]
    rope_q, rope_k = rope_tables()
    alibi, window, cmp_mask, seen = tail_tables()
    per_tile = lambda w: w.reshape(-1, P, w.shape[-1]).transpose(1, 0, 2)
    pe = lambda w: w.reshape(CB // 2, P).T
    out = dict(
        x_t=feature_major(f["x"][0]), p_t=np.stack([feature_major(f["p"][i, 0]) for i in range(DEPTH)]),
        wstream=chunked(stream), gains=np.concatenate(gains, 1), rel_bias=f["rel_bias"],
        c_rope_q=rope_q, c_rope_k=rope_k, c_onehot=bucket_table(), c_eye=np.eye(P, dtype=np.float32),
        c_causal=shifted(lambda d: np.where(d >= 0, 0.0, BIG)), c_strict=shifted(lambda d: d > 0),
        w_ada=per_tile(f["w_ada_2"][0]),
        w_cmp1=np.stack([per_tile(f["w_cmp_k1_2"][0]), per_tile(f["w_cmp_v1_2"][0])], 1),
        w_cmp2=np.stack([per_tile(f["w_cmp_k2_2"][0]), per_tile(f["w_cmp_v2_2"][0])], 1),
        pe_t=np.stack([pe(f["pe_cmp_k_2"][0]), pe(f["pe_cmp_v_2"][0])], 1),
        sinks=f["sinks_2"],
        c_alibi=alibi, c_window=window, c_cmp=cmp_mask, c_seen=seen)
    return {k: np.ascontiguousarray(v) for k, v in out.items()}


def kernel(**inputs):
    import concourse.bacc as bacc
    from concourse.bass_utils import run_bass_kernel_spmd

    arrays = layout(inputs)
    nc = bacc.Bacc("TRN2", target_bir_lowering=False, num_devices=1)
    args = {k: nc.dram_tensor(f"in_{k}", v.shape, F32, kind="ExternalInput").ap() for k, v in arrays.items()}
    out = nc.dram_tensor("out_t", (P, KD, S), F32, kind="ExternalOutput").ap()
    build(nc, out_t=out, **args)
    r = run_bass_kernel_spmd(nc, [{f"in_{k}": v for k, v in arrays.items()}], core_ids=[0])
    got = np.asarray(r.results[0]["out_t"])
    return np.ascontiguousarray(got.transpose(2, 1, 0)).reshape(1, S, D)
```

```python
import numpy as np

import concourse.bass as bass
from concourse import mybir

F32 = mybir.dt.float32
F32R = mybir.dt.float32r
ALU = mybir.AluOpType
ACT = mybir.ActivationFunctionType
AX_X = mybir.AxisListType.X

P = 128
S = 512
NT = S // P
D = 1024
KD = D // P
DEPTH = 2
EPS = 1e-6
BIG = 1e30

Q_LORA, KV_LORA, NOPE, ROPE, VDIM = 384, 256, 64, 32, 64
MLA_H, DSA_H, SB_H, IDX_H = 6, 5, 5, 8
HD = 64
TOPK = min(256, S // 4)
D_FF = -(-8 * D // (3 * 256)) * 256
FG = 2
FJ = D_FF // P // FG
PLE = 256
REL_BUCKETS, REL_MAX = 32, 128
MIX_H = MLA_H + DSA_H + SB_H

BLK = 8
SLOTS = 3

NSA_H = 8
CB, CS, CH = 32, 16, 256
NC = (S - CB) // CS + 1
NCP = 32

HEADS = [("m", 0), ("s", 0), ("m", 1), ("s", 1), ("m", 2), ("s", 2), ("m", 3), ("s", 3),
         ("m", 4), ("s", 4), ("m", 5), ("d", 0), ("d", 1), ("d", 2), ("d", 3), ("d", 4)]
def first_tile(i):
    return NT - 1 if i % 2 else 0


def last_tile(i):
    return 0 if i % 2 else NT - 1


UNITS = [(i, t) if e == 0 else (i + 1, NT - 1 - t) for i in range(0, MIX_H, 2) for t in range(NT) for e in range(2)]
UNIT_AT = {u: n for n, u in enumerate(UNITS)}
FILLS = [("sq", 1), ("sk", 1), ("s4", 0), ("dq", 0), ("dq", 1)]
LAG = 4
EARLY_ROUNDS = 11
O_DELAY = 2
BUFS = 4
SB_BUFS = 3


PLE_ORDER = [("pp", n) for n in range(4)] + [("pg", 0, 1), ("norm", 4), ("pg", 2)] + \
    [x for n in range(3, KD) for x in ([("pp", n + 1)] if n + 1 < KD else []) + [("pg", n)]]


def attention_order(n_units, last_of_head, lag, delay=1):
    order = []
    for u in range(n_units + lag + delay):
        if u < n_units:
            order.append(("S", u))
        if 0 <= u - lag < n_units:
            order.append(("T", u - lag))
        if u >= lag + delay and last_of_head(u - lag - delay):
            order.append(("O", u - lag - delay))
    return order


def at_step(units, v, stick_kind=None):
    def unit(d, stick=None):
        if not 0 <= v - d < len(units):
            return None
        i, t = units[v - d]
        return (i, t) if stick is None or (HEADS[i][0] == stick_kind) == stick else None
    return unit


def layer_groups():
    g = [("norm", 0)] + [("iq", j) for j in range(4)] + [("iw", 0), ("dqik", 0)]
    g += [("cq", j) for j in range(3)] + [("ckv", j) for j in range(2)] + [("x", 0)]
    g += [("ix", t, h) for t in range(1, NT) for h in range(IDX_H)] + [("norm", 1), ("norm", 2)]
    g += [("tv", t) for t in range(NT)] + [("sq", 0), ("sk", 0)] + [("uk", j) for j in range(3)]
    g += [("uv", t) for t in range(NT)] + [("uq", n) for n in range(MLA_H)]
    for k, u in attention_order(len(UNITS), lambda u: UNITS[u][1] == last_tile(UNITS[u][0]), LAG, O_DELAY):
        if k == "S" and u % KD == KD - 1 and u // KD < len(FILLS):
            g.append(FILLS[u // KD])
        g.append((k, *UNITS[u]) if k != "O" else (k, UNITS[u][0]))
    g += [("wo", j) for j in range(KD)]
    for f in range(FG):
        for j in range(FJ):
            g += [("fg", f, j), ("fu", f, j)] + ([("norm", 3)] if f == j == 0 else [])
        g += [("fd", f, j) for j in range(KD)]
    for kind, *j in PLE_ORDER:
        g += [(kind, n) for n in j]
    return g


def place_groups(order):
    pools = {"S": (3, 4, 5), "fill": (2,), "ix": (4, 5, 6, 7), "T": (6, 7), "O": (0, 1), "pp": (4, 5, 6, 7),
             "small norm": (6, 7)}
    turn, last, out = {}, {}, {}
    for n, key in enumerate(order):
        kind = "fill" if key in FILLS else "small norm" if key in (("norm", 1), ("norm", 2)) else key[0]
        pool = pools.get(kind, (0, 1, 2, 3))
        i = turn.get(pool, 0)
        turn[pool] = i + 1
        bank = pool[i % len(pool)]
        out[key] = (bank, n + 1, last.get(bank))
        last[bank] = key
    return out, last


LAYER_ORDER = layer_groups()
LAYER_GROUPS, LAYER_LAST = place_groups(LAYER_ORDER)

NORMS = [(0, KD, D), (KD, 3, Q_LORA), (KD + 3, 2, KV_LORA), (KD + 5, KD, D), (2 * KD + 5, KD, D)]
NORM_TILES = 3 * KD + 5
N_IX = (NT - 1) * IDX_H
MD_UNITS = [u for u in UNITS if HEADS[u[0]][0] != "s"]
SB_UNITS = [u for u in UNITS if HEADS[u[0]][0] == "s"]
MD_AT = {u: n for n, u in enumerate(MD_UNITS)}
SB_AT = {u: n for n, u in enumerate(SB_UNITS)}
D_AT = {u: n for n, u in enumerate(u for u in UNITS if HEADS[u[0]][0] == "d")}
N_DSA = DSA_H * NT

PER = dict(
    norm_sq=NORM_TILES, norm_sum=NORM_TILES, norm_ln=5, norm_rstd=5, norm_x=NORM_TILES, norm_hi=NORM_TILES,
    norm_lo=NORM_TILES,
    iw_out=1, iq_out=4, dqik_out=3, c_out=5, dk_out=2, kr_step=3, kr_copied=2,
    ix_relu=N_IX, ix_acc=N_IX, ix_masked=NT - 1, topk_max=TOPK // 8 * (NT - 1), topk_cut=TOPK // 8 * (NT - 1),
    sel_out=NT - 1, mq_out=MLA_H, mk_out=MLA_H, mv_out=NT, dq_out=2, sqk_out=6, tv_out=NT,
    biased=N_DSA, masked=len(MD_UNITS), exped=len(MD_UNITS), inverted=len(MD_UNITS), scaled=len(MD_UNITS),
    sb_abs=len(SB_UNITS), sb_exp=len(SB_UNITS), sb_ln=len(SB_UNITS), sb_neg=len(SB_UNITS), sb_scan=len(SB_UNITS),
    sb_log=len(SB_UNITS), sb_masked=len(SB_UNITS), sb_w=len(SB_UNITS),
    pt_act=len(MD_UNITS), pt_dve=len(SB_UNITS), o_hi=MIX_H, o_lo=MIX_H,
    g_scaled=FG * FJ, u_scaled=FG * FJ, pg_scaled=KD,
    h_wo=KD, silu_out=FG * FJ, ff_out=FG * FJ, ff_hi=FG * FJ, ff_lo=FG * FJ, h_ffn=FG * KD,
    p_hi=1, p_lo=1, sig_out=KD, ple_out=KD, h_ple=KD,
)

def released(key):
    kind, n = key[0], key[1]
    if kind == "norm":
        return [("norm_ln", n + 1)]
    if kind == "O":
        return [("o_lo", n + 1)]
    if kind == "x":
        return [("kr_step", 2), ("dk_out", 2)]
    if kind in ("S", "T"):
        u = key[1:]
        head, i = HEADS[n]
        if kind == "T":
            return [("pt_dve", SB_AT[u] + 1) if head == "s" else ("pt_act", MD_AT[u] + 1)]
        if head == "s":
            return [("sb_log", SB_AT[u] + 1)]
        return [("masked", MD_AT[u] + 1) if head == "m" else ("biased", D_AT[u] + 1)]
    return [{
        "iw": ("iw_out", 1), "iq": ("iq_out", n + 1), "dqik": ("dqik_out", 3), "cq": ("c_out", n + 1),
        "ckv": ("c_out", n + 4), "ix": ("ix_relu", (n - 1) * IDX_H + key[-1] + 1),
        "uq": ("mq_out", n + 1), "uk": ("mk_out", 2 * n + 2), "uv": ("mv_out", n + 1), "dq": ("dq_out", n + 1),
        "sq": ("sqk_out", 2 * n + 1), "sk": ("sqk_out", 2 * n + 2), "s4": ("sqk_out", 6), "tv": ("tv_out", n + 1),
        "wo": ("h_wo", n + 1), "fg": ("g_scaled", n * FJ + key[-1] + 1), "fu": ("u_scaled", n * FJ + key[-1] + 1),
        "fd": ("h_ffn", n * KD + key[-1] + 1), "pp": ("ple_out", n + 1), "pg": ("pg_scaled", n + 1),
    }[kind]]


SLOPES = [2.0 ** (-8.0 * (n + 1) / NSA_H) for n in range(NSA_H)]
assert S // 64 <= 16
TAIL_LAG = 3
SUBS = [(b, j, e) for j in range(4) for e in range(2) for b in ("sel", "win")] + \
       [("swa", j, e) for j in range(4) for e in range(2)]
TUNITS = [(i, t) for i in range(len(SUBS)) for t in range(NT)]
N_SWA = NSA_H


def tail_groups():
    g = [("mod", 0), ("norm", 0), ("norm", 1), ("kc", 0), ("vc", 0), ("gw", 0)]
    g += [("qa", j) for j in range(4)] + [("hid", 0), ("hid", 1)]
    g += [("ks", 0), ("kw", 0)] + [("hT", 0), ("hT", 1)] + [("vt", t) for t in range(NT)]
    g += [("kcT", 0), ("vcT", 0)]
    g += [("cS", t) for t in range(NT)]
    g += [("qb", j) for j in range(4)] + [("kb", 0)]
    for t in range(NT):
        g += [("cT", t)]
    for k, u in attention_order(len(TUNITS), lambda u: TUNITS[u][1] == NT - 1, TAIL_LAG):
        g.append((k, *TUNITS[u]) if k != "O" else (k, TUNITS[u][0]))
    g += [("z", j) for j in range(8)]
    for j in range(KD):
        g += [("ma", j), ("ya", j), ("mb", j), ("yb", j)]
    g += [("wout", j) for j in range(KD)] + [("norm", 2)]
    return g


def shares_bank(key):
    return key[0] == "O" and key[1] % (4 if SUBS[key[1]][0] != "swa" else 2) != 0


def place_tail():
    out, last, turn = {}, {}, {}
    pools = {"S": (4, 5), "cS": (4, 5, 6, 7), "T": (6, 7), "cT": (6, 7), "hT": (6, 7)}
    for n, key in enumerate(tail_groups()):
        if shares_bank(key):
            bank = out["O", key[1] - 1][0]
            out[key] = (bank, n + 1, "same")
            last[bank] = key
            continue
        pool = pools.get(key[0], (0, 1, 2, 3))
        i = turn.get(pool, 0)
        turn[pool] = i + 1
        bank = pool[i % len(pool)]
        out[key] = (bank, n + 1, last.get(bank))
        last[bank] = key
    return out


TAIL_GROUPS = place_tail()


def tail_released(key):
    kind, n = key[0], key[1]
    if kind == "O":
        b, j, e = SUBS[n]
        return [("heads_out", j + 1 + (4 if b == "swa" else 0))]
    if kind == "S":
        return [("t_masked", n * NT + key[2] + 1)]
    if kind == "T":
        return [("t_pt", n * NT + key[2] + 1)]
    return [{
        "mod": ("mod_out", 1), "norm": ("t_ln", n + 1), "gw": ("gates_out", 1), "kc": ("cmp_in", 4), "vc": ("cmp_in", 8),
        "qa": ("q_out", n + 1), "qb": ("q_out", n + 5), "hid": ("hid_out", n + 1), "hT": ("hidT_out", n + 1),
        "ks": ("k_out", 1), "kw": ("k_out", 2), "kb": ("k_out", 3), "vt": ("v_out", n + 1),
        "kcT": ("kc_out", 2), "vcT": ("vc_out", 4), "cS": ("c_masked", n + 1), "cT": ("c_pt", n + 1),
        "z": ("z_out", n + 1), "ma": ("merge_out", 2 * n + 1), "mb": ("merge_out", 2 * n + 2),
        "ya": ("y_part", 2 * n + 1), "yb": ("y_part", 2 * n + 2), "wout": ("y2_out", n + 1),
    }[kind]]


ADA = 3 * KD
GAIN_PER_LAYER = NORM_TILES
G_FINAL = DEPTH * GAIN_PER_LAYER
G_PRE = G_FINAL + KD
G_POST = G_PRE + KD
G_BADA = G_POST + KD
G_C = G_BADA + 3 * KD
N_GAINS = G_C + KD


def tail_blocks():
    up = lambda n: -(-n // BLK) * BLK
    n = 2 + KD * (2 + 4 + 2)
    n = up(n) + KD // 2 * BLK
    n += KD * (4 + 1 + 8) + KD * (2 * KD + 2 * 4) + KD * KD
    return -(-up(n) // (BLK * SLOTS)) * BLK * SLOTS


def layer_blocks():
    up = lambda n: -(-n // BLK) * BLK
    n = up(1 + 4 * KD + KD + 5 * KD + KD) + KD // 2 * BLK
    n = up(n + 2 * KD + 2 * 3) + BLK
    n += 3 * MLA_H + 5 * KD
    return up(n + KD * KD + FG * (2 * FJ * KD + KD * FJ) + KD * (2 + KD))


def build(nc, x_t, p_t, wstream, gains, rel_bias, c_rope_q, c_rope_k, c_onehot, c_eye, c_causal, c_strict,
          w_ada, w_cmp1, w_cmp2, pe_t, sinks, c_alibi, c_window, c_cmp, c_seen,
          out_t, layers=DEPTH):
    total_chunks = wstream.shape[0]
    layer_chunks = layer_blocks() // BLK
    sem_handles = {}

    def sem(name):
        if name not in sem_handles:
            sem_handles[name] = nc.semaphore(name).__enter__()
        return sem_handles[name]

    base = -(-nc.sbuf_base // 64) * 64
    cursor = [base]

    def sb(name, shape, dt=F32, offset=None):
        words = int(np.prod(shape[1:]))
        at_ = cursor[0] if offset is None else offset
        t = nc.alloc_sbuf_tensor_at(name, shape, dt, offset=at_)
        if offset is None:
            cursor[0] += -(-words * 4 // 32) * 32
        return t

    banks = [nc.psum_tensor(f"bank{b}", [P, S], F32).__enter__() for b in range(8)]

    raw = [sb(f"raw{s}", [P, BLK * P]) for s in range(SLOTS)]
    w_hi = [sb(f"w_hi{s}", [P, BLK * P], F32R) for s in range(SLOTS)]
    w_lo = [sb(f"w_lo{s}", [P, BLK * P], F32R) for s in range(SLOTS)]
    h = sb("h", [P, KD, S])
    act_hi = sb("act_hi", [P, KD, S], F32R)
    act_lo = sb("act_lo", [P, KD, S], F32R)
    norm_at = cursor[0]
    sq = sb("sq", [P, 2, S])
    ssum = sb("ssum", [P, S])
    rstd = sb("rstd", [P, S])
    xn = sb("xn", [P, 2, S])
    isc = sb("isc", [P, NT - 1, S], offset=norm_at)
    eye = sb("eye", [P, P])
    ones = sb("ones", [P, P])
    rope_q = sb("rope_q", [P, S])
    rope_k = sb("rope_k", [P, S])
    causal = sb("causal", [P, S])
    strict = sb("strict", [P, S])
    strict_neg = sb("strict_neg", [P, P])
    g_sb = sb("g_sb", [P, N_GAINS])
    eps_col = sb("eps_col", [P, 1])
    iw_w = sb("iw_w", [P, NT, IDX_H])
    stat_min = sb("stat_min", [P, 4])
    stat_sum = sb("stat_sum", [P, 4])
    stat_inv = sb("stat_inv", [P, 4])
    top8 = sb("top8", [P, NT - 1, 8])
    nc_small = cursor[0]
    cursor[0] += 4 * (5 * KD + NT * 3 * NSA_H)
    tail_region = cursor[0]
    bias = sb("bias", [P, DSA_H, S])
    sq_b = sb("sq_b", [P, 2, S], offset=tail_region)
    ssum_b = sb("ssum_b", [P, S], offset=tail_region + 2 * 4 * S)
    rstd_b = sb("rstd_b", [P, S], offset=tail_region + 3 * 4 * S)
    region = cursor[0]
    rel_sb = sb("rel_sb", [REL_BUCKETS, DSA_H], offset=region)
    onehot = sb("onehot", [REL_BUCKETS, 640], offset=region + 64)
    rows_sb = sb("rows_sb", [DSA_H, 640], offset=region + 64 + 4 * 640)
    o_hi_low = sb("o_hi_low", [P, MLA_H, S], F32R, offset=cursor[0])
    mq = sb("mq", [P, MLA_H, S])
    o_lo_low = sb("o_lo_low", [P, MLA_H, S], F32R, offset=cursor[0])
    mk = sb("mk", [P, MLA_H, S])
    relu = sb("relu", [P, 3, S], offset=cursor[0])
    mv = sb("mv", [P, NT, MLA_H * VDIM])
    dq = sb("dq", [P, 3, S])
    dk = sb("dk", [P, S])
    tv_at = cursor[0]
    tv = sb("tv", [P, NT, HD * (1 + SB_H)])
    sq_c = sb("sq_c", [P, 2, S], offset=tv_at)
    ssum_c = sb("ssum_c", [P, S], offset=tv_at + 2 * 4 * S)
    share = cursor[0]
    iq = sb("iq", [P, 4, S], offset=share)
    ik = sb("ik", [P, S], offset=share + 4 * 4 * S)
    bq = sb("bq", [P, 3, S])
    bk = sb("bk", [P, 3, S])
    work = cursor[0]
    c_raw = sb("c_raw", [P, 5, S])
    c_hi = sb("c_hi", [P, 5, S], F32R)
    c_lo = sb("c_lo", [P, 5, S], F32R)
    top = cursor[0]
    cursor[0] = work
    xs = sb("xs", [P, 3, S])
    z1 = sb("z1", [P, 2, S])
    pr = sb("pr", [P, 3, S])
    pt = sb("pt", [P, 2, NT, S])
    xs_of = [xs[:, b, :] for b in range(3)] + [sb("xs_more", [P, S], offset=norm_at + 3 * 4 * S)]
    pr_of = [pr[:, b, :] for b in range(3)] + [sb("pr_more", [P, S], offset=norm_at + 4 * 4 * S)]
    z1_of = [z1[:, b, :] for b in range(2)] + [sb("z1_more", [P, S], offset=norm_at + 5 * 4 * S)]
    kr = sb("kr", [P, 2, S], offset=work + 5 * 4 * S * 3)
    top = max(top, cursor[0], work + 5 * 4 * S * 3 + 2 * 4 * S)
    cursor[0] = region
    ff_hi = sb("ff_hi", [P, FJ, S], F32R)
    ff_lo = sb("ff_lo", [P, FJ, S], F32R)
    gate = sb("gate", [P, 2, S])
    ffx = sb("ffx", [P, 2, S])
    p_raw = sb("p_raw", [P, 2, S])
    pp_hi = sb("pp_hi", [P, 2, S], F32R)
    pp_lo = sb("pp_lo", [P, 2, S], F32R)
    top = max(top, cursor[0])
    ada = sb("ada", [P, 2, D])
    mod_acc = sb("mod_acc", [P, 3 * D])
    top = max(top, cursor[0])
    mod = sb("mod", [P, 3 * KD], offset=nc_small)
    gain_pre = sb("gain_pre", [P, KD], offset=nc_small + 4 * 3 * KD)
    gain_post = sb("gain_post", [P, KD], offset=nc_small + 4 * 4 * KD)
    gates = sb("gates", [P, NT, 3 * NSA_H], offset=nc_small + 4 * 5 * KD)
    cursor[0] = tail_region
    KB = 1024
    qa = sb("qa", [P, 4, S])
    w1_at = cursor[0]
    alibi = sb("alibi", [P, NSA_H, S])
    window = sb("window", [P, NSA_H, 2 * P + 1])
    qb_at = cursor[0]
    qb = sb("qb", [P, 4, S])
    w1 = sb("w1", [P, 2, CB // 2, CH], offset=w1_at)
    assert w1_at + 32 * KB <= cursor[0]
    cmp_mask = sb("cmp_mask", [P, NT, NSA_H * NCP])
    ks = sb("ks", [P, S])
    kw = sb("kw", [P, S])
    kb = sb("kb", [P, S])
    vt = sb("vt", [P, NT, 3 * P])
    kct = sb("kct", [P, 2 * NCP])
    vbd = sb("vbd", [P, P])
    cpt = sb("cpt", [P, 2, S])
    cst = sb("cst", [P, 4, NSA_H])
    seen = sb("seen", [P, NT])
    sink_row = sb("sink_row", [1, NSA_H])
    ones_row = sb("ones_row", [1, P])
    pe_sb = sb("pe_sb", [P, 2, CB // 2])
    w2 = sb("w2", [P, 2, 2, HD])
    tail_work = cursor[0]
    xs2 = sb("xs2", [P, 3, S])
    pr2 = sb("pr2", [P, 3, S])
    pt2 = sb("pt2", [P, 2, NT, S])
    cx_of = [xs2[:, t, 0:NSA_H * NCP] for t in range(3)] + [pr2[:, 0, 0:NSA_H * NCP]]
    top = max(top, cursor[0])
    cursor[0] = tail_work
    cmp_x = sb("cmp_x", [P, 2, CB // 2, 2 * NCP])
    hid = sb("hid", [2 * NCP, 2, CH])
    hid_t = sb("hid_t", [P, 2, 2, 2 * NCP])
    assert cursor[0] <= tail_work + 12 * KB
    cursor[0] = w1_at
    u_hi = sb("u_hi", [P, 8, S], F32R)
    silu_z = sb("silu_z", [P, 2, S])
    ux = sb("ux", [P, 2, S])
    assert cursor[0] <= qb_at
    cursor[0] = qb_at + 8 * KB
    u_lo = sb("u_lo", [P, 8, S], F32R)
    y_hi = sb("y_hi", [P, KD, S], F32R)
    y_lo = sb("y_lo", [P, KD, S], F32R)
    yx = sb("yx", [P, 4, S], offset=tail_region)
    y2 = sb("y2", [P, KD, S], offset=w1_at)
    top = max(top, cursor[0])
    assert top <= nc.sbuf_usable_end
    bias_dram = nc.dram_tensor("bias_rows", (DSA_H, 640), F32, kind="Internal")

    n_groups = len(LAYER_ORDER)
    block = nc.Block().__enter__()

    class Layer:

        def __init__(self, n):
            self.n = n

        def at(self, name, count):
            return sem(name), self.n * PER.get(name, 0) + count

        def psum(self, *key):
            bank, place, _ = LAYER_GROUPS[key]
            return banks[bank], (sem("psum_ready"), self.n * n_groups + place)

    class Tail(Layer):

        def psum(self, *key):
            bank, place, _ = TAIL_GROUPS[key]
            return banks[bank], (sem("psum_ready"), self.n * n_groups + place)

    def mixed(j):
        if j < MLA_H:
            return o_hi_low[:, j, :], o_lo_low[:, j, :]
        return act_hi[:, j, :], act_lo[:, j, :]

    def norm_space(i):
        return (sq_c, (ssum_c, rstd)[i - 1]) if i in (1, 2) else (sq, ssum)

    def width(t):
        return (t + 1) * P

    def keys_of(sub, t):
        return (0, t + 1) if SUBS[sub][0] != "swa" else (max(t - 1, 0), min(t, 1) + 1)

    def half(i):
        return slice(64 * (i % 2), 64 * (i % 2) + 64)

    @block.sync
    def _(sp):
        sp.dma_start(g_sb[:], gains).then_inc(sem("gains_in"), 16)
        for c in range(KD // 2):
            sp.dma_start(h[:, 2 * c:2 * c + 2, :], x_t[:, 2 * c:2 * c + 2, :]).then_inc(sem(f"x_in{c}"), 16)
        for s in range(SLOTS):
            sp.dma_start(raw[s][:], wstream[s]).then_inc(sem(f"raw_in{s}"), 16)
        sp.dma_start(rel_sb[:], rel_bias).then_inc(sem("rel_in"), 16)
        sp.dma_start(onehot[:], c_onehot).then_inc(sem("rel_in"), 16)
        for dst, src in ((eye, c_eye), (rope_q, c_rope_q), (rope_k, c_rope_k), (causal, c_causal), (strict, c_strict)):
            sp.dma_start(dst[:], src).then_inc(sem("consts_in"), 16)
        with sp.Fori(1, total_chunks // SLOTS) as i:
            for s in range(SLOTS):
                sp.wait_ge(sem("split_lo"), i * SLOTS + (s + 1 - SLOTS))
                sp.dma_start(raw[s][:], wstream[i * SLOTS + s]).then_inc(sem(f"raw_in{s}"), 16)
        for k in range(KD):
            sp.wait_ge(sem("x_final"), k + 1)
            sp.dma_start(out_t[:, k, :], h[:, k, :]).then_inc(sem("stored"), 16)
        sp.wait_ge(sem("stored"), 16 * KD)

    @block.gpsimd
    def _(pool):
        pool.memset(ones[:], 1.0).then_inc(sem("ones_set"), 1)
        pool.memset(eps_col[:], EPS).then_inc(sem("eps_set"), 1)

        def split(s, count, used):
            pool.wait_ge(sem(f"raw_in{s}"), count)
            if used is not None:
                pool.wait_ge(sem("chunk_used"), used)
            pool.sem_inc(sem("slot_turn"), 1)
            pool.tensor_scalar(w_hi[s][:], raw[s][:], 1.0, 0.0, ALU.mult, ALU.add).then_inc(sem("split_hi"), 1)
            return s

        def rest(s, hi_count):
            pool.wait_ge(sem("split_hi"), hi_count)
            pool.tensor_tensor(w_lo[s][:], raw[s][:], w_hi[s][:].bitcast(F32), ALU.subtract)\
                .then_inc(sem("split_lo"), 1)

        for s in range(SLOTS):
            split(s, 16, None)
            rest(s, s + 1)
        with pool.Fori(1, total_chunks // SLOTS) as i:
            for s in range(SLOTS):
                landed, used, hi_done = [pool.snap(v) for v in (i * 16 + 16, i * SLOTS + (s + 1 - SLOTS),
                                                                i * SLOTS + (s + 1))]
                split(s, landed, used)
                rest(s, hi_done)

    @block.tensor
    def _(pe):
        stream = {"block": 0, "pending": 0}

        def finish(ins, last):
            if last:
                ins.then_inc(sem("psum_ready"), 1)
            elif stream["pending"]:
                ins.then_inc(sem("chunk_used"), stream["pending"])
                stream["pending"] = 0
            return ins

        def open_group(L, key):
            if isinstance(L, Tail):
                bank, _, prev = TAIL_GROUPS[key]
                if prev != "same":
                    for name, count in released(LAYER_LAST[bank]) if prev is None else tail_released(prev):
                        pe.wait_ge(*Layer(L.n - (prev is None)).at(name, count))
                return banks[bank]
            bank, _, prev = LAYER_GROUPS[key]
            n = L.n
            if prev is None:
                n, prev = n - 1, LAYER_LAST[bank]
            if n >= 0:
                for name, count in released(prev):
                    pe.wait_ge(*Layer(n).at(name, count))
            return banks[bank]

        def next_block(n=1):
            b = stream["block"]
            chunk = b // BLK
            assert (b + n - 1) // BLK == chunk
            if b % BLK == 0:
                pe.wait_ge(sem("split_lo"), chunk + 1)
            stream["block"] = b + n
            cols = slice(b % BLK * P, (b % BLK + n) * P)
            return w_hi[chunk % SLOTS][:, cols], w_lo[chunk % SLOTS][:, cols]

        def end_block():
            if stream["block"] % BLK == 0:
                stream["pending"] += 1

        def align():
            if stream["block"] % BLK:
                stream["block"] += BLK - stream["block"] % BLK
                stream["pending"] += 1

        def linear(L, key, tiles, ready=None):
            acc = open_group(L, key)
            n = len(tiles)
            for k, (hi, lo) in enumerate(tiles):
                if ready is not None:
                    pe.wait_ge(*ready(k))
                wh, wl = next_block()
                finish(pe.matmul(acc[:], wh, hi, start=k == 0, stop=False), False)
                finish(pe.matmul(acc[:], wh, lo, start=False, stop=False), False)
                ins = pe.matmul(acc[:], wl, hi, start=False, stop=k == n - 1)
                end_block()
                finish(ins, k == n - 1)

        def linear_pair(L, keys, tiles, ready=None):
            accs = [open_group(L, key) for key in keys]
            n = len(tiles)
            for k, (hi, lo) in enumerate(tiles):
                if ready is not None:
                    pe.wait_ge(*ready(k))
                for acc in accs:
                    wh, wl = next_block()
                    finish(pe.matmul(acc[:], wh, hi, start=k == 0, stop=False), False)
                    finish(pe.matmul(acc[:], wh, lo, start=False, stop=False), False)
                    ins = pe.matmul(acc[:], wl, hi, start=False, stop=k == n - 1)
                    end_block()
                    finish(ins, k == n - 1)

        def tiles_of(hi, lo, n, first=0):
            return [(hi[:, k, :], lo[:, k, :]) for k in range(first, first + n)]

        def token_major(L, kind, hi, lo, n, first=0, per_chunk=2, n_blocks=3):
            accs = [open_group(L, (kind, t)) for t in range(NT)]
            align()
            for k in range(n):
                wh, wl = next_block(n_blocks)
                for t in range(NT):
                    cols = slice(t * P, t * P + P)
                    o = accs[t][:, 0:n_blocks * P]
                    a_hi, a_lo = hi[:, first + k, cols], lo[:, first + k, cols]
                    finish(pe.matmul(o, a_hi, wh, start=k == 0, stop=False), False)
                    finish(pe.matmul(o, a_lo, wh, start=False, stop=False), False)
                    ins = pe.matmul(o, a_hi, wl, start=False, stop=k == n - 1)
                    finish(ins, k == n - 1)
                if k % per_chunk == per_chunk - 1 or k == n - 1:
                    align()

        def fill(L, key, k):
            acc = open_group(L, key) if k == 0 else banks[LAYER_GROUPS[key][0]]
            wh, wl = next_block()
            finish(pe.matmul(acc[:], wh, act_hi[:, k, :], start=k == 0, stop=False), False)
            finish(pe.matmul(acc[:], wh, act_lo[:, k, :], start=False, stop=False), False)
            ins = pe.matmul(acc[:], wl, act_hi[:, k, :], start=False, stop=k == KD - 1)
            end_block()
            finish(ins, k == KD - 1)

        def norm_sum(L, i):
            first, n, _ = NORMS[i]
            acc = open_group(L, ("norm", i))
            pe.wait_ge(*L.at("norm_sum", first + n))
            finish(pe.matmul(acc[:], ones[:], norm_space(i)[1][:], start=True, stop=True), True)

        def attention(L):
            def scores(i, t):
                kind, n = HEADS[i]
                acc = open_group(L, ("S", i, t))
                cols = slice(t * P, t * P + P)
                if kind == "m":
                    pe.wait_ge(*L.at("mq_out", n + 1))
                    pe.wait_ge(*L.at("mk_out", n + 1))
                    pe.wait_ge(*L.at("kr_copied", 2))
                    q, k = mq[:, n, cols], mk[:, n, 0:width(t)]
                elif kind == "d":
                    if n < 4:
                        pe.wait_ge(*L.at("dq_out", n // 2 + 1))
                    pe.wait_ge(*L.at("dqik_out", 3))
                    pe.wait_ge(*L.at("dk_out", 2))
                    q, k = dq[half(n), n // 2, cols], dk[half(n), 0:width(t)]
                else:
                    pe.wait_ge(*L.at("sqk_out", 2 * (n // 2) + 2))
                    q, k = bq[half(n), n // 2, cols], bk[half(n), n // 2, 0:width(t)]
                finish(pe.matmul(acc[:, 0:width(t)], q, k, start=True, stop=True), True)

            def transpose(i, t):
                kind, n = HEADS[i]
                acc = open_group(L, ("T", i, t))
                if kind == "s":
                    pe.wait_ge(*L.at("sb_w", SB_AT[i, t] + 1))
                else:
                    pe.wait_ge(*L.at("scaled", MD_AT[i, t] + 1))
                src = pr_of[UNIT_AT[i, t] % BUFS]
                for k in range(t + 1):
                    cols = slice(k * P, k * P + P)
                    finish(pe.transpose(acc[:, cols], src[:, cols], eye[:]), k == t)

            def output(i):
                kind, n = HEADS[i]
                acc = open_group(L, ("O", i))
                if kind == "s":
                    pe.wait_ge(*L.at("pt_dve", SB_AT[i, last_tile(i)] + 1))
                else:
                    pe.wait_ge(*L.at("pt_act", MD_AT[i, last_tile(i)] + 1))
                if kind == "m":
                    pe.wait_ge(*L.at("mv_out", NT))
                else:
                    pe.wait_ge(*L.at("tv_out", NT))
                for k in range(NT):
                    if kind == "m":
                        v = mv[:, k, n * VDIM:(n + 1) * VDIM]
                    elif kind == "d":
                        v = tv[:, k, 0:HD]
                    else:
                        v = tv[:, k, HD * (1 + n):HD * (2 + n)]
                    finish(pe.matmul(acc[half(i), k * P:S], v, pt[:, i % 2, k, k * P:S], start=k == 0,
                                     stop=k == NT - 1), k == NT - 1)

            for kind, u in attention_order(len(UNITS), lambda u: UNITS[u][1] == last_tile(UNITS[u][0]), LAG, O_DELAY):
                if kind == "S":
                    if u // KD < len(FILLS):
                        fill(L, FILLS[u // KD], u % KD)
                    scores(*UNITS[u])
                elif kind == "T":
                    transpose(*UNITS[u])
                else:
                    output(UNITS[u][0])

        pe.wait_ge(sem("ones_set"), 1)
        for layer in range(layers):
            L = Layer(layer)
            stream["block"] = layer * layer_chunks * BLK
            hn = tiles_of(act_hi, act_lo, KD)
            norm_sum(L, 0)
            linear_pair(L, [("iq", 0), ("iq", 1)], hn, lambda k: L.at("norm_lo", k + 1))
            for j in range(2, 4):
                linear(L, ("iq", j), hn)
            acc = open_group(L, ("iw", 0))
            wh, wl = next_block()
            for t in range(NT):
                for k in range(KD):
                    cols = slice(t * P, t * P + P)
                    o = acc[:, t * IDX_H:(t + 1) * IDX_H]
                    ws = slice(k * IDX_H, (k + 1) * IDX_H)
                    finish(pe.matmul(o, act_hi[:, k, cols], wh[:, ws], start=k == 0, stop=False), False)
                    finish(pe.matmul(o, act_lo[:, k, cols], wh[:, ws], start=False, stop=False), False)
                    ins = pe.matmul(o, act_hi[:, k, cols], wl[:, ws], start=False, stop=k == KD - 1)
                    finish(ins, t == NT - 1 and k == KD - 1)
            end_block()
            if layer == 0:
                pe.wait_ge(sem("rel_in"), 32)
                for c in range(2):
                    pe.matmul(banks[6 + c][0:DSA_H, 0:320], rel_sb[:], onehot[:, c * 320:(c + 1) * 320], start=True,
                              stop=True).then_inc(sem("rows_ready"), 1)
            linear(L, ("dqik", 0), hn)
            for j in range(3):
                linear(L, ("cq", j), hn)
            for j in range(2):
                linear(L, ("ckv", j), hn)
            linear(L, ("x", 0), hn)
            if layer == 0:
                pe.wait_ge(sem("rows_out"), 2)
            for t in range(1, NT):
                for n in range(IDX_H):
                    acc = open_group(L, ("ix", t, n))
                    pe.wait_ge(*L.at("dqik_out", 3))
                    pe.wait_ge(*L.at("iq_out", 4))
                    finish(pe.matmul(acc[:, 0:width(t)], iq[half(n), n // 2, t * P:t * P + P],
                                     ik[half(n), 0:width(t)], start=True, stop=True), True)
            norm_sum(L, 1)
            norm_sum(L, 2)
            token_major(L, "tv", act_hi, act_lo, KD)
            linear(L, ("sq", 0), hn)
            linear(L, ("sk", 0), hn)
            for j in range(3):
                linear(L, ("uk", j), tiles_of(c_hi, c_lo, 2, 3), lambda k: L.at("norm_lo", KD + 3 + k + 1))
            token_major(L, "uv", c_hi, c_lo, 2, 3)
            for n in range(MLA_H):
                linear(L, ("uq", n), tiles_of(c_hi, c_lo, 3), lambda k: L.at("norm_lo", KD + k + 1))
            if layer == 0:
                pe.wait_ge(sem("consts_in"), 16 * 5)
            attention(L)
            for j in range(KD):
                linear(L, ("wo", j), [mixed(k) for k in range(KD)], lambda k: L.at("o_lo", 2 * k + 2))
            for f in range(FG):
                for j in range(FJ):
                    if f == j == 0:
                        linear_pair(L, [("fg", f, j), ("fu", f, j)], hn,
                                    lambda k: L.at("norm_lo", NORMS[3][0] + k + 1))
                        norm_sum(L, 3)
                    else:
                        linear(L, ("fg", f, j), hn)
                        linear(L, ("fu", f, j), hn)
                for j in range(KD):
                    ready = (lambda k: L.at("ff_lo", f * FJ + k + 1)) if j == 0 else None
                    linear(L, ("fd", f, j), tiles_of(ff_hi, ff_lo, FJ), ready)
            for kind, *j in PLE_ORDER:
                if kind == "norm":
                    norm_sum(L, 4)
                elif kind == "pp":
                    linear(L, ("pp", *j), tiles_of(pp_hi, pp_lo, 2), lambda k: L.at("p_lo", 1))
                elif len(j) == 2:
                    linear_pair(L, [("pg", n) for n in j], hn, lambda k: L.at("norm_lo", NORMS[4][0] + k + 1))
                else:
                    linear(L, ("pg", *j), hn)
            align()
            assert stream["block"] <= (layer + 1) * layer_chunks * BLK
            while stream["block"] < (layer + 1) * layer_chunks * BLK:
                stream["block"] += BLK
                stream["pending"] += 1

        L = Tail(layers)
        stream["block"] = layers * layer_chunks * BLK
        acc = open_group(L, ("mod", 0))
        pe.wait_ge(sem("ada_summed"), ADA)
        for n in range(3 * KD):
            finish(pe.matmul(acc[:, n:n + 1], mod_acc[:, n * P:(n + 1) * P], ones[:, 0:1], start=True, stop=True),
                   n == 3 * KD - 1)
        for n in range(2):
            acc = open_group(L, ("norm", n))
            pe.wait_ge(sem("t_sum"), 2 * KD - 1 + n)
            finish(pe.matmul(acc[:], ones[:], (ssum, ssum_b)[n][:], start=True, stop=True), True)
        hn = tiles_of(act_hi, act_lo, KD)
        linear_pair(L, [("kc", 0), ("vc", 0)], hn, lambda k: (sem("t_lo"), k + 1))
        acc = open_group(L, ("gw", 0))
        wh, wl = next_block(2)
        for t in range(NT):
            for k in range(KD):
                cols, ws = slice(t * P, t * P + P), slice(k * 3 * NSA_H, (k + 1) * 3 * NSA_H)
                o = acc[:, t * 3 * NSA_H:(t + 1) * 3 * NSA_H]
                finish(pe.matmul(o, act_hi[:, k, cols], wh[:, ws], start=k == 0, stop=False), False)
                finish(pe.matmul(o, act_lo[:, k, cols], wh[:, ws], start=False, stop=False), False)
                finish(pe.matmul(o, act_hi[:, k, cols], wl[:, ws], start=False, stop=k == KD - 1),
                       t == NT - 1 and k == KD - 1)
        for j in range(4):
            linear(L, ("qa", j), hn)
        pe.wait_ge(sem("cmp_w_in"), 16 * 2)
        for n in range(2):
            acc = open_group(L, ("hid", n))
            pe.wait_ge(sem("cmp_in"), 4 * n + 4)
            for k in range(CB // 2):
                finish(pe.matmul(acc[0:2 * NCP, 0:CH], cmp_x[:, n, k, :], w1[:, n, k, :], start=k == 0,
                                 stop=k == CB // 2 - 1), k == CB // 2 - 1)
        linear(L, ("ks", 0), hn)
        linear(L, ("kw", 0), hn)
        for n in range(2):
            acc = open_group(L, ("hT", n))
            pe.wait_ge(sem("hid_out"), n + 1)
            for c in range(2):
                finish(pe.transpose(acc[:, c * 2 * NCP:(c + 1) * 2 * NCP], hid[:, n, c * P:(c + 1) * P],
                                    eye[0:2 * NCP, 0:2 * NCP]), c == 1)
        token_major(L, "vt", act_hi, act_lo, KD)
        acc = open_group(L, ("kcT", 0))
        pe.wait_ge(sem("hidT_out"), 1)
        for c in range(2):
            finish(pe.matmul(acc[0:HD, 0:2 * NCP], w2[:, 0, c, :], hid_t[:, 0, c, :], start=c == 0, stop=c == 1), c == 1)
        acc = open_group(L, ("vcT", 0))
        pe.wait_ge(sem("hidT_out"), 2)
        for c in range(2):
            finish(pe.matmul(acc[0:2 * NCP, 0:HD], hid_t[:, 1, c, :], w2[:, 1, c, :], start=c == 0, stop=c == 1), c == 1)
        for t in range(NT):
            acc = open_group(L, ("cS", t))
            pe.wait_ge(sem("kc_out"), 2)
            pe.wait_ge(sem("q_out"), 4)
            for j in range(4):
                finish(pe.matmul(acc[:, j * 2 * NCP:(j + 1) * 2 * NCP], qa[:, j, t * P:t * P + P], kct[:],
                                 start=True, stop=True), j == 3)
        for j in range(4):
            linear(L, ("qb", j), hn)
        linear(L, ("kb", 0), hn)
        for t in range(NT):
            acc = open_group(L, ("cT", t))
            pe.wait_ge(sem("c_scaled"), t + 1)
            for c in range(2):
                finish(pe.transpose(acc[:, c * P:(c + 1) * P], cx_of[t][:, c * P:(c + 1) * P], eye[:]), c == 1)

        def t_scores(i, t):
            b, j, e = SUBS[i]
            acc = open_group(L, ("S", i, t))
            first, n = keys_of(i, t)
            pe.wait_ge(sem("q_out"), 8)
            pe.wait_ge(sem("k_out"), 3)
            q = (qb if b == "swa" else qa)[half(e), j, t * P:t * P + P]
            k = {"sel": ks, "win": kw, "swa": kb}[b][half(e), first * P:(first + n) * P]
            finish(pe.matmul(acc[:, 0:n * P], q, k, start=True, stop=True), b != "swa")
            if b == "swa":
                head = j + 4 * e
                finish(pe.matmul(acc[:, n * P:n * P + 1], ones_row[:], sink_row[:, head:head + 1], start=True,
                                 stop=True), True)

        def t_transpose(i, t):
            acc = open_group(L, ("T", i, t))
            pe.wait_ge(sem("t_scaled"), i * NT + t + 1)
            _, n = keys_of(i, t)
            for k in range(n):
                cols = slice(k * P, k * P + P)
                finish(pe.transpose(acc[:, cols], pr2[:, (i * NT + t) % 3, cols], eye[:]), k == n - 1)

        def t_output(i):
            b, j, e = SUBS[i]
            acc = open_group(L, ("O", i))
            pe.wait_ge(sem("t_pt"), (i + 1) * NT)
            if b == "sel" and e == 0:
                pe.wait_ge(sem("vc_out"), 4)
                pe.wait_ge(sem("c_pt"), NT)
                rows = half(j)
                finish(pe.matmul(acc[:], vbd[rows, :], cpt[rows, j // 2, :], start=True, stop=False), False)
            pe.wait_ge(sem("v_out"), NT)
            v0 = {"sel": 0, "win": P, "swa": 2 * P}[b] + e * HD
            if b == "swa":
                for t in range(NT):
                    first, n = keys_of(i, t)
                    for k in range(first, first + n):
                        cols = slice(t * P, t * P + P)
                        finish(pe.matmul(acc[half(e), cols], vt[:, k, v0:v0 + HD], pt2[:, i % 2, k, cols],
                                         start=k == first, stop=k == first + n - 1), t == NT - 1 and k == NT - 1)
            else:
                for k in range(NT):
                    last = k == NT - 1
                    finish(pe.matmul(acc[half(e), k * P:S], vt[:, k, v0:v0 + HD], pt2[:, i % 2, k, k * P:S],
                                     start=False, stop=last and b == "win"), last)

        pe.wait_ge(sem("sinks_in"), 16)
        pe.wait_ge(sem("ones_row_set"), 1)
        for kind, u in attention_order(len(TUNITS), lambda u: TUNITS[u][1] == NT - 1, TAIL_LAG):
            if kind == "S":
                t_scores(*TUNITS[u])
            elif kind == "T":
                t_transpose(*TUNITS[u])
            else:
                t_output(TUNITS[u][0])
        for j in range(8):
            linear(L, ("z", j), hn)
        for j in range(KD):
            linear(L, ("ma", j), hn)
            linear(L, ("ya", j), tiles_of(u_hi, u_lo, 4), lambda k: L.at("u_lo", k + 1))
            linear(L, ("mb", j), hn)
            linear(L, ("yb", j), tiles_of(u_hi, u_lo, 4, 4), lambda k: L.at("u_lo", k + 5))
        for j in range(KD):
            linear(L, ("wout", j), tiles_of(y_hi, y_lo, KD), lambda k: L.at("y_lo", k + 1))
        acc = open_group(L, ("norm", 2))
        pe.wait_ge(sem("t_sum"), 3 * KD)
        finish(pe.matmul(acc[:], ones[:], ssum[:], start=True, stop=True), True)

    @block.scalar
    def _(act):
        def use_exp_ln():
            act.preload_act_table_set("natural_log_exp_and_others")

        def squares(L, i, src, ready, only=None):
            first, n, _ = NORMS[i]
            for k in range(n) if only is None else [only]:
                act.wait_ge(*ready(k))
                if first + k >= 2 or L.n:
                    act.wait_ge(*L.at("norm_sum", first + k - 1))
                act.activation(norm_space(i)[0][:, (first + k) % 2, :], src(k), ACT.Square)\
                    .then_inc(sem("norm_sq"), 1)

        def late_norm(L, i, name, done, last_reader):
            first, _, _ = NORMS[i]
            for k in range(KD):
                squares(L, i, lambda k: h[:, k, :], lambda k: L.at(name, done + k + 1), only=k)
                act.wait_ge(*L.at("norm_x", first + k + 1))
                if last_reader is not None and k >= MLA_H:
                    act.wait_ge(*last_reader)
                act.activation(act_hi[:, k, :], xn[:, (first + k) % 2, :], ACT.Copy).then_inc(sem("norm_hi"), 1)

        def norm_rest(L, i, hi=None, first_tile=0):
            first, n, dim = NORMS[i]
            ps, ready = L.psum("norm", i)
            act.wait_ge(*ready)
            if i == 0:
                if L.n:
                    act.wait_ge(*Layer(L.n - 1).at("pg_scaled", KD))
            elif i == 4:
                act.wait_ge(*L.at("u_scaled", FG * FJ))
            else:
                act.wait_ge(*L.at("norm_x", first))
            act.activation(rstd[:], ps[:], ACT.Ln, bias=eps_col[:], scale=1.0 / dim).then_inc(sem("norm_ln"), 1)
            act.wait_ge(*L.at("norm_ln", i + 1))
            act.activation(rstd[:], rstd[:], ACT.Exp, scale=-0.5).then_inc(sem("norm_rstd"), 1)
            for k in range(n if hi is not None else 0):
                act.wait_ge(*L.at("norm_x", first + k + 1))
                act.activation(hi[:, first_tile + k, :], xn[:, (first + k) % 2, :], ACT.Copy)\
                    .then_inc(sem("norm_hi"), 1)

        def take(L, key, name, pairs, scale=1.0):
            ps, ready = L.psum(*key)
            act.wait_ge(*ready)
            for dst, rows in pairs:
                act.activation(dst, ps[rows, :], ACT.Copy, scale=scale).then_inc(sem(name), 1)

        full, lower, upper = slice(0, P), slice(0, 64), slice(64, P)

        def ada_load(n):
            if n < ADA:
                if n >= 2:
                    act.wait_ge(sem("ada_summed"), n - 1)
                k, c = divmod(n, 3)
                act.dma_start(ada[:, n % 2, :], w_ada[:, k, c * D:(c + 1) * D]).then_inc(sem(f"ada_in{n % 2}"), 16)

        def t_squares(k, ready):
            act.wait_ge(*ready)
            if k < 2:
                act.wait_ge(*Layer(layers - 1).at("norm_sum", NORM_TILES))
            else:
                act.wait_ge(sem("t_sum"), 2 * k - 2)
            act.activation(sq[:, k % 2, :], h[:, k, :], ACT.Square).then_inc(sem("t_sq"), 1)
            act.activation(sq_b[:, k % 2, :], h[:, k, :], ACT.Square, scale=g_sb[:, G_FINAL + k:G_FINAL + k + 1])\
                .then_inc(sem("t_sq"), 1)

        act.wait_ge(sem("eps_set"), 1)
        act.wait_ge(sem("gains_in"), 16)
        for layer in range(layers):
            L = Layer(layer)
            if layer == 0:
                use_exp_ln()
                squares(L, 0, lambda k: h[:, k, :], lambda k: (sem(f"x_in{k // 2}"), 16))
            norm_rest(L, 0, act_hi)
            for j in range(4):
                take(L, ("iq", j), "iq_out", [(iq[:, j, :], full)], HD ** -0.5)
            ps, ready = L.psum("iw", 0)
            act.wait_ge(*ready)
            act.activation(iw_w[:].rearrange("p t h -> p (t h)"), ps[:, 0:NT * IDX_H], ACT.Copy,
                           scale=IDX_H ** -0.5).then_inc(sem("iw_out"), 1)
            if layer == 0:
                act.wait_ge(sem("rows_out"), 2)
                act.dma_start(bias_dram.ap(), rows_sb[:]).then_inc(sem("rows_stored"), 16)
            ps, ready = L.psum("dqik", 0)
            act.wait_ge(*ready)
            act.activation(dq[lower, 2, :], ps[lower, :], ACT.Copy, scale=-HD ** -0.5).then_inc(sem("dqik_out"), 1)
            act.activation(ik[lower, :], ps[upper, :], ACT.Copy).then_inc(sem("dqik_out"), 1)
            act.activation(ik[upper, :], ps[upper, :], ACT.Copy).then_inc(sem("dqik_out"), 1)
            for j in range(3):
                take(L, ("cq", j), "c_out", [(c_raw[:, j, :], full)])
            for j in range(2):
                take(L, ("ckv", j), "c_out", [(c_raw[:, 3 + j, :], full)])
            ps, ready = L.psum("x", 0)
            act.wait_ge(*ready)
            act.activation(dk[lower, :], ps[lower, :], ACT.Copy).then_inc(sem("dk_out"), 1)
            act.activation(dk[upper, :], ps[lower, :], ACT.Copy).then_inc(sem("dk_out"), 1)
            def index_relu(t):
                for n in range(IDX_H):
                    u = (t - 1) * IDX_H + n
                    ps, ready = L.psum("ix", t, n)
                    act.wait_ge(*ready)
                    if u >= 3:
                        act.wait_ge(*L.at("ix_acc", u - 2))
                    act.activation(relu[:, u % 3, 0:width(t)], ps[:, 0:width(t)], ACT.Relu)\
                        .then_inc(sem("ix_relu"), 1)

            def projection_out(name, j):
                if name == "dq":
                    take(L, ("dq", j), "dq_out", [(dq[:, j, :], full)], -HD ** -0.5)
                elif name == "sq":
                    take(L, ("sq", j), "sqk_out", [(bq[:, j, :], full)], HD ** -0.5)
                elif name == "sk":
                    take(L, ("sk", j), "sqk_out", [(bk[:, j, :], full)])
                elif name == "s4":
                    take(L, ("s4", 0), "sqk_out", [(bq[lower, 2, :], lower)], HD ** -0.5)
                    take(L, ("s4", 0), "sqk_out", [(bk[lower, 2, :], upper)])

            squares(L, 1, lambda k: c_raw[:, k, :], lambda k: L.at("c_out", k + 1))
            squares(L, 2, lambda k: c_raw[:, 3 + k, :], lambda k: L.at("c_out", 4 + k))
            for t in range(1, NT):
                index_relu(t)
            act.wait_ge(*L.psum("norm", 2)[1])
            norm_rest(L, 1, c_hi, 0)
            norm_rest(L, 2, c_hi, 3)
            if layer == 0:
                act.wait_ge(sem("rows_stored"), 16)
                for n in range(DSA_H):
                    act.dma_start(bias[:, n, :], bass.AP(bias_dram, n * 640, [[1, P], [1, S]]))\
                        .then_inc(sem("bias_in"), 16)
            act.wait_ge(*L.at("kr_step", 3))
            for r in (64, 96):
                act.activation(mk[r:r + 32, :, :], kr[64:96, 0, :].unsqueeze(1).broadcast_to([32, MLA_H, S]),
                               ACT.Copy).then_inc(sem("kr_copied"), 1)
            act.wait_ge(*L.at("norm_sum", KD + 5))
            for t in range(NT):
                ps, ready = L.psum("tv", t)
                act.wait_ge(*ready)
                act.activation(tv[:, t, :], ps[:, 0:HD * (1 + SB_H)], ACT.Copy).then_inc(sem("tv_out"), 1)
            projection_out("sq", 0)
            projection_out("sk", 0)
            for j in range(3):
                take(L, ("uk", j), "mk_out", [(mk[lower, 2 * j, :], lower), (mk[lower, 2 * j + 1, :], upper)])
            act.wait_ge(*L.at("ix_acc", N_IX))
            for t in range(NT):
                ps, ready = L.psum("uv", t)
                act.wait_ge(*ready)
                act.activation(mv[:, t, :], ps[:, 0:MLA_H * VDIM], ACT.Copy).then_inc(sem("mv_out"), 1)

            def before_scores_out(i, t):
                u = UNIT_AT[i, t]
                if u >= BUFS:
                    act.wait_ge(*L.psum("T", *UNITS[u - BUFS])[1])

            def softmax_exp(i, t):
                n = MD_AT[i, t]
                u = UNIT_AT[i, t]
                before_scores_out(i, t)
                act.wait_ge(*L.at("masked", n + 1))
                if n >= 4:
                    act.wait_ge(*L.at("inverted", n - 3))
                act.activation(pr_of[u % BUFS][:, 0:width(t)], xs_of[u % BUFS][:, 0:width(t)], ACT.Exp,
                               bias=stat_min[:, n % 4:n % 4 + 1], scale=-1.0,
                               accum_out=stat_sum[:, n % 4:n % 4 + 1]).then_inc(sem("exped"), 1)

            def stick_logs(i, t):
                n = SB_AT[i, t]
                w = width(t)
                ps, ready = L.psum("S", i, t)
                act.wait_ge(*ready)
                if n >= SB_BUFS:
                    act.wait_ge(*L.at("sb_log", n - SB_BUFS + 1))
                b = z1_of[n % SB_BUFS][:, 0:w]
                act.activation(b, ps[:, 0:w], ACT.Abs).then_inc(sem("sb_abs"), 1)
                act.wait_ge(*L.at("sb_abs", n + 1))
                act.activation(b, b, ACT.Exp, scale=-1.0).then_inc(sem("sb_exp"), 1)
                act.wait_ge(*L.at("sb_exp", n + 1))
                act.activation(b, b, ACT.Ln, bias=1.0).then_inc(sem("sb_ln"), 1)

            def stick_exp(i, t):
                n = SB_AT[i, t]
                u = UNIT_AT[i, t]
                before_scores_out(i, t)
                act.wait_ge(*L.at("sb_masked", n + 1))
                act.activation(pr_of[u % BUFS][:, 0:width(t)], xs_of[u % BUFS][:, 0:width(t)], ACT.Exp)\
                    .then_inc(sem("sb_w"), 1)

            def probs_out(i, t):
                ps, ready = L.psum("T", i, t)
                act.wait_ge(*ready)
                if t == first_tile(i) and i >= 2:
                    act.wait_ge(*L.psum("O", i - 2)[1])
                act.activation(pt[:, i % 2, 0:t + 1, t * P:t * P + P],
                               ps[:, 0:width(t)].rearrange("p (k q) -> p k q", q=P), ACT.Copy)\
                    .then_inc(sem("pt_act"), 1)

            def head_out(i):
                ps, ready = L.psum("O", i)
                act.wait_ge(*ready)
                act.activation(mixed(i // 2)[0][half(i), :], ps[half(i), :], ACT.Copy).then_inc(sem("o_hi"), 1)

            for v in range(len(UNITS) + LAG + 1 + O_DELAY):
                unit = at_step(UNITS, v, "s")
                if v % KD == 0 and 0 < v // KD <= len(FILLS):
                    projection_out(*FILLS[v // KD - 1])
                if unit(LAG + 1, stick=False):
                    probs_out(*unit(LAG + 1))
                if unit(LAG + 1 + O_DELAY) and unit(LAG + 1 + O_DELAY)[1] == last_tile(unit(LAG + 1 + O_DELAY)[0]):
                    head_out(unit(LAG + 1 + O_DELAY)[0])
                if unit(0, stick=True):
                    stick_logs(*unit(0))
                if unit(1, stick=False):
                    softmax_exp(*unit(1))
                if unit(2, stick=True):
                    stick_exp(*unit(2))

            late_norm(L, 3, "h_wo", 0, L.psum("wo", KD - 1)[1])
            norm_rest(L, 3)
            act.dma_start(p_raw[:], p_t[layer]).then_inc(sem("p_in"), 16)
            act.wait_ge(sem("p_in"), 16 * (layer + 1))
            act.activation(pp_hi[:], p_raw[:], ACT.Copy).then_inc(sem("p_hi"), 1)
            if layer == layers - 1:
                ada_load(0)
                ada_load(1)
            for f in range(FG):
                for j in range(FJ):
                    n = f * FJ + j
                    act.wait_ge(*L.at("g_scaled", n + 1))
                    act.activation(gate[:, n % 2, :], gate[:, n % 2, :], ACT.Silu).then_inc(sem("silu_out"), 1)
                    act.wait_ge(*L.at("ff_out", n + 1))
                    act.activation(ff_hi[:, j, :], ffx[:, n % 2, :], ACT.Copy).then_inc(sem("ff_hi"), 1)
                    if layer == layers - 1 and n < ADA // 2:
                        ada_load(2 * n + 2)
                        ada_load(2 * n + 3)
            use_exp_ln()
            late_norm(L, 4, "h_ffn", KD, None)
            norm_rest(L, 4)
            def next_squares(k):
                ready = L.at("h_ple", k + 1)
                if layer < layers - 1:
                    squares(Layer(layer + 1), 0, lambda k: h[:, k, :], lambda k: ready, only=k)
                else:
                    t_squares(k, ready)

            for j in range(KD):
                act.wait_ge(*L.at("pg_scaled", j + 1))
                act.activation(gate[:, j % 2, :], gate[:, j % 2, :], ACT.Sigmoid).then_inc(sem("sig_out"), 1)
                if j:
                    next_squares(j - 1)
            use_exp_ln()
            next_squares(KD - 1)

        L = Tail(layers)

        def t_rstd(i, ps, out):
            act.activation(out[:], ps[:], ACT.Ln, bias=eps_col[:], scale=1.0 / D).then_inc(sem("t_ln"), 1)
            act.wait_ge(sem("t_ln"), i + 1)
            act.activation(out[:], out[:], ACT.Exp, scale=-0.5).then_inc(sem("t_rstd"), 1)

        act.wait_ge(*L.psum("norm", 0)[1])
        act.wait_ge(*Layer(layers - 1).at("pg_scaled", KD))
        t_rstd(0, L.psum("norm", 0)[0], rstd)
        act.wait_ge(sem("mean_b"), 2)
        t_rstd(1, rstd_b, rstd_b)
        act.wait_ge(sem("mod_out"), 1)
        act.dma_start(pe_sb[:], pe_t).then_inc(sem("pe_in"), 16)
        act.dma_start(w1[:], w_cmp1).then_inc(sem("cmp_w_in"), 16)
        act.dma_start(w2[:], w_cmp2).then_inc(sem("cmp_w_in"), 16)
        act.dma_start(sink_row[:], sinks).then_inc(sem("sinks_in"), 16)
        act.dma_start(seen[:], c_seen).then_inc(sem("cmp_mask_in"), 16)
        act.dma_start(cmp_mask[:], c_cmp).then_inc(sem("cmp_mask_in"), 16)
        for k in range(KD):
            act.wait_ge(sem("t_x"), k + 1)
            act.activation(act_hi[:, k, :], xn[:, k % 2, :], ACT.Identity, bias=mod[:, k:k + 1])\
                .then_inc(sem("t_hi"), 1)
        ps, ready = L.psum("gw", 0)
        act.wait_ge(*ready)
        act.activation(gates[:].rearrange("p t h -> p (t h)"), ps[:, 0:NT * 3 * NSA_H], ACT.Sigmoid)\
            .then_inc(sem("gates_out"), 1)
        for j in range(4):
            take(L, ("qa", j), "q_out", [(qa[:, j, :], full)], -HD ** -0.5)
        for n in range(2):
            ps, ready = L.psum("hid", n)
            act.wait_ge(*ready)
            act.activation(hid[:, n, :], ps[0:2 * NCP, 0:CH], ACT.Silu).then_inc(sem("hid_out"), 1)
        act.dma_start(alibi[:], c_alibi).then_inc(sem("masks_in"), 16)
        act.dma_start(window[:], c_window).then_inc(sem("masks_in"), 16)
        use_exp_ln()
        take(L, ("ks", 0), "k_out", [(ks[:], full)])
        take(L, ("kw", 0), "k_out", [(kw[:], full)])
        for n in range(2):
            ps, ready = L.psum("hT", n)
            act.wait_ge(*ready)
            act.activation(hid_t[:, n, :, :].rearrange("p a b -> p (a b)"), ps[:, 0:4 * NCP], ACT.Copy)\
                .then_inc(sem("hidT_out"), 1)
        for t in range(NT):
            ps, ready = L.psum("vt", t)
            act.wait_ge(*ready)
            act.activation(vt[:, t, :], ps[:, 0:3 * P], ACT.Copy).then_inc(sem("v_out"), 1)
        ps, ready = L.psum("kcT", 0)
        act.wait_ge(*ready)
        act.wait_ge(sem("kct_set"), 1)
        for e in range(2):
            act.activation(kct[half(e), e * NCP:(e + 1) * NCP], ps[0:HD, e * NCP:(e + 1) * NCP], ACT.Copy).then_inc(sem("kc_out"), 1)
        ps, ready = L.psum("vcT", 0)
        act.wait_ge(*ready)
        act.wait_ge(sem("vbd_set"), 1)
        for r in range(4):
            e = r % 2
            act.activation(vbd[r * NCP:(r + 1) * NCP, e * HD:(e + 1) * HD], ps[e * NCP:(e + 1) * NCP, 0:HD], ACT.Copy)\
                .then_inc(sem("vc_out"), 1)
        for t in range(NT):
            act.wait_ge(sem("c_centred"), t + 1)
            act.activation(cx_of[t], cx_of[t], ACT.Exp).then_inc(sem("c_exped"), 1)
        for j in range(4):
            take(L, ("qb", j), "q_out", [(qb[:, j, :], full)], -HD ** -0.5)
        take(L, ("kb", 0), "k_out", [(kb[:], full)])
        for t in range(NT):
            ps, ready = L.psum("cT", t)
            act.wait_ge(*ready)
            act.activation(cpt[:, :, t * P:t * P + P], ps[:, 0:2 * P].rearrange("p (c q) -> p c q", q=P), ACT.Copy)\
                .then_inc(sem("c_pt"), 1)
        def t_exp(i, t):
            b, j, e = SUBS[i]
            u = i * NT + t
            w = keys_of(i, t)[1] * P + (b == "swa")
            act.wait_ge(sem("t_masked"), u + 1)
            if u >= 3:
                act.wait_ge(*L.psum("T", *TUNITS[u - 3])[1])
            if u >= 4:
                act.wait_ge(sem("t_inverted"), u - 3)
            act.activation(pr2[:, u % 3, 0:w], xs2[:, u % 3, 0:w], ACT.Exp, bias=stat_min[:, u % 4:u % 4 + 1],
                           scale=-1.0, accum_out=stat_sum[:, u % 4:u % 4 + 1]).then_inc(sem("t_exped"), 1)

        def t_probs_out(i, t):
            first, n = keys_of(i, t)
            ps, ready = L.psum("T", i, t)
            act.wait_ge(*ready)
            if t == 0 and i >= 2:
                act.wait_ge(*L.psum("O", i - 2)[1])
            act.activation(pt2[:, i % 2, first:first + n, t * P:t * P + P],
                           ps[:, 0:n * P].rearrange("p (k q) -> p k q", q=P), ACT.Copy).then_inc(sem("t_pt"), 1)

        def t_heads_out(i):
            b, j, e = SUBS[i]
            if e == 1 and b != "sel":
                ps, ready = L.psum("O", i)
                act.wait_ge(*ready)
                act.activation((qb if b == "swa" else qa)[:, j, :], ps[:], ACT.Copy).then_inc(sem("heads_out"), 1)

        for v in range(len(TUNITS) + TAIL_LAG + 2):
            unit = at_step(TUNITS, v)
            if unit(TAIL_LAG + 1):
                t_probs_out(*unit(TAIL_LAG + 1))
            if unit(TAIL_LAG + 2) and unit(TAIL_LAG + 2)[1] == NT - 1:
                t_heads_out(unit(TAIL_LAG + 2)[0])
            if unit(1):
                t_exp(*unit(1))
        for j in range(8):
            ps, ready = L.psum("z", j)
            act.wait_ge(*ready)
            if j >= 2:
                act.wait_ge(sem("u_out"), j - 1)
            act.activation(silu_z[:, j % 2, :], ps[:], ACT.Silu).then_inc(sem("z_out"), 1)
            act.wait_ge(sem("u_out"), j + 1)
            act.activation(u_hi[:, j, :], ux[:, j % 2, :], ACT.Copy).then_inc(sem("u_hi"), 1)
        for j in range(KD):
            for c, name in enumerate(("ma", "mb")):
                ps, ready = L.psum(name, j)
                act.wait_ge(*ready)
                if j:
                    act.wait_ge(sem("y_part"), 2 * j + c - 1)
                act.activation(yx[:, c, :], ps[:], ACT.Sigmoid).then_inc(sem("merge_out"), 1)
            act.wait_ge(sem("y_out"), j + 1)
            act.activation(y_hi[:, j, :], yx[:, 2 + j % 2, :], ACT.Copy).then_inc(sem("y_hi"), 1)
        use_exp_ln()
        for j in range(KD):
            take(L, ("wout", j), "y2_out", [(y2[:, j, :], full)])
            if j >= 2:
                act.wait_ge(sem("t_sum"), 2 * KD + j - 1)
            act.wait_ge(sem("y2_out"), j + 1)
            act.activation(sq[:, j % 2, :], y2[:, j, :], ACT.Square).then_inc(sem("t_sq"), 1)
        act.wait_ge(*L.psum("norm", 2)[1])
        act.wait_ge(sem("fin_x"), KD)
        t_rstd(2, L.psum("norm", 2)[0], rstd)

    @block.vector
    def _(dve):
        def sums(L, i):
            first, n, _ = NORMS[i]
            squares, total = norm_space(i)
            for k in range(n):
                b = squares[:, (first + k) % 2, :]
                dve.wait_ge(*L.at("norm_sq", first + k + 1))
                if k:
                    dve.wait_ge(*L.at("norm_sum", first + k))
                    dve.tensor_tensor(total[:], total[:], b, ALU.add).then_inc(sem("norm_sum"), 1)
                else:
                    if i != 2 and (i or L.n):
                        Lp, ip = (L, i - 1) if i else (Layer(L.n - 1), 4)
                        dve.wait_ge(*Lp.psum("norm", ip)[1])
                    dve.tensor_copy(total[:], b).then_inc(sem("norm_sum"), 1)

        def normed(L, i, src, lo, hi, first_tile=0):
            first, n, _ = NORMS[i]
            g0 = L.n * GAIN_PER_LAYER + first
            dve.wait_ge(*L.at("norm_rstd", i + 1))

            def low(k):
                dve.wait_ge(*L.at("norm_hi", first + k + 1))
                dve.tensor_tensor(lo[:, first_tile + k, :], xn[:, (first + k) % 2, :],
                                  hi[:, first_tile + k, :].bitcast(F32), ALU.subtract).then_inc(sem("norm_lo"), 1)

            for k in range(n):
                if first + k >= 2 or L.n:
                    dve.wait_ge(*L.at("norm_lo", first + k - 1))
                dve.scalar_tensor_tensor(xn[:, (first + k) % 2, :], src(k), g_sb[:, g0 + k:g0 + k + 1], rstd[:],
                                         ALU.mult, ALU.mult).then_inc(sem("norm_x"), 1)
                if k:
                    low(k - 1)
            low(n - 1)

        def ada_sum(n):
            k, c = divmod(n, 3)
            dve.wait_ge(sem(f"ada_in{n % 2}"), 16 * (n // 2 + 1))
            acc, col = mod_acc[:, c * D:(c + 1) * D], g_sb[:, G_C + k:G_C + k + 1]
            if k == 0:
                dve.tensor_scalar(acc, ada[:, n % 2, :], col, None, ALU.mult).then_inc(sem("ada_summed"), 1)
            else:
                dve.wait_ge(sem("ada_summed"), n - 2)
                dve.scalar_tensor_tensor(acc, ada[:, n % 2, :], col, acc, ALU.mult, ALU.add)\
                    .then_inc(sem("ada_summed"), 1)

        dve.wait_ge(sem("gains_in"), 16)
        for layer in range(layers):
            L = Layer(layer)
            if layer == 0:
                sums(L, 0)
                for c in range(KD // 2):
                    dve.wait_ge(sem(f"x_in{c}"), 16)
            normed(L, 0, lambda k: h[:, k, :], act_lo, act_hi)
            if layer == 0:
                for c in range(2):
                    dve.wait_ge(sem("rows_ready"), c + 1)
                    dve.tensor_scalar(rows_sb[:, c * 320:(c + 1) * 320], banks[6 + c][0:DSA_H, 0:320], -1.0, None,
                                      ALU.mult).then_inc(sem("rows_out"), 1)
                dve.wait_ge(sem("consts_in"), 16 * 5)
                dve.tensor_scalar(strict_neg[:], strict[:, S - P:S], BIG, -BIG, ALU.mult, ALU.add)\
                    .then_inc(sem("strict_set"), 1)
                dve.wait_ge(sem("strict_set"), 1)
            ps, ready = L.psum("x", 0)
            dve.wait_ge(*ready)
            dve.tensor_tensor(kr[64:96, 0, :], ps[64:96, :], rope_k[64:96, :], ALU.mult).then_inc(sem("kr_step"), 1)
            dve.tensor_tensor(kr[64:96, 1, :], ps[96:128, :], rope_k[96:128, :], ALU.mult).then_inc(sem("kr_step"), 1)
            dve.wait_ge(*L.at("kr_step", 2))
            dve.tensor_tensor(kr[64:96, 0, :], kr[64:96, 0, :], kr[64:96, 1, :], ALU.add).then_inc(sem("kr_step"), 1)
            def index_sum(t):
                w = width(t)
                for n in range(IDX_H):
                    u = (t - 1) * IDX_H + n
                    dve.wait_ge(*L.at("ix_relu", u + 1))
                    col = iw_w[:, t, n:n + 1]
                    if n == 0:
                        dve.tensor_scalar(isc[:, t - 1, 0:w], relu[:, u % 3, 0:w], col, None, ALU.mult)\
                            .then_inc(sem("ix_acc"), 1)
                    else:
                        dve.wait_ge(*L.at("ix_acc", u))
                        dve.scalar_tensor_tensor(isc[:, t - 1, 0:w], relu[:, u % 3, 0:w], col, isc[:, t - 1, 0:w],
                                                 ALU.mult, ALU.add).then_inc(sem("ix_acc"), 1)
                dve.wait_ge(*L.at("ix_acc", t * IDX_H))
                dve.tensor_tensor(isc[:, t - 1, w - P:w], isc[:, t - 1, w - P:w], causal[:, S - P:S], ALU.subtract)\
                    .then_inc(sem("ix_masked"), 1)

            def rotated_query(n):
                ps, ready = L.psum("uq", n)
                dve.wait_ge(*ready)
                dve.tensor_tensor(mq[:, n, :], ps[:], rope_q[:], ALU.mult).then_inc(sem("mq_out"), 1)

            sums(L, 1)
            sums(L, 2)
            dve.wait_ge(*L.at("iw_out", 1))
            for t in range(1, NT):
                index_sum(t)
            normed(L, 1, lambda k: c_raw[:, k, :], c_lo, c_hi, 0)
            normed(L, 2, lambda k: c_raw[:, 3 + k, :], c_lo, c_hi, 3)
            def topk_max(r, t):
                if r:
                    dve.wait_ge(*L.at("topk_cut", (r - 1) * (NT - 1) + t))
                dve.max(top8[:, t - 1, :], isc[:, t - 1, 0:width(t)]).then_inc(sem("topk_max"), 1)

            def topk_cut(r, t):
                dve.wait_ge(*L.at("topk_max", r * (NT - 1) + t))
                dve.match_replace(isc[:, t - 1, 0:width(t)], top8[:, t - 1, :], isc[:, t - 1, 0:width(t)], -3e38)\
                    .then_inc(sem("topk_cut"), 1)

            def select(t):
                dve.wait_ge(*L.at("topk_cut", (TOPK // 8 - 1) * (NT - 1) + t))
                dve.tensor_scalar(isc[:, t - 1, 0:width(t)], isc[:, t - 1, 0:width(t)], -2e38, BIG,
                                  ALU.is_gt, ALU.mult).then_inc(sem("sel_out"), 1)

            assert 2 * (NT - 1) * (TOPK // 8 - EARLY_ROUNDS + 1) <= UNITS.index((HEADS.index(("d", 0)), NT - 1))

            def late_selection(n):
                r, t = EARLY_ROUNDS + n // (NT - 1), n % (NT - 1) + 1
                if r < TOPK // 8:
                    topk_max(r, t)
                    topk_cut(r, t)
                elif r == TOPK // 8:
                    select(t)

            dve.wait_ge(*L.at("ix_masked", NT - 1))
            for r in range(EARLY_ROUNDS):
                for t in range(1, NT):
                    topk_max(r, t)
                for t in range(1, NT):
                    topk_cut(r, t)
            for n in range(MLA_H):
                rotated_query(n)

            def softmax_mask(i, t):
                kind, m = HEADS[i]
                n, u, w = MD_AT[i, t], UNIT_AT[i, t], width(t)
                ps, ready = L.psum("S", i, t)
                dve.wait_ge(*ready)
                if u >= BUFS:
                    free_x(*UNITS[u - BUFS])
                if n >= 4:
                    dve.wait_ge(*L.at("exped", n - 3))
                x = xs_of[u % BUFS][:, 0:w]
                least = stat_min[:, n % 4:n % 4 + 1]
                src = ps[:, 0:w]
                mask = causal[:, S - w:S]
                if kind == "d":
                    dve.tensor_tensor(x, src, bias[:, m, 0:w][:, ::-1], ALU.add).then_inc(sem("biased"), 1)
                    dve.wait_ge(*L.at("biased", D_AT[i, t] + 1))
                    src = x
                    if t:
                        dve.wait_ge(*L.at("sel_out", t))
                        mask = isc[:, t - 1, 0:w]
                dve.tensor_tensor_reduce(out=x, in0=src, in1=mask, scale=1.0, scalar=3e38, op0=ALU.add, op1=ALU.min,
                                         accum_out=least).then_inc(sem("masked"), 1)

            def free_x(i, t):
                if HEADS[i][0] == "s":
                    dve.wait_ge(*L.at("sb_w", SB_AT[i, t] + 1))
                else:
                    dve.wait_ge(*L.at("exped", MD_AT[i, t] + 1))

            def softmax_scale(i, t):
                n, u, w = MD_AT[i, t], UNIT_AT[i, t], width(t)
                dve.wait_ge(*L.at("exped", n + 1))
                if n >= 4:
                    dve.wait_ge(*L.at("scaled", n - 3))
                inv = stat_inv[:, n % 4:n % 4 + 1]
                dve.reciprocal(inv, stat_sum[:, n % 4:n % 4 + 1]).then_inc(sem("inverted"), 1)
                dve.wait_ge(*L.at("inverted", n + 1))
                dve.tensor_scalar(pr_of[u % BUFS][:, 0:w], pr_of[u % BUFS][:, 0:w], inv, None, ALU.mult)\
                    .then_inc(sem("scaled"), 1)

            def stick_sums(i, t):
                n, u, w = SB_AT[i, t], UNIT_AT[i, t], width(t)
                ps, _ = L.psum("S", i, t)
                if u >= BUFS:
                    free_x(*UNITS[u - BUFS])
                x, b = xs_of[u % BUFS][:, 0:w], z1_of[n % SB_BUFS][:, 0:w]
                dve.wait_ge(*L.at("sb_ln", n + 1))
                dve.scalar_tensor_tensor(x, ps[:, 0:w], 0.0, b, ALU.max, ALU.add).then_inc(sem("sb_neg"), 1)
                dve.wait_ge(*L.at("sb_neg", n + 1))
                dve.tensor_tensor_scan(b[:, ::-1], x[:, ::-1], strict[:, S - w:S][:, ::-1], 0.0, ALU.add, ALU.mult)\
                    .then_inc(sem("sb_scan"), 1)
                dve.wait_ge(*L.at("sb_scan", n + 1))
                dve.tensor_tensor(x, ps[:, 0:w], b, ALU.subtract).then_inc(sem("sb_log"), 1)
                dve.wait_ge(*L.at("sb_log", n + 1))
                dve.tensor_tensor(x[:, w - P:w], x[:, w - P:w], strict_neg[:], ALU.add)\
                    .then_inc(sem("sb_masked"), 1)

            def probs_out(i, t):
                ps, ready = L.psum("T", i, t)
                dve.wait_ge(*ready)
                if t == first_tile(i) and i >= 2:
                    dve.wait_ge(*L.psum("O", i - 2)[1])
                dve.tensor_copy(pt[:, i % 2, 0:t + 1, t * P:t * P + P],
                                ps[:, 0:width(t)].rearrange("p (k q) -> p k q", q=P)).then_inc(sem("pt_dve"), 1)

            if layer == 0:
                dve.wait_ge(sem("bias_in"), 16 * DSA_H)
            def head_low(i):
                dve.wait_ge(*L.at("o_hi", i + 1))
                o_hi, o_lo = mixed(i // 2)
                dve.tensor_tensor(o_lo[half(i), :], L.psum("O", i)[0][half(i), :],
                                  o_hi[half(i), :].bitcast(F32), ALU.subtract).then_inc(sem("o_lo"), 1)

            for v in range(len(UNITS) + LAG + 1 + O_DELAY):
                unit = at_step(UNITS, v, "s")
                if unit(0, stick=False):
                    softmax_mask(*unit(0))
                if unit(LAG + 1, stick=True):
                    probs_out(*unit(LAG + 1))
                if unit(1, stick=True):
                    stick_sums(*unit(1))
                if unit(2, stick=False):
                    softmax_scale(*unit(2))
                if v % 2:
                    late_selection(v // 2)
                if unit(LAG + 1 + O_DELAY) and unit(LAG + 1 + O_DELAY)[1] == last_tile(unit(LAG + 1 + O_DELAY)[0]):
                    head_low(unit(LAG + 1 + O_DELAY)[0])

            def add_to_h(key, name, j):
                ps, ready = L.psum(*key)
                dve.wait_ge(*ready)
                dve.tensor_tensor(h[:, j, :], h[:, j, :], ps[:], ALU.add).then_inc(sem(name), 1)

            def sum_of(i, k, L=L):
                first, n, _ = NORMS[i]
                b = sq[:, (first + k) % 2, :]
                dve.wait_ge(*L.at("norm_sq", first + k + 1))
                if k:
                    dve.wait_ge(*L.at("norm_sum", first + k))
                    dve.tensor_tensor(ssum[:], ssum[:], b, ALU.add).then_inc(sem("norm_sum"), 1)
                else:
                    dve.wait_ge(*(L.psum("norm", i - 1) if i else Layer(L.n - 1).psum("norm", 4))[1])
                    dve.tensor_copy(ssum[:], b).then_inc(sem("norm_sum"), 1)

            def gained(i, k):
                n = NORMS[i][0] + k
                dve.wait_ge(*L.at("norm_lo", n - 1))
                dve.tensor_scalar(xn[:, n % 2, :], h[:, k, :], g_sb[:, L.n * GAIN_PER_LAYER + n:][:, 0:1], None,
                                  ALU.mult).then_inc(sem("norm_x"), 1)

            def gained_low(i, k):
                n = NORMS[i][0] + k
                dve.wait_ge(*L.at("norm_hi", n + 1))
                dve.tensor_tensor(act_lo[:, k, :], xn[:, n % 2, :], act_hi[:, k, :].bitcast(F32), ALU.subtract)\
                    .then_inc(sem("norm_lo"), 1)

            def update(i, k, key, name, count):
                add_to_h(key, name, k)
                dve.wait_ge(*L.at(name, count))
                gained(i, k)
                if k:
                    sum_of(i, k - 1)
                    gained_low(i, k - 1)
                if k == KD - 1:
                    gained_low(i, k)
                    sum_of(i, k)

            for j in range(KD):
                update(3, j, ("wo", j), "h_wo", j + 1)
            dve.wait_ge(*L.at("p_hi", 1))
            dve.tensor_tensor(pp_lo[:], p_raw[:], pp_hi[:].bitcast(F32), ALU.subtract).then_inc(sem("p_lo"), 1)
            for f in range(FG):
                for j in range(FJ):
                    n = f * FJ + j
                    ps, ready = L.psum("fg", f, j)
                    dve.wait_ge(*ready)
                    dve.wait_ge(*L.at("norm_rstd", 4))
                    if n >= 2:
                        dve.wait_ge(*L.at("ff_out", n - 1))
                    dve.tensor_tensor(gate[:, n % 2, :], ps[:], rstd[:], ALU.mult).then_inc(sem("g_scaled"), 1)
                    ps, ready = L.psum("fu", f, j)
                    dve.wait_ge(*ready)
                    if n >= 2:
                        dve.wait_ge(*L.at("ff_lo", n - 1))
                    dve.tensor_tensor(ffx[:, n % 2, :], ps[:], rstd[:], ALU.mult).then_inc(sem("u_scaled"), 1)
                    dve.wait_ge(*L.at("silu_out", n + 1))
                    dve.wait_ge(*L.at("u_scaled", n + 1))
                    dve.tensor_tensor(ffx[:, n % 2, :], gate[:, n % 2, :], ffx[:, n % 2, :], ALU.mult)\
                        .then_inc(sem("ff_out"), 1)
                    dve.wait_ge(*L.at("ff_hi", n + 1))
                    dve.tensor_tensor(ff_lo[:, j, :], ffx[:, n % 2, :], ff_hi[:, j, :].bitcast(F32), ALU.subtract)\
                        .then_inc(sem("ff_lo"), 1)
                    if layer == layers - 1 and n < ADA // 2:
                        ada_sum(2 * n)
                        ada_sum(2 * n + 1)
                for j in range(KD):
                    if f:
                        dve.wait_ge(*L.at("h_ffn", j + 1))
                        update(4, j, ("fd", f, j), "h_ffn", KD + j + 1)
                    else:
                        add_to_h(("fd", f, j), "h_ffn", j)
            def next_sum(k):
                if layer < layers - 1:
                    sum_of(0, k, Layer(layer + 1))
                    return
                for c, (squared, total) in enumerate(((sq, ssum), (sq_b, ssum_b))):
                    dve.wait_ge(sem("t_sq"), 2 * k + c + 1)
                    if k:
                        dve.wait_ge(sem("t_sum"), 2 * k + c - 1)
                        dve.tensor_tensor(total[:], total[:], squared[:, k % 2, :], ALU.add).then_inc(sem("t_sum"), 1)
                    else:
                        dve.wait_ge(*L.psum("norm", 4)[1])
                        dve.tensor_copy(total[:], squared[:, 0, :]).then_inc(sem("t_sum"), 1)

            for j in range(KD):
                ps, ready = L.psum("pg", j)
                dve.wait_ge(*ready)
                dve.wait_ge(*L.at("norm_rstd", 5))
                if j >= 2:
                    dve.wait_ge(*L.at("ple_out", j - 1))
                else:
                    dve.wait_ge(*L.at("ff_out", FG * FJ))
                dve.tensor_tensor(gate[:, j % 2, :], ps[:], rstd[:], ALU.mult).then_inc(sem("pg_scaled"), 1)
                dve.wait_ge(*L.at("sig_out", j + 1))
                if j >= 2:
                    dve.wait_ge(*L.at("h_ple", j - 1))
                dve.tensor_tensor(ffx[:, j % 2, :], gate[:, j % 2, :], L.psum("pp", j)[0][:], ALU.mult)\
                    .then_inc(sem("ple_out"), 1)
                dve.wait_ge(*L.at("ple_out", j + 1))
                dve.tensor_tensor(h[:, j, :], h[:, j, :], ffx[:, j % 2, :], ALU.add).then_inc(sem("h_ple"), 1)
                if j:
                    next_sum(j - 1)
            next_sum(KD - 1)

        L = Tail(layers)
        ps, ready = L.psum("mod", 0)
        dve.wait_ge(*ready)
        dve.tensor_tensor(mod[:], ps[:, 0:3 * KD], g_sb[:, G_BADA:G_BADA + 3 * KD], ALU.add).then_inc(sem("mod_out"), 1)
        dve.wait_ge(sem("mod_out"), 1)
        dve.scalar_tensor_tensor(gain_pre[:], mod[:, KD:2 * KD], 1.0, g_sb[:, G_PRE:G_PRE + KD], ALU.add, ALU.mult)\
            .then_inc(sem("gains_set"), 1)
        dve.wait_ge(sem("gains_set"), 1)
        dve.tensor_tensor(gain_pre[:], gain_pre[:], g_sb[:, G_FINAL:G_FINAL + KD], ALU.mult).then_inc(sem("gains_set"), 1)
        dve.tensor_tensor(gain_post[:], mod[:, 2 * KD:3 * KD], g_sb[:, G_POST:G_POST + KD], ALU.mult)\
            .then_inc(sem("gains_set"), 1)
        ps, ready = L.psum("norm", 1)
        dve.wait_ge(*ready)
        dve.wait_ge(sem("t_rstd"), 1)
        dve.tensor_tensor(rstd_b[:], ps[:], rstd[:], ALU.mult).then_inc(sem("mean_b"), 1)
        dve.wait_ge(sem("mean_b"), 1)
        dve.tensor_tensor(rstd_b[:], rstd_b[:], rstd[:], ALU.mult).then_inc(sem("mean_b"), 1)
        dve.wait_ge(sem("t_rstd"), 2)
        dve.tensor_tensor(rstd_b[:], rstd_b[:], rstd[:], ALU.mult).then_inc(sem("rstd_both"), 1)
        dve.wait_ge(sem("rstd_both"), 1)
        dve.wait_ge(sem("gains_set"), 3)

        def t_low(k):
            dve.wait_ge(sem("t_hi"), k + 1)
            dve.scalar_tensor_tensor(act_lo[:, k, :], xn[:, k % 2, :], mod[:, k:k + 1], act_hi[:, k, :].bitcast(F32),
                                     ALU.add, ALU.subtract).then_inc(sem("t_lo"), 1)

        for k in range(KD):
            if k >= 2:
                dve.wait_ge(sem("t_lo"), k - 1)
            dve.scalar_tensor_tensor(xn[:, k % 2, :], h[:, k, :], gain_pre[:, k:k + 1], rstd_b[:], ALU.mult, ALU.mult)\
                .then_inc(sem("t_x"), 1)
            if k:
                t_low(k - 1)
        t_low(KD - 1)
        dve.memset(ones_row[:], -1.0).then_inc(sem("ones_row_set"), 1)
        dve.memset(vbd[:], 0.0).then_inc(sem("vbd_set"), 1)
        dve.memset(kct[:], 0.0).then_inc(sem("kct_set"), 1)
        dve.memset(cmp_x[:], 0.0).then_inc(sem("cmp_x_set"), 1)
        dve.wait_ge(sem("pe_in"), 16)
        dve.wait_ge(sem("cmp_x_set"), 1)
        for n, name in enumerate(("kc", "vc")):
            ps, ready = L.psum(name, 0)
            dve.wait_ge(*ready)
            for g in range(2):
                for e in range(2):
                    src = ps[half(g), :]
                    src = bass.AP(src.tensor, src.offset + e, [src.ap[0], [2, CB // 2], [CS, NC]])
                    pos = pe_sb[half(e), n, :].unsqueeze(2).broadcast_to([64, CB // 2, NC])
                    dve.tensor_tensor(cmp_x[half(e), n, :, g * NCP:g * NCP + NC], src, pos, ALU.add)\
                        .then_inc(sem("cmp_in"), 1)
        for k in range(KD):
            dve.wait_ge(sem("t_x"), k + 1)
            dve.scalar_tensor_tensor(h[:, k, :], h[:, k, :], g_sb[:, G_FINAL + k:G_FINAL + k + 1], rstd[:],
                                     ALU.mult, ALU.mult).then_inc(sem("fin_x"), 1)
        dve.wait_ge(sem("cmp_mask_in"), 16 * 2)
        dve.wait_ge(sem("gates_out"), 1)
        for t in range(NT):
            ps, ready = L.psum("cS", t)
            dve.wait_ge(*ready)
            flat = cx_of[t]
            x = flat.rearrange("p (h c) -> p h c", c=NCP)
            col = [cst[:, c, :] for c in range(4)]
            wide = lambda a: a.unsqueeze(2).broadcast_to([P, NSA_H, NCP])
            dve.tensor_tensor(flat, ps[:, 0:NSA_H * NCP], cmp_mask[:, t, :], ALU.add).then_inc(sem("c_masked"), 1)
            dve.wait_ge(sem("c_masked"), t + 1)
            dve.tensor_reduce(col[0], x, AX_X, ALU.min).then_inc(sem("c_min"), 1)
            dve.wait_ge(sem("c_min"), t + 1)
            dve.tensor_tensor(x, wide(col[0]), x, ALU.subtract).then_inc(sem("c_centred"), 1)
            dve.wait_ge(sem("c_exped"), t + 1)
            dve.tensor_reduce(col[1], x, AX_X, ALU.add).then_inc(sem("c_sum"), 1)
            dve.wait_ge(sem("c_sum"), t + 1)
            dve.reciprocal(col[2], col[1]).then_inc(sem("c_inv"), 1)
            dve.wait_ge(sem("c_inv"), t + 1)
            dve.scalar_tensor_tensor(col[3], col[2], seen[:, t:t + 1], gates[:, t, 0:NSA_H], ALU.mult, ALU.mult)\
                .then_inc(sem("c_coef"), 1)
            dve.wait_ge(sem("c_coef"), t + 1)
            dve.tensor_tensor(x, x, wide(col[3]), ALU.mult).then_inc(sem("c_scaled"), 1)

        def t_mask(i, t):
            b, j, e = SUBS[i]
            u = i * NT + t
            _, n = keys_of(i, t)
            ps, ready = L.psum("S", i, t)
            dve.wait_ge(*ready)
            if u >= 3:
                dve.wait_ge(sem("t_exped"), u - 2)
            else:
                dve.wait_ge(*L.psum("cT", NT - 1)[1])
            head = j + 4 * e
            if b == "swa":
                w = n * P + 1
                mask = window[:, head, 2 * P + 1 - w:2 * P + 1]
            else:
                w = n * P
                mask = alibi[:, head, S - w:S]
            dve.tensor_tensor_reduce(out=xs2[:, u % 3, 0:w], in0=ps[:, 0:w], in1=mask, scale=1.0, scalar=3e38,
                                     op0=ALU.add, op1=ALU.min, accum_out=stat_min[:, u % 4:u % 4 + 1])\
                .then_inc(sem("t_masked"), 1)

        def t_scale(i, t):
            b, j, e = SUBS[i]
            u = i * NT + t
            w = keys_of(i, t)[1] * P
            dve.wait_ge(sem("t_exped"), u + 1)
            if u >= 4:
                dve.wait_ge(sem("t_scaled"), u - 3)
            inv = stat_inv[:, u % 4:u % 4 + 1]
            dve.reciprocal(inv, stat_sum[:, u % 4:u % 4 + 1]).then_inc(sem("t_inverted"), 1)
            dve.wait_ge(sem("t_inverted"), u + 1)
            x = pr2[:, u % 3, 0:w]
            if b == "swa":
                dve.tensor_scalar(x, x, inv, None, ALU.mult).then_inc(sem("t_scaled"), 1)
            else:
                g = (1 if b == "sel" else 2) * NSA_H + 2 * j + e
                dve.tensor_scalar(x, x, inv, gates[:, t, g:g + 1], ALU.mult, ALU.mult).then_inc(sem("t_scaled"), 1)

        dve.wait_ge(sem("masks_in"), 16 * 2)
        for v in range(len(TUNITS) + 2):
            unit = at_step(TUNITS, v)
            if unit(2):
                t_scale(*unit(2))
            if unit(0):
                t_mask(*unit(0))
        for j in range(8):
            dve.wait_ge(sem("z_out"), j + 1)
            if j >= 2:
                dve.wait_ge(sem("u_lo"), j - 1)
            dve.wait_ge(sem("heads_out"), 8)
            dve.tensor_tensor(ux[:, j % 2, :], silu_z[:, j % 2, :], (qa if j < 4 else qb)[:, j % 4, :],
                              ALU.mult).then_inc(sem("u_out"), 1)
            dve.wait_ge(sem("u_hi"), j + 1)
            dve.tensor_tensor(u_lo[:, j, :], ux[:, j % 2, :], u_hi[:, j, :].bitcast(F32), ALU.subtract)\
                .then_inc(sem("u_lo"), 1)
        for j in range(KD):
            for c, name in enumerate(("ya", "yb")):
                ps, ready = L.psum(name, j)
                dve.wait_ge(*ready)
                dve.wait_ge(sem("merge_out"), 2 * j + c + 1)
                dve.tensor_tensor(yx[:, c, :], yx[:, c, :], ps[:], ALU.mult).then_inc(sem("y_part"), 1)
            dve.wait_ge(sem("y_part"), 2 * j + 2)
            if j >= 2:
                dve.wait_ge(sem("y_lo"), j - 1)
            dve.tensor_tensor(yx[:, 2 + j % 2, :], yx[:, 0, :], yx[:, 1, :], ALU.add).then_inc(sem("y_out"), 1)
            dve.wait_ge(sem("y_hi"), j + 1)
            dve.tensor_tensor(y_lo[:, j, :], yx[:, 2 + j % 2, :], y_hi[:, j, :].bitcast(F32), ALU.subtract)\
                .then_inc(sem("y_lo"), 1)
        for k in range(KD):
            dve.wait_ge(sem("t_sq"), 2 * KD + k + 1)
            if k:
                dve.wait_ge(sem("t_sum"), 2 * KD + k)
                dve.tensor_tensor(ssum[:], ssum[:], sq[:, k % 2, :], ALU.add).then_inc(sem("t_sum"), 1)
            else:
                dve.tensor_copy(ssum[:], sq[:, 0, :]).then_inc(sem("t_sum"), 1)
        dve.wait_ge(sem("t_rstd"), 3)
        for k in range(KD):
            if k >= 2:
                dve.wait_ge(sem("x_final"), k - 1)
            dve.scalar_tensor_tensor(xn[:, k % 2, :], y2[:, k, :], gain_post[:, k:k + 1], rstd[:], ALU.mult, ALU.mult)\
                .then_inc(sem("post_x"), 1)
            dve.wait_ge(sem("post_x"), k + 1)
            dve.tensor_tensor(h[:, k, :], h[:, k, :], xn[:, k % 2, :], ALU.add).then_inc(sem("x_final"), 1)


def bucket_table():
    import math
    dist = np.maximum(np.arange(S + P) - (P - 1), 0)
    half_b = REL_BUCKETS // 2
    d = np.maximum(dist, 1).astype(np.float32)
    large = half_b + (np.log(d / np.float32(half_b)) / np.float32(math.log(REL_MAX / half_b))
                      * np.float32(REL_BUCKETS - half_b)).astype(np.int32)
    bucket = np.where(dist < half_b, dist, np.minimum(large, REL_BUCKETS - 1))
    return (np.arange(REL_BUCKETS)[:, None] == bucket[None, :]).astype(np.float32)


def rope_tables():
    half_r = ROPE // 2
    inv = np.float32(10000.0) ** (-np.arange(half_r, dtype=np.float32) / np.float32(half_r))
    ang = np.arange(S, dtype=np.float32)[None, :] * inv[:, None]
    cos, sin = np.cos(ang).astype(np.float32), np.sin(ang).astype(np.float32)
    t = np.concatenate([np.ones((NOPE, S), np.float32), cos, cos, -sin, sin])
    return (t * np.float32(-(NOPE + ROPE) ** -0.5)).astype(np.float32), t


def shifted(fn):
    dist = np.arange(P)[:, None] + (S - P) - np.arange(S)[None, :]
    return fn(dist).astype(np.float32)


def blocks(w):
    return [w[k * P:(k + 1) * P] for k in range(w.shape[0] // P)]


def pad_cols(w, n=P):
    return np.concatenate([w, np.zeros((w.shape[0], n - w.shape[1]), w.dtype)], 1) if w.shape[1] < n else w


def padded(out):
    while len(out) % BLK:
        out.append(np.zeros((P, P), np.float32))


def layer_stream(w_in, w_uq, w_ukv, w_o, w_gate, w_up, w_down, w_pg, w_pp):
    cuts = np.cumsum([0, Q_LORA, KV_LORA, ROPE, DSA_H * HD, HD, HD, IDX_H * HD, HD, IDX_H,
                      SB_H * HD, SB_H * HD, SB_H * HD])
    cq, ckv, kr, dq, dk, dv, iq, ik, iw, sq, sk, sv = [w_in[:, a:b] for a, b in zip(cuts[:-1], cuts[1:])]
    swap = np.r_[ROPE // 2:ROPE, 0:ROPE // 2]
    out = []

    def tile(*ws):
        for w in ws:
            out.extend(blocks(w))

    def side_by_side(*ws):
        for group in zip(*(blocks(w) for w in ws)):
            out.extend(group)

    def tiles(w):
        for j in range(w.shape[1] // P):
            tile(w[:, j * P:(j + 1) * P])

    def rows(w, per_chunk=2):
        padded(out)
        for k, b in enumerate(blocks(w)):
            out.extend(b[:, j * P:(j + 1) * P] for j in range(w.shape[1] // P))
            if k % per_chunk == per_chunk - 1:
                padded(out)
        padded(out)

    side_by_side(iq[:, :P], iq[:, P:2 * P])
    tiles(iq[:, 2 * P:])
    out.append(pad_cols(np.concatenate(blocks(iw), 1)))
    tile(np.concatenate([dq[:, 4 * HD:], ik], 1))
    tiles(cq)
    tiles(ckv)
    tile(np.concatenate([dk, kr, kr[:, swap]], 1))
    rows(np.concatenate([dv, sv], 1))
    uq = w_uq.reshape(Q_LORA, MLA_H, NOPE + ROPE)
    ukv = w_ukv.reshape(KV_LORA, MLA_H, NOPE + VDIM)

    def projection(name, j):
        if name == "s4":
            tile(np.concatenate([sq[:, 4 * HD:], sk[:, 4 * HD:]], 1))
        else:
            tile({"dq": dq, "sq": sq, "sk": sk}[name][:, j * P:(j + 1) * P])

    projection("sq", 0)
    projection("sk", 0)
    tiles(ukv[:, :, :NOPE].reshape(KV_LORA, -1))
    rows(ukv[:, :, NOPE:].reshape(KV_LORA, -1))
    for n in range(MLA_H):
        r = uq[:, n, NOPE:]
        tile(np.concatenate([uq[:, n, :NOPE], r, r[:, swap]], 1))
    for name, j in FILLS:
        projection(name, j)
    first = {"m": 0, "d": MLA_H, "s": MLA_H + DSA_H}
    tiles(np.concatenate([w_o[(first[k] + n) * HD:(first[k] + n + 1) * HD] for k, n in HEADS]))
    for f in range(FG):
        for j in range(f * FJ, (f + 1) * FJ):
            (tile if j else side_by_side)(w_gate[:, j * P:(j + 1) * P], w_up[:, j * P:(j + 1) * P])
        tiles(w_down[f * FJ * P:(f + 1) * FJ * P])
    for kind, *j in PLE_ORDER:
        if kind == "pp":
            tile(w_pp[:, j[0] * P:(j[0] + 1) * P])
        elif kind == "pg":
            side_by_side(*(w_pg[:, n * P:(n + 1) * P] for n in j))
    padded(out)
    assert len(out) == layer_blocks(), (len(out), layer_blocks())
    return out


def tail_stream(w_in, w_o_nsa, w_o_swa, w_out):
    pair = np.array([j + 4 * e for j in range(4) for e in range(2)])
    by_pair = (pair[:, None] * HD + np.arange(HD)).reshape(-1)
    cuts = np.cumsum([0, NSA_H * HD, P, P, P, P, P, P, 3 * NSA_H, NSA_H * HD, NSA_H * HD, P, P, NSA_H * HD, D, D])
    qa, kc, vc, ks, vs, kw, vw, gw, za, qb, kb, vb, zb, ma, mb = [w_in[:, a:b] for a, b in zip(cuts[:-1], cuts[1:])]
    gw = gw.reshape(D, 3, NSA_H)[:, :, pair].reshape(D, 3 * NSA_H)
    gw = pad_cols(np.concatenate(blocks(gw), 1), 2 * P)
    out = []

    def tiles(w):
        for j in range(w.shape[1] // P):
            out.extend(blocks(w[:, j * P:(j + 1) * P]))

    for pair_of_blocks in zip(blocks(kc), blocks(vc)):
        out.extend(pair_of_blocks)
    out.extend([gw[:, :P], gw[:, P:]])
    for w in (qa[:, by_pair], ks, kw):
        tiles(w)
    padded(out)
    for k, b in enumerate(blocks(np.concatenate([vs, vw, vb], 1))):
        out.extend(b[:, j * P:(j + 1) * P] for j in range(3))
        if k % 2:
            padded(out)
    for w in (qb[:, by_pair], kb, za[:, by_pair], zb[:, by_pair]):
        tiles(w)
    for j in range(KD):
        cols = slice(j * P, (j + 1) * P)
        for w in (ma, w_o_nsa[by_pair], mb, w_o_swa[by_pair]):
            tiles(w[:, cols])
    tiles(w_out)
    while len(out) < tail_blocks():
        out.append(np.zeros((P, P), np.float32))
    assert len(out) == tail_blocks()
    return out


def tail_tables():
    d = np.arange(P)[:, None] + (S - P) - np.arange(S)[None, :]
    alibi = np.stack([np.where(d >= 0, s * d, BIG) for s in SLOPES], 1)
    d = np.arange(P)[:, None] + P - np.arange(2 * P)[None, :]
    window = np.zeros((P, NSA_H, 2 * P + 1))
    for n, s in enumerate(SLOPES):
        window[:, n, :2 * P] = np.where((d >= 0) & (d < P), s * d, BIG)
    cmp_mask = np.full((P, NT, NSA_H, NCP), BIG)
    for t in range(NT):
        d = (np.arange(P) + t * P)[:, None] - (np.arange(NC) * CS + CB - 1)[None, :]
        for j in range(4):
            for e in range(2):
                cmp_mask[:, t, 2 * j + e, :NC] = np.where(d >= 0, SLOPES[j + 4 * e] * d, BIG)
    seen = (np.arange(P)[:, None] + np.arange(NT)[None, :] * P >= CB - 1)
    return [a.astype(np.float32) for a in (alibi, window, cmp_mask.reshape(P, NT, -1), seen)]


def chunked(out):
    a = np.stack(out).reshape(-1, BLK, P, P)
    return np.ascontiguousarray(a.transpose(0, 2, 1, 3).reshape(-1, P, BLK * P))


def columns(v):
    return np.asarray(v).reshape(-1, P).T


def feature_major(x):
    return np.ascontiguousarray(x.T.reshape(-1, P, S).transpose(1, 0, 2))


def layout(a):
    f = {k: np.asarray(v) for k, v in a.items()}
    stream = []
    for i in range(DEPTH):
        stream += layer_stream(*(f[k][i] for k in ("w_in", "mla_w_uq", "mla_w_ukv", "w_o", "w_gate", "w_up", "w_down",
                                                   "w_ple_gate", "w_ple_proj")))
    stream += tail_stream(*(f[k][0] for k in ("w_in_2", "w_o_nsa_2", "w_o_swa_2", "w_out_2")))
    gains = [columns(f[k][i]) for i in range(DEPTH)
             for k in ("attn_norm", "mla_q_norm", "mla_kv_norm", "ffn_norm", "ple_norm")]
    gains += [columns(f[k]) for k in ("final_norm", "g_pre_2", "g_post_2", "b_ada_2", "c_2")]
    rope_q, rope_k = rope_tables()
    alibi, window, cmp_mask, seen = tail_tables()
    per_tile = lambda w: w.reshape(-1, P, w.shape[-1]).transpose(1, 0, 2)
    pe = lambda w: w.reshape(CB // 2, P).T
    out = dict(
        x_t=feature_major(f["x"][0]), p_t=np.stack([feature_major(f["p"][i, 0]) for i in range(DEPTH)]),
        wstream=chunked(stream), gains=np.concatenate(gains, 1), rel_bias=f["rel_bias"],
        c_rope_q=rope_q, c_rope_k=rope_k, c_onehot=bucket_table(), c_eye=np.eye(P, dtype=np.float32),
        c_causal=shifted(lambda d: np.where(d >= 0, 0.0, BIG)), c_strict=shifted(lambda d: d > 0),
        w_ada=per_tile(f["w_ada_2"][0]),
        w_cmp1=np.stack([per_tile(f["w_cmp_k1_2"][0]), per_tile(f["w_cmp_v1_2"][0])], 1),
        w_cmp2=np.stack([per_tile(f["w_cmp_k2_2"][0]), per_tile(f["w_cmp_v2_2"][0])], 1),
        pe_t=np.stack([pe(f["pe_cmp_k_2"][0]), pe(f["pe_cmp_v_2"][0])], 1),
        sinks=f["sinks_2"],
        c_alibi=alibi, c_window=window, c_cmp=cmp_mask, c_seen=seen)
    return {k: np.ascontiguousarray(v) for k, v in out.items()}


def kernel(**inputs):
    import concourse.bacc as bacc
    from concourse.bass_utils import run_bass_kernel_spmd

    arrays = layout(inputs)
    nc = bacc.Bacc("TRN2", target_bir_lowering=False, num_devices=1)
    args = {k: nc.dram_tensor(f"in_{k}", v.shape, F32, kind="ExternalInput").ap() for k, v in arrays.items()}
    out = nc.dram_tensor("out_t", (P, KD, S), F32, kind="ExternalOutput").ap()
    build(nc, out_t=out, **args)
    r = run_bass_kernel_spmd(nc, [{f"in_{k}": v for k, v in arrays.items()}], core_ids=[0])
    got = np.asarray(r.results[0]["out_t"])
    return np.ascontiguousarray(got.transpose(2, 1, 0)).reshape(1, S, D)
```
